# Optimizing a Trainium2 kernel written in Bass

```python
import math
import jax, jax.numpy as jnp
from jax import lax
import numpy as np

D_MODEL = 1024
BATCH = 1
SEQ = 512
DEPTH = 1
DEC_BATCH = 8
DEC_SEQ = 4
PAST_LEN = 2048
PAGE_SIZE = 128

D_MIX = D_MODEL
D_HGRN = D_MIX // 2
H_HGRN = 4
DK_HGRN = D_HGRN // H_HGRN
DV_HGRN = D_HGRN // H_HGRN
D_FOX = D_MIX - D_HGRN
H_FOX = 8
DH_FOX = D_FOX // H_FOX
D_FF = 2816
CHUNK_HGRN = 64
Q_BLOCK = 128
EPS = 1e-6
TINY = 1e-30
NEG = -1e30
D_IN = 4 * D_HGRN + 3 * D_FOX + H_FOX

kernel_name = 'hymba_hgrn2_fox_macaron_step'

def rmsnorm(x, g):
    xf = x.astype(jnp.float32)
    y = xf * lax.rsqrt(jnp.mean(xf * xf, axis=-1, keepdims=True) + EPS)
    return (y * g.astype(jnp.float32)).astype(x.dtype)

def headnorm(o, gain):
    h, d = o.shape[-2], o.shape[-1]
    y = o * lax.rsqrt(jnp.mean(o * o, axis=-1, keepdims=True) + EPS)
    y = y * gain.astype(jnp.float32).reshape(h, d)
    return y.reshape(o.shape[:-2] + (h * d,))

def swiglu(h, w_in, w_out):
    a, b = jnp.split(h @ w_in, 2, axis=-1)
    return (jax.nn.silu(a) * b) @ w_out

def hgrn_lower_bounds(lb_param):
    p = jax.nn.softmax(lb_param.astype(jnp.float32), axis=0)
    return jnp.cumsum(p, axis=0) - p[0]

def hgrn2(a_q, a_f, a_i, a_g, lb, gain, state0):
    bn, t_len, _ = a_q.shape
    f32 = jnp.float32
    f_gate = lb + (1.0 - lb) * jax.nn.sigmoid(a_f.astype(f32))
    logf = jnp.log(jnp.maximum(f_gate, TINY))
    k = 1.0 - f_gate
    q = a_q.astype(f32)
    v = a_i.astype(f32)
    c = math.gcd(t_len, CHUNK_HGRN)
    n = t_len // c

    def chunks(a):
        return a.reshape(bn, n, c, H_HGRN, a.shape[-1] // H_HGRN).transpose(1, 0, 3, 2, 4)

    qc, kc, lfc, vc = chunks(q), chunks(k), chunks(logf), chunks(v)
    causal = jnp.tril(jnp.ones((c, c), dtype=bool))[:, :, None]

    def step(s_prev, inp):
        qb, kb, lfb, vb = inp
        a_cum = jnp.cumsum(lfb, axis=2)
        diff = a_cum[:, :, :, None, :] - a_cum[:, :, None, :, :]
        decay = jnp.where(causal, jnp.exp(jnp.where(causal, diff, 0.0)), 0.0)
        scores = jnp.einsum('bhtd,bhsd,bhtsd->bhts', qb, kb, decay)
        o = jnp.einsum('bhts,bhsv->bhtv', scores, vb) + jnp.einsum('bhtd,bhdv->bhtv', qb * jnp.exp(a_cum), s_prev)
        a_last = a_cum[:, :, -1:, :]
        s_new = jnp.exp(a_last[:, :, 0, :])[..., None] * s_prev + jnp.einsum('bhsd,bhsv->bhdv', kb * jnp.exp(a_last - a_cum), vb)
        return s_new, o

    s_fin, oc = lax.scan(step, state0.astype(f32), (qc, kc, lfc, vc))
    o = oc.transpose(1, 0, 3, 2, 4).reshape(bn, t_len, H_HGRN, DV_HGRN)
    o = headnorm(o, gain) * jax.nn.silu(a_g.astype(f32))
    return o.astype(a_q.dtype), s_fin.astype(state0.dtype)

def fox_prompt(q, k, v, logf):
    bn, t_len = q.shape[0], q.shape[1]
    f32 = jnp.float32
    scale = DH_FOX ** -0.5
    qf, kf, vf = q.astype(f32) * scale, k.astype(f32), v.astype(f32)
    cum = jnp.cumsum(logf, axis=1).transpose(0, 2, 1)
    nb = t_len // Q_BLOCK
    qb = qf.reshape(bn, nb, Q_BLOCK, H_FOX, DH_FOX).transpose(1, 0, 2, 3, 4)
    cb = cum.reshape(bn, H_FOX, nb, Q_BLOCK).transpose(2, 0, 1, 3)
    pos_q = jnp.arange(t_len).reshape(nb, Q_BLOCK)
    pos_k = jnp.arange(t_len)

    def block(args):
        qi, ci, pq = args
        s = jnp.einsum('bqhd,bkhd->bhqk', qi, kf) + ci[..., None] - cum[:, :, None, :]
        s = jnp.where(pq[:, None] >= pos_k[None, :], s, NEG)
        p = jax.nn.softmax(s, axis=-1)
        return jnp.einsum('bhqk,bkhd->bqhd', p, vf)

    o = lax.map(block, (qb, cb, pos_q))
    return o.transpose(1, 0, 2, 3, 4).reshape(bn, t_len, H_FOX, DH_FOX)

def fox_decode(q, k, v, logf, k_past, v_past, logf_past):
    f32 = jnp.float32
    t_len = q.shape[1]
    p_len = k_past.shape[1]
    scale = DH_FOX ** -0.5
    qf = q.astype(f32) * scale
    lfp = logf_past.astype(f32)
    suffix = (lax.cumsum(lfp, axis=1, reverse=True) - lfp).transpose(0, 2, 1)
    cq = jnp.cumsum(logf, axis=1).transpose(0, 2, 1)
    s_past = jnp.einsum('bqhd,bkhd->bhqk', qf, k_past.astype(f32)) + cq[..., None] + suffix[:, :, None, :]
    s_new = jnp.einsum('bqhd,bkhd->bhqk', qf, k.astype(f32)) + cq[..., :, None] - cq[..., None, :]
    causal = jnp.tril(jnp.ones((t_len, t_len), dtype=bool))
    s_new = jnp.where(causal, s_new, NEG)
    p = jax.nn.softmax(jnp.concatenate([s_past, s_new], axis=-1), axis=-1)
    o = jnp.einsum('bhqk,bkhd->bqhd', p[..., :p_len], v_past.astype(f32))
    return o + jnp.einsum('bhqk,bkhd->bqhd', p[..., p_len:], v.astype(f32))

def token_mix(h, w_in, f_bias, lb, hgrn_gain, fox_gain, w_out, state0, attend):
    bn, t_len, _ = h.shape
    p = h @ w_in
    cuts = [D_HGRN, 2 * D_HGRN, 3 * D_HGRN, 4 * D_HGRN, 4 * D_HGRN + D_FOX, 4 * D_HGRN + 2 * D_FOX, 4 * D_HGRN + 3 * D_FOX]
    a_q, a_f, a_i, a_g, f_q, f_k, f_v, f_f = jnp.split(p, cuts, axis=-1)
    o_a, s_fin = hgrn2(a_q, a_f, a_i, a_g, lb, hgrn_gain, state0)
    q = f_q.reshape(bn, t_len, H_FOX, DH_FOX)
    k = f_k.reshape(bn, t_len, H_FOX, DH_FOX)
    v = f_v.reshape(bn, t_len, H_FOX, DH_FOX)
    logf = jax.nn.log_sigmoid(f_f.astype(jnp.float32) + f_bias.astype(jnp.float32))
    o_f = headnorm(attend(q, k, v, logf), fox_gain).astype(h.dtype)
    out = jnp.concatenate([o_a, o_f], axis=-1) @ w_out
    return out, k, v, logf, s_fin

def setup_inputs(seed: int = 0) -> dict:
    key = jax.random.key(seed)
    ks = jax.random.split(key, 24)
    n_pages = PAST_LEN // PAGE_SIZE
    n_used = DEC_BATCH * n_pages
    n_pool = n_used + max(1, n_used // 4)
    nrm = jax.random.normal
    f32 = jnp.float32
    page_table = jax.random.permutation(ks[0], n_pool)[:n_used].reshape(DEC_BATCH, n_pages).astype(jnp.int32)
    return {
        'x_prompt': nrm(ks[1], (BATCH, SEQ, D_MODEL), f32),
        'x_sample': nrm(ks[2], (DEC_BATCH, DEC_SEQ, D_MODEL), f32),
        'cache_k': nrm(ks[3], (DEPTH, n_pool, PAGE_SIZE, H_FOX, DH_FOX), f32),
        'cache_v': nrm(ks[4], (DEPTH, n_pool, PAGE_SIZE, H_FOX, DH_FOX), f32),
        'cache_logf': jax.nn.log_sigmoid(3.0 + nrm(ks[5], (DEPTH, n_pool, PAGE_SIZE, H_FOX), f32)),
        'state_hgrn': 0.5 * nrm(ks[6], (DEPTH, DEC_BATCH, H_HGRN, DK_HGRN, DV_HGRN), f32),
        'page_table': page_table,
        'norm_ffn1': 1.0 + 0.02 * nrm(ks[7], (DEPTH, D_MODEL), f32),
        'ffn1_w_in': nrm(ks[8], (DEPTH, D_MODEL, 2 * D_FF), f32) * D_MODEL ** -0.5,
        'ffn1_w_out': nrm(ks[9], (DEPTH, D_FF, D_MODEL), f32) * D_FF ** -0.5,
        'norm_mix': 1.0 + 0.02 * nrm(ks[10], (DEPTH, D_MODEL), f32),
        'w_in_mix': nrm(ks[11], (DEPTH, D_MODEL, D_IN), f32) * D_MODEL ** -0.5,
        'hgrn_lb': nrm(ks[12], (DEPTH, D_HGRN), f32),
        'fox_f_bias': 3.0 + 0.5 * nrm(ks[13], (DEPTH, H_FOX), f32),
        'hgrn_out_gain': 1.0 + 0.02 * nrm(ks[14], (DEPTH, D_HGRN), f32),
        'fox_out_gain': 1.0 + 0.02 * nrm(ks[15], (DEPTH, D_FOX), f32),
        'w_out_mix': nrm(ks[16], (DEPTH, D_MIX, D_MODEL), f32) * D_MIX ** -0.5,
        'norm_ffn2': 1.0 + 0.02 * nrm(ks[17], (DEPTH, D_MODEL), f32),
        'ffn2_w_in': nrm(ks[18], (DEPTH, D_MODEL, 2 * D_FF), f32) * D_MODEL ** -0.5,
        'ffn2_w_out': nrm(ks[19], (DEPTH, D_FF, D_MODEL), f32) * D_FF ** -0.5,
        'norm_final': 1.0 + 0.02 * nrm(ks[20], (D_MODEL,), f32),
    }

def reference(x_prompt, x_sample, cache_k, cache_v, cache_logf, state_hgrn, page_table,
              norm_ffn1, ffn1_w_in, ffn1_w_out, norm_mix, w_in_mix, hgrn_lb, fox_f_bias,
              hgrn_out_gain, fox_out_gain, w_out_mix, norm_ffn2, ffn2_w_in, ffn2_w_out, norm_final):
    lbs = hgrn_lower_bounds(hgrn_lb)
    db = x_sample.shape[0]

    def sample_attend(l):
        k_past = cache_k[l, page_table].reshape(db, -1, H_FOX, DH_FOX)
        v_past = cache_v[l, page_table].reshape(db, -1, H_FOX, DH_FOX)
        lf_past = cache_logf[l, page_table].reshape(db, -1, H_FOX)
        return lambda q, k, v, lf: fox_decode(q, k, v, lf, k_past, v_past, lf_past)

    def run(x, state0_of, attend_of):
        ks, vs, lfs, ss = [], [], [], []
        for l in range(DEPTH):
            x = x + 0.5 * swiglu(rmsnorm(x, norm_ffn1[l]), ffn1_w_in[l], ffn1_w_out[l])
            m, k, v, lf, s_fin = token_mix(rmsnorm(x, norm_mix[l]), w_in_mix[l], fox_f_bias[l], lbs[l],
                                           hgrn_out_gain[l], fox_out_gain[l], w_out_mix[l],
                                           state0_of(l), attend_of(l))
            x = x + m
            x = x + 0.5 * swiglu(rmsnorm(x, norm_ffn2[l]), ffn2_w_in[l], ffn2_w_out[l])
            ks.append(k)
            vs.append(v)
            lfs.append(lf)
            ss.append(s_fin)
        return rmsnorm(x, norm_final), jnp.stack(ks), jnp.stack(vs), jnp.stack(lfs), jnp.stack(ss)

    zero_state = jnp.zeros((x_prompt.shape[0], H_HGRN, DK_HGRN, DV_HGRN), state_hgrn.dtype)
    y_prompt, new_k_prompt, new_v_prompt, new_logf_prompt, new_hgrn_prompt = run(
        x_prompt, lambda l: zero_state, lambda l: fox_prompt)
    y_sample, new_k_sample, new_v_sample, new_logf_sample, new_hgrn_sample = run(
        x_sample, lambda l: state_hgrn[l], sample_attend)
    return (y_prompt, y_sample, new_k_prompt, new_v_prompt, new_logf_prompt, new_hgrn_prompt,
            new_k_sample, new_v_sample, new_logf_sample, new_hgrn_sample)


_drawn_inputs = setup_inputs


def setup_inputs(seed=0):
    import zlib

    import numpy as np

    out = dict(_drawn_inputs(seed))
    spreads = {}
    factors = {'norm_ffn1': 4.959,
     'hgrn_out_gain': 8.0,
     'fox_out_gain': 5.144,
     'norm_ffn2': 8.0,
     'norm_final': 2.963}
    for name, (base, spread) in spreads.items():
        noise = np.random.default_rng([zlib.crc32(name.encode()), seed]).standard_normal(out[name].shape)
        drawn = base * np.exp(spread * noise) if base else spread * noise
        out[name] = __import__('jax').numpy.asarray(drawn.astype(out[name].dtype))
    for name, factor in factors.items():
        out[name] = (out[name] * factor).astype(out[name].dtype)
    return out
```

```python
from contextlib import ExitStack

import numpy as np

import concourse.bass as bass
from concourse import mybir

F32 = mybir.dt.float32
F32R = mybir.dt.float32r
I32 = mybir.dt.int32
U8 = mybir.dt.uint8
ACT = mybir.ActivationFunctionType
ALU = mybir.AluOpType
AX_X = mybir.AxisListType.X
ds = bass.ds

P = 128
EPS = 1e-6
TINY = 1e-30
NEG = -1e30

D = 1024
SEQ = 512
DB, DS_ = 8, 4
NS = DB * DS_
T = SEQ + NS
HALF = T // 2
TT = SEQ // P
D_FF = 2816
KD = D // P
KF = D_FF // P
CHUNKS = (12, 10)
H_HG, H_FX, DH = 4, 8, 64
D_HG = D_FX = 512
D_IN = 4 * D_HG + 3 * D_FX + H_FX
MIX_TILES = (4 * D_HG + 3 * D_FX) // P
PAGES, PAGE, N_POOL = 16, 128, 160
PAST = PAGES * PAGE
UC = 2 * P
SLOT = max(CHUNKS) * UC
SCALE = DH ** -0.5

assert sum(CHUNKS) == KF and all(c % 2 == 0 for c in CHUNKS) and SEQ % P == 0


def build(nc, io):
    y_prompt, y_sample, k_prompt, v_prompt, lf_prompt, s_prompt, k_sample, v_sample, lf_sample, s_sample = io["outs"]
    ctx = ExitStack()
    with ctx:
        ROW = 4 * T
        X0 = (nc.sbuf_base + 63) // 64 * 64
        Z0 = X0 + KD * ROW
        T0 = Z0 + 2 * KD * ROW + 2 * CHUNKS[0] * ROW
        RING = T0 + 4 * ROW
        C0 = RING + 6 * 4 * SLOT
        END = nc.sbuf_usable_end

        def at(name, shape, dt, offset):
            size = int(np.prod(shape[1:])) * (1 if dt == U8 else 4)
            assert offset + size <= END, (name, offset + size, END)
            return nc.alloc_sbuf_tensor_at(name, shape, dt, offset=offset)

        top = [C0]

        def const(name, shape, dt=F32):
            t = at(name, shape, dt, top[0])
            top[0] += (int(np.prod(shape[1:])) * (1 if dt == U8 else 4) + 31) // 32 * 32
            return t

        xT = at("xT", [P, KD, T], F32, X0)
        n_hi = [at("n1_hi", [P, KD, T], F32R, Z0), at("n2_hi", [P, KD, T], F32R, Z0 + 2 * CHUNKS[0] * ROW)]
        n_lo = [at("n1_lo", [P, KD, T], F32R, Z0 + KD * ROW),
                at("n2_lo", [P, KD, T], F32R, Z0 + (2 * CHUNKS[0] + KD) * ROW)]
        g_hi = [at("g1_hi", [P, CHUNKS[0], T], F32R, Z0 + 2 * KD * ROW), at("g2_hi", [P, CHUNKS[0], T], F32R, Z0)]
        g_lo = [at("g1_lo", [P, CHUNKS[0], T], F32R, Z0 + (2 * KD + CHUNKS[0]) * ROW),
                at("g2_lo", [P, CHUNKS[0], T], F32R, Z0 + CHUNKS[0] * ROW)]
        pT = at("mix_projT", [P, MIX_TILES, T], F32, Z0 + 2 * KD * ROW)
        o_hi = at("mix_out_hi", [P, KD, T], F32R, Z0)
        o_lo = at("mix_out_lo", [P, KD, T], F32R, Z0 + KD * ROW)
        x_nat = at("x_nat", [P, TT + 1, D], F32, Z0 + 2 * KD * ROW)
        yT = at("yT", [P, KD, T], F32, Z0 + 2 * KD * ROW)
        y_nat = at("y_nat", [P, 2, D], F32, RING)
        a_n = at("ffn_a", [P, 2, HALF], F32, T0)
        b_n = at("ffn_b", [P, 2, HALF], F32, T0 + ROW)
        a_silu = at("ffn_a_silu", [P, 2, HALF], F32, T0 + 2 * ROW)
        g_f = at("ffn_gated", [P, 2, HALF], F32, T0 + 3 * ROW)
        w_raw = [at(f"w_raw{s}", [P, SLOT], F32, RING + s * 4 * SLOT) for s in range(2)]
        w_hi = [at(f"w_hi{s}", [P, SLOT], F32R, RING + (2 + s) * 4 * SLOT) for s in range(2)]
        w_lo = [at(f"w_lo{s}", [P, SLOT], F32R, RING + (4 + s) * 4 * SLOT) for s in range(2)]
        rstd = const("rstd", [P, 2, HALF])
        SUMSQ_AT = top[0]
        sumsq = const("sumsq", [P, T])
        SQ_AT = top[0]
        sq = const("sq", [P, T])
        ms = const("mean_sq", [P, T])
        root = sq
        ident = const("ident", [P, P])
        ones = const("ones", [P, P])
        gains = const("gains", [P, 4, KD])
        wf = const("w_forget", [P, KD, H_FX])
        wf_hi = const("w_forget_hi", [P, KD, H_FX], F32R)
        wf_lo = const("w_forget_lo", [P, KD, H_FX], F32R)
        ffT = const("forgetT", [H_FX, T])

        ps = ctx.enter_context(nc.psum_tensor("ps", [P, 8, 512], F32))

        def sem(name):
            return ctx.enter_context(nc.semaphore(name))

        const_ready = sem("const_ready")
        gains_landed = sem("gains_landed")
        x_landed = [sem(f"x_landed{i}") for i in range(TT + 1)]
        w_landed = [sem("w_landed0"), sem("w_landed1")]
        w_hi_ready = sem("w_hi_ready")
        w_lo_ready = sem("w_lo_ready")
        mm_done = sem("mm_done")
        drained = sem("drained")
        xt_done = sem("xt_done")
        xt_copied = sem("xt_copied")
        x_ready = sem("x_ready")
        nhi_ready = sem("nhi_ready")
        n_ready = sem("n_ready")
        a_ready = sem("a_ready")
        silu_done = sem("silu_done")
        gated_ready = sem("gated_ready")
        ghi_ready = sem("ghi_ready")
        g_ready = sem("g_ready")
        sq_done = sem("sq_done")
        sq_added = sem("sq_added")
        sumsq_ready = sem("sumsq_ready")
        ss_done = sem("ss_done")
        ms_ready = sem("ms_ready")
        root_ready = sem("root_ready")
        rstd_step = sem("rstd_step")
        wf_split = sem("wf_split")
        ff_done = sem("ff_done")
        ff_ready = sem("ff_ready")
        yt_ready = sem("yt_ready")
        yt_done = sem("yt_done")
        y_copied = sem("y_copied")
        y_stored = [sem("y_stored0"), sem("y_stored1")]

        P_FFN = [0, 24]
        IN_A, OUT_A = CHUNKS[0] // 2, KD // 4
        IN_B, OUT_B = CHUNKS[1] // 2, KD // 4
        P_MIX_IN = IN_A + OUT_A + IN_B + OUT_B
        MIX_PAIRS = MIX_TILES // 4
        P_MIX_OUT = P_MIX_IN + MIX_PAIRS
        P_FFN[1] = P_MIX_OUT + KD // 4
        N_CONST_LOADS = 11
        N_TOK = [P] * TT + [NS]

        def halves(t):
            return t.rearrange("p (s c) -> p s c", s=2)

        def bank(b, n=HALF):
            return ps[:, b, 0:n]

        def unit_psum(j, t):
            return ps[:, 4 * j + 2 * t:4 * j + 2 * t + 2, 0:HALF]

        SS = unit_psum(1, 1)

        block = ctx.enter_context(nc.Block())

        T_Q, T_F, T_I, T_G, T_FQ, T_FK, T_FV = (4 * n for n in range(7))
        LEVELS = (6, 5, 4, 3, 2, 1, 0)
        DIAG = len(LEVELS)

        neg_mask = const("neg_mask", [P, P])
        hg_reset = const("hg_reset", [P, T])
        fx_reset = const("fx_reset", [H_FX, T])
        hg_mask = const("hg_mask", [P, DIAG + 1, SEQ], U8)
        f_bias = const("f_bias", [H_FX, 1])
        hg_lb = const("hg_lb", [P, H_HG])
        hg_gain = const("hg_gain", [P, H_HG])
        fx_gain = const("fx_gain", [P, H_HG])
        lb = const("lb", [P, H_HG])
        one_lb = const("one_minus_lb", [P, H_HG])
        two_heads = const("two_heads", [P, P])
        page_ids = const("page_ids", [P, 1], I32)
        page_row = const("page_row", [1, P], I32)

        ring_top = [RING]

        def buf(name, shape, dt=F32):
            t = at(name, shape, dt, ring_top[0])
            ring_top[0] += (int(np.prod(shape[1:])) * (1 if dt == U8 else 4) + 31) // 32 * 32
            assert ring_top[0] <= C0, (name, ring_top[0] - C0)
            return t

        v_nat = buf("v_nat", [P, TT + 1, D_FX])
        k_st = buf("k_staged", [P, 2, D_FX])
        fx_z = buf("forget_z", [H_FX, T])
        fx_t = buf("forget_t", [H_FX, T])
        fx_lf = buf("forget_log", [H_FX, T])
        fx_cum = buf("forget_cum", [H_FX, T])
        fx_ncum = buf("forget_neg_cum", [H_FX, T])
        lf_nat = buf("lf_nat", [P, TT + 1, H_FX])
        q_aug = [buf(f"q_aug{j}", [97, SEQ]) for j in range(2)]
        k_aug = [buf(f"k_aug{j}", [97, SEQ]) for j in range(2)]
        v_st = [buf(f"v_head{j}", [P, TT, DH]) for j in range(2)]
        prob = [buf(f"prob{j}", [P, TT, SEQ]) for j in range(2)]
        probT = buf("probT", [P, TT, SEQ])
        fx_max = buf("fx_max", [P, 2, TT])
        fx_nmax = buf("fx_neg_max", [P, 2, TT])
        fx_sum = buf("fx_sum", [P, 2, TT])
        fx_inv = buf("fx_inv", [P, 2, TT])
        oF = pT
        cum_d = nc.dram_tensor("cum_scratch", (2, H_FX, SEQ), F32, kind="Internal").ap()

        const_done = sem("const_done")
        mix_consts = sem("mix_consts")
        kt_done, vt_done = sem("kt_done"), sem("vt_done")
        k_copied, v_copied = sem("k_copied"), sem("v_copied")
        k_stored = [sem("k_stored0"), sem("k_stored1")]
        v_stored = sem("v_stored")
        fx_step = sem("fx_step")
        lft_done, lf_copied, lf_stored = sem("lft_done"), sem("lf_copied"), sem("lf_stored")
        cum_stored = sem("cum_stored")
        aug_const = sem("aug_const")
        q_staged, k_staged, v_staged = sem("q_staged"), sem("k_staged_s"), sem("v_staged")
        cum_landed = [sem("cum_landed0"), sem("cum_landed1")]
        fs_done = sem("fs_done")
        fs_masked = sem("fs_masked")
        fs_max = sem("fs_max")
        fs_exp = sem("fs_exp")
        fs_inv = sem("fs_inv")
        fs_prob = sem("fs_prob")
        fpt_done = sem("fpt_done")
        fpt_copied = sem("fpt_copied")
        fo_done, fo_copied = sem("fo_done"), sem("fo_copied")

        def mix_tile(base, i, parts=slice(0, P), cols=slice(0, T)):
            return pT[parts, ds(i + base, 1), cols].rearrange("p o t -> p (o t)")

        def nat(dst_prompt, dst_sample, i):
            if i < TT:
                return dst_prompt[0, 0, i * P:(i + 1) * P].rearrange("t h d -> t (h d)")
            return dst_sample[0].rearrange("b t h d -> (b t) (h d)")

        def mid_sync(sp):
            for i in range(TT + 1):
                n = N_TOK[i]
                sp.wait_ge(k_copied, i + 1)
                sp.dma_start(nat(k_prompt, k_sample, i), k_st[0:n, i % 2, :]).then_inc(k_stored[i % 2], 16)
                sp.wait_ge(v_copied, i + 1)
                sp.dma_start(nat(v_prompt, v_sample, i), v_nat[0:n, i, :]).then_inc(v_stored, 16)
            sp.wait_ge(fx_step, 8)
            sp.dma_start(cum_d[0], fx_cum[:, 0:SEQ]).then_inc(cum_stored, 16)
            sp.dma_start(cum_d[1], fx_ncum[:, 0:SEQ]).then_inc(cum_stored, 16)
            sp.wait_ge(lf_copied, 1)
            sp.dma_start(lf_prompt[0, 0].rearrange("(i p) h -> p i h", p=P), lf_nat[:, 0:TT, :],
                         allow_slow_non_contiguous=True).then_inc(lf_stored, 16)
            sp.dma_start(lf_sample[0].rearrange("b t h -> (b t) h"), lf_nat[0:NS, TT, :]).then_inc(lf_stored, 16)
            sp.wait_ge(cum_stored, 32)
            sp.wait_ge(aug_const, 8)

            def cum_rows(h, j):
                sp.dma_start(q_aug[j][64:65, :], cum_d[0, ds(h, 1), :]).then_inc(cum_landed[j], 16)
                sp.dma_start(k_aug[j][96:97, :], cum_d[1, ds(h, 1), :]).then_inc(cum_landed[j], 16)

            for j in range(2):
                cum_rows(j, j)
            with sp.Fori(1, H_FX // 2) as i:
                for j in range(2):
                    sp.wait_ge(fs_done, i * (2 * TT) + (j - 1) * TT)
                    cum_rows(i * 2 + j, j)
            mid2_sync(sp)

        def mid_stores_waited(sp):
            sp.wait_ge(k_stored[0], 16 * 3)
            sp.wait_ge(k_stored[1], 16 * 2)
            sp.wait_ge(v_stored, 16 * (TT + 1))
            sp.wait_ge(lf_stored, 32)
            mid2_stores_waited(sp)

        def mid_tensor(pe):
            for i in range(TT + 1):
                n = N_TOK[i]
                for src, b, copied, done in ((T_FK, 2 + i % 2, k_copied, kt_done), (T_FV, 4 + i % 2, v_copied, vt_done)):
                    if i >= 2:
                        pe.wait_ge(copied, i - 1)
                    else:
                        pe.wait_ge(drained, 2 * P_MIX_OUT)
                    for q in range(4):
                        mm = pe.transpose(ps[0:n, b, q * P:(q + 1) * P], pT[:, src + q, i * P:i * P + n], ident[:, :])
                    mm.then_inc(done, 1)
            pe.wait_ge(fx_step, 6)
            for i in range(TT + 1):
                n = N_TOK[i]
                mm = pe.transpose(ps[0:n, 6, i * H_FX:(i + 1) * H_FX], fx_lf[:, i * P:i * P + n], ident[0:H_FX, 0:H_FX])
            mm.then_inc(lft_done, 1)

            def scores(h, j, pair, first=False):
                pe.wait_ge(q_staged, h + 1)
                pe.wait_ge(k_staged, h + 1)
                pe.wait_ge(cum_landed[j], pair * 32 + 32)
                for t in range(TT):
                    if not first:
                        pe.wait_ge(fs_exp, h * TT + (t + 1 - TT))
                    pe.matmul(ps[:, t, 0:(t + 1) * P], q_aug[j][:, t * P:(t + 1) * P], k_aug[j][:, 0:(t + 1) * P],
                              start=True, stop=True).then_inc(fs_done, 1)

            def attend(h, j, first=False):
                pe.wait_ge(fs_prob, h * TT + TT)
                pe.wait_ge(v_staged, h + 1)
                for s in range(TT):
                    b = 4 + s % 2
                    if first and s < 2:
                        pe.wait_ge(v_copied, TT + 1)
                    else:
                        pe.wait_ge(fpt_copied, h * TT + (s - 1))
                    for t in range(s, TT):
                        mm = pe.transpose(ps[:, b, (t - s) * P:(t - s + 1) * P], prob[j][:, t, s * P:(s + 1) * P],
                                          ident[:, :])
                    mm.then_inc(fpt_done, 1)
                if first:
                    pe.wait_ge(lf_copied, 1)
                else:
                    pe.wait_ge(fo_copied, h)
                for s in range(TT):
                    pe.wait_ge(fpt_copied, h * TT + (s + 1))
                    mm = pe.matmul(ps[0:DH, 6, s * P:SEQ], v_st[j][:, s, :], probT[:, s, 0:SEQ - s * P],
                                   start=(s == 0), stop=(s == TT - 1))
                mm.then_inc(fo_done, 1)

            pe.wait_ge(k_copied, TT + 1)
            pe.wait_ge(ff_ready, 1)
            scores(0, 0, 0, first=True)
            scores(1, 1, 0)
            attend(0, 0, first=True)
            with pe.Fori(1, H_FX // 2) as i:
                scores(i * 2, 0, i)
                attend(i * 2 - 1, 1)
                scores(i * 2 + 1, 1, i)
                attend(i * 2, 0)
            attend(H_FX - 1, 1)
            new_rows_tensor(pe)
            mid2_tensor(pe)

        def mid_scalar(act):
            for i in range(TT + 1):
                n = N_TOK[i]
                act.wait_ge(kt_done, i + 1)
                if i >= 2:
                    act.wait_ge(k_stored[i % 2], 16 * (i // 2))
                nc.scalar.activation(k_st[0:n, i % 2, :], ps[0:n, 2 + i % 2, :], ACT.Copy).then_inc(k_copied, 1)
                if i == 1:
                    act.wait_ge(fx_step, 3)
                    nc.scalar.activation(fx_t[:, :], fx_t[:, :], ACT.Exp).then_inc(fx_step, 1)
                    act.wait_ge(fx_step, 4)
                    nc.scalar.activation(fx_t[:, :], fx_t[:, :], ACT.Ln, bias=1.0).then_inc(fx_step, 1)

            act.wait_ge(aug_const, 8)

            def stage_q(j, i):
                nc.scalar.activation(q_aug[j][0:DH, :], mix_tile(T_FQ, i, slice(j * DH, (j + 1) * DH), slice(0, SEQ)),
                                     ACT.Copy, scale=SCALE).then_inc(q_staged, 1)

            def exps(h, j):
                for t in range(TT):
                    act.wait_ge(fs_max, h * TT + (t + 1))
                    nc.scalar.activation(prob[j][:, t, 0:(t + 1) * P], ps[:, t, 0:(t + 1) * P], ACT.Exp,
                                         bias=fx_nmax[:, j, t:t + 1], accum_out=fx_sum[:, j, t:t + 1]).then_inc(fs_exp, 1)

            def copy_probT(h, s):
                act.wait_ge(fpt_done, h * TT + (s + 1))
                nc.scalar.activation(probT[:, s, 0:SEQ - s * P], ps[:, 4 + s % 2, 0:SEQ - s * P],
                                     ACT.Copy).then_inc(fpt_copied, 1)

            for j in range(2):
                stage_q(j, 0)
            exps(0, 0)
            exps(1, 1)
            for s in range(TT):
                copy_probT(0, s)
            with act.Fori(1, H_FX // 2) as i:
                for j in range(2):
                    act.wait_ge(fs_done, i * (2 * TT) + (j - 1) * TT)
                    stage_q(j, i)
                for j in range(2):
                    act.wait_ge(fpt_done, i * (2 * TT) + (j - 1) * TT)
                    exps(i * 2 + j, j)
                    for s in range(TT):
                        copy_probT(i * 2 + (j - 1), s)
            for s in range(TT):
                copy_probT(H_FX - 1, s)
            new_rows_scalar(act)
            mid2_scalar(act)

        def mid_vector(dve):
            dve.wait_ge(ff_ready, 1)
            dve.wait_ge(gains_landed, 16 * N_CONST_LOADS)
            nc.vector.tensor_scalar(fx_z[:, :], ffT[:, :], f_bias[:, 0:1], None, ALU.add).then_inc(fx_step, 1)
            dve.wait_ge(fx_step, 1)
            nc.vector.tensor_scalar(fx_t[:, :], fx_z[:, :], -1.0, None, ALU.mult).then_inc(fx_step, 1)
            dve.wait_ge(fx_step, 2)
            nc.vector.tensor_tensor(fx_t[:, :], fx_t[:, :], fx_z[:, :], ALU.min).then_inc(fx_step, 1)
            for j in range(2):
                nc.vector.memset(q_aug[j][:, :], 0.0).then_inc(aug_const, 1)
                nc.vector.memset(k_aug[j][:, :], 0.0).then_inc(aug_const, 1)
            dve.wait_ge(aug_const, 4)
            for j in range(2):
                nc.vector.memset(q_aug[j][96:97, :], 1.0).then_inc(aug_const, 1)
                nc.vector.memset(k_aug[j][64:65, :], 1.0).then_inc(aug_const, 1)
            for i in range(TT + 1):
                dve.wait_ge(vt_done, i + 1)
                nc.vector.tensor_copy(v_nat[0:N_TOK[i], i, :], ps[0:N_TOK[i], 4 + i % 2, :]).then_inc(v_copied, 1)
            dve.wait_ge(fx_step, 5)
            nc.vector.scalar_tensor_tensor(fx_lf[:, :], fx_z[:, :], 0.0, fx_t[:, :], ALU.min,
                                           ALU.subtract).then_inc(fx_step, 1)
            dve.wait_ge(fx_step, 6)
            dve.wait_ge(mix_consts, 1)
            nc.vector.tensor_tensor_scan(fx_cum[:, :], fx_reset[:, :], fx_lf[:, :], 0.0, ALU.mult,
                                         ALU.add).then_inc(fx_step, 1)
            dve.wait_ge(fx_step, 7)
            nc.vector.tensor_scalar(fx_ncum[:, :], fx_cum[:, :], -1.0, None, ALU.mult).then_inc(fx_step, 1)
            dve.wait_ge(lft_done, 1)
            nc.vector.tensor_copy(lf_nat[:, 0:TT, :], ps[:, 6, 0:TT * H_FX].rearrange("p (i h) -> p i h", h=H_FX))
            nc.vector.tensor_copy(lf_nat[0:NS, TT, :], ps[0:NS, 6, TT * H_FX:(TT + 1) * H_FX]).then_inc(lf_copied, 1)
            dve.wait_ge(lf_copied, 1)

            def stage_k(j, i):
                nc.vector.tensor_copy(k_aug[j][0:DH, :], mix_tile(T_FK, i, slice(j * DH, (j + 1) * DH), slice(0, SEQ)))\
                    .then_inc(k_staged, 1)

            def maxima(h, j):
                for t in range(TT):
                    dve.wait_ge(fs_done, h * TT + (t + 1))
                    tile = ps[:, t, t * P:(t + 1) * P]
                    nc.vector.tensor_tensor(tile, tile, neg_mask[:, :], ALU.add).then_inc(fs_masked, 1)
                    dve.wait_ge(fs_masked, h * (2 * TT) + (2 * t + 1))
                    nc.vector.tensor_reduce(fx_max[:, j, t:t + 1], ps[:, t, 0:(t + 1) * P], AX_X, ALU.max)\
                        .then_inc(fs_masked, 1)
                    dve.wait_ge(fs_masked, h * (2 * TT) + (2 * t + 2))
                    nc.vector.tensor_scalar(fx_nmax[:, j, t:t + 1], fx_max[:, j, t:t + 1], -1.0, None,
                                            ALU.mult).then_inc(fs_max, 1)

            def normalise(h, j):
                for t in range(TT):
                    dve.wait_ge(fs_exp, h * TT + (t + 1))
                    nc.vector.reciprocal(fx_inv[:, j, t:t + 1], fx_sum[:, j, t:t + 1]).then_inc(fs_inv, 1)
                    dve.wait_ge(fs_inv, h * TT + (t + 1))
                    row = prob[j][:, t, 0:(t + 1) * P]
                    nc.vector.tensor_scalar(row, row, fx_inv[:, j, t:t + 1], None, ALU.mult).then_inc(fs_prob, 1)

            def copy_out(h, j, i):
                dve.wait_ge(fo_done, h + 1)
                nc.vector.tensor_copy(mix_tile(T_FV, i, slice(j * DH, (j + 1) * DH), slice(0, SEQ)),
                                      ps[0:DH, 6, :]).then_inc(fo_copied, 1)

            dve.wait_ge(aug_const, 8)
            for j in range(2):
                stage_k(j, 0)
            maxima(0, 0)
            normalise(0, 0)
            maxima(1, 1)
            normalise(1, 1)
            copy_out(0, 0, 0)
            with dve.Fori(1, H_FX // 2) as i:
                for j in range(2):
                    dve.wait_ge(fs_done, i * (2 * TT) + (j - 1) * TT)
                    stage_k(j, i)
                for j in range(2):
                    maxima(i * 2 + j, j)
                    normalise(i * 2 + j, j)
                    copy_out(i * 2 + (j - 1), 1 - j, i - (1 - j))
            copy_out(H_FX - 1, 1, H_FX // 2 - 1)
            new_rows_vector(dve)
            mid2_vector(dve)

        def mid_gpsimd(pool):
            def stage_v(h, j):
                src = v_nat[:, 0:TT, ds(h * DH, DH)]
                nc.gpsimd.tensor_copy(v_st[j][:, :, :], src).then_inc(v_staged, 1)

            pool.wait_ge(v_copied, TT + 1)
            for j in range(2):
                stage_v(j, j)
            with pool.Fori(1, H_FX // 2) as i:
                for j in range(2):
                    pool.wait_ge(fo_done, i * 2 + (j - 1))
                    stage_v(i * 2 + j, j)
            mid2_gpsimd(pool)

        tok_t = at("tok_t", [P, SEQ], I32, Z0 + (2 * KD + CHUNKS[0]) * ROW)
        tok_s = at("tok_s", [P, SEQ], I32, Z0 + (2 * KD + CHUNKS[0] + 1) * ROW)
        tok_x = at("tok_x", [P, SEQ], I32, Z0 + (2 * KD + CHUNKS[0] + 2) * ROW)
        tok_y = at("tok_y", [P, 2, SEQ], I32, Z0 + (2 * KD + CHUNKS[0] + 3) * ROW)
        iota_done, mask_step = sem("iota_done"), sem("mask_step")
        lb_step = sem("lb_step")

        def mix_prologue_scalar(act):
            act.wait_ge(lb_step, 1)
            nc.scalar.activation(lb[:, :], lb[:, :], ACT.Exp).then_inc(lb_step, 1)

        def mix_prologue(dve):
            dve.wait_ge(iota_done, 3)
            nc.vector.tensor_tensor(tok_t[:, :], tok_t[:, :], tok_s[:, :], ALU.bitwise_xor).then_inc(mask_step, 1)
            dve.wait_ge(mask_step, 1)
            nc.vector.tensor_tensor(tok_x[:, :], tok_t[:, :], tok_x[:, :], ALU.mult).then_inc(mask_step, 1)
            dve.wait_ge(mask_step, 2)
            nc.vector.tensor_scalar(hg_mask[:, DIAG, :], tok_t[:, :], 0.0, None, ALU.is_equal)
            for n, level in enumerate(LEVELS):
                nc.vector.tensor_scalar(tok_y[:, n % 2, :], tok_x[:, :], level, None,
                                        ALU.logical_shift_right).then_inc(mask_step, 1)
                dve.wait_ge(mask_step, 3 + n)
                nc.vector.tensor_scalar(hg_mask[:, n, :], tok_y[:, n % 2, :], 1.0, None, ALU.is_equal)
            dve.wait_ge(gains_landed, 16 * N_CONST_LOADS)
            nc.vector.tensor_tensor(lb[:, :], hg_lb[:, :], hg_lb[:, :], ALU.subtract).then_inc(lb_step, 1)
            dve.wait_ge(lb_step, 2)
            nc.vector.reciprocal(one_lb[:, :], lb[:, :]).then_inc(lb_step, 1)
            dve.wait_ge(lb_step, 3)
            nc.vector.tensor_tensor(lb[:, :], lb[:, :], one_lb[:, :], ALU.mult).then_inc(lb_step, 1)
            dve.wait_ge(lb_step, 4)
            nc.vector.tensor_tensor(lb[:, :], lb[:, :], lb[:, :], ALU.subtract).then_inc(lb_step, 1)
            dve.wait_ge(lb_step, 5)
            nc.vector.tensor_scalar(one_lb[:, :], lb[:, :], -1.0, 1.0, ALU.mult, ALU.add).then_inc(lb_step, 1)

        def make_mix_consts(pool):
            nc.gpsimd.iota(tok_t[:, :], pattern=[[0, TT], [1, P]], base=0, channel_multiplier=0).then_inc(iota_done, 1)
            nc.gpsimd.iota(tok_s[:, :], pattern=[[0, SEQ]], base=0, channel_multiplier=1).then_inc(iota_done, 1)
            nc.gpsimd.memset(tok_x[:, :], 1).then_inc(const_done, 1)
            pool.wait_ge(const_done, 1)
            nc.gpsimd.affine_select(tok_x[:, :], tok_x[:, :], pattern=[[0, TT], [1, P]], compare_op=ALU.is_gt, fill=0.0,
                                    base=0, channel_multiplier=-1).then_inc(iota_done, 1)
            nc.gpsimd.memset(neg_mask[:, :], 0.0).then_inc(const_done, 1)
            nc.gpsimd.memset(hg_reset[:, :], 1.0).then_inc(const_done, 1)
            nc.gpsimd.memset(fx_reset[:, :], 1.0).then_inc(const_done, 1)
            pool.wait_ge(const_done, 4)
            nc.gpsimd.affine_select(neg_mask[:, :], neg_mask[:, :], pattern=[[-1, P]], compare_op=ALU.is_ge, fill=NEG,
                                    base=0, channel_multiplier=1).then_inc(const_done, 1)
            nc.gpsimd.memset(hg_reset[:, 0:SEQ:P], 0.0).then_inc(const_done, 1)
            nc.gpsimd.memset(hg_reset[:, SEQ:T:DS_], 0.0).then_inc(const_done, 1)
            nc.gpsimd.memset(fx_reset[:, SEQ:T:DS_], 0.0).then_inc(const_done, 1)
            nc.gpsimd.memset(bmask[:, :], 1.0).then_inc(const_done, 1)
            pool.wait_ge(const_done, 9)
            nc.gpsimd.affine_select(bmask[:, :], bmask[:, :], pattern=[[-DS_, DB]], compare_op=ALU.is_ge, fill=0.0,
                                    base=0, channel_multiplier=1).then_inc(const_done, 1)
            pool.wait_ge(const_done, 10)
            nc.gpsimd.affine_select(bmask[:, :], bmask[:, :], pattern=[[DS_, DB]], compare_op=ALU.is_ge, fill=0.0,
                                    base=DS_ - 1, channel_multiplier=-1).then_inc(const_done, 1)
            pool.wait_ge(const_done, 11)
            nc.gpsimd.memset(d_sel[:, :], 1.0).then_inc(const_done, 1)
            nc.gpsimd.memset(d_causal[:, :], 0.0).then_inc(const_done, 1)
            pool.wait_ge(const_done, 13)
            nc.gpsimd.affine_select(two_heads[:, :].rearrange("p (a c) -> p a c", c=DH), ones[:, :].rearrange(
                "p (a c) -> p a c", c=DH), pattern=[[-DH, 2], [0, DH]], compare_op=ALU.is_ge, fill=0.0, base=0,
                channel_multiplier=1).then_inc(const_done, 1)
            nc.gpsimd.affine_select(d_later[:, :], ones[:, :], pattern=[[-1, P]], compare_op=ALU.is_ge, fill=0.0,
                                    base=0, channel_multiplier=1).then_inc(const_done, 1)
            nc.gpsimd.affine_select(d_sel[:, :], d_sel[:, :], pattern=[[-H_FX, DS_]], compare_op=ALU.is_ge, fill=0.0,
                                    base=0, channel_multiplier=1).then_inc(const_done, 1)
            nc.gpsimd.affine_select(d_causal[:, :], d_causal[:, :], pattern=[[-H_FX, DS_]], compare_op=ALU.is_ge,
                                    fill=NEG, base=0, channel_multiplier=1).then_inc(const_done, 1)
            pool.wait_ge(const_done, 17)
            nc.gpsimd.affine_select(two_heads[:, :].rearrange("p (a c) -> p a c", c=DH), two_heads[:, :].rearrange(
                "p (a c) -> p a c", c=DH), pattern=[[DH, 2], [0, DH]], compare_op=ALU.is_ge, fill=0.0, base=DH - 1,
                channel_multiplier=-1).then_inc(const_done, 1)
            nc.gpsimd.affine_select(d_later[:, :].rearrange("p (b g) -> p b g", g=PAGES), d_later[:, :].rearrange(
                "p (b g) -> p b g", g=PAGES), pattern=[[PAGES, DB], [0, PAGES]], compare_op=ALU.is_ge, fill=0.0,
                base=PAGES - 1, channel_multiplier=-1).then_inc(const_done, 1)
            nc.gpsimd.affine_select(d_sel[:, :], d_sel[:, :], pattern=[[H_FX, DS_]], compare_op=ALU.is_ge, fill=0.0,
                                    base=H_FX - 1, channel_multiplier=-1).then_inc(const_done, 1)
            pool.wait_ge(const_done, 20)
            pool.sem_inc(mix_consts, 1)

        class Steps:

            def __init__(self, name, steps):
                self.sem, self.steps = sem(name), steps.split()

            def after(self, step, turn):
                return turn * len(self.steps) + (self.steps.index(step) + 1)

        NL = len(LEVELS)
        S_LEVELS = [n for n, level in enumerate(LEVELS) if 2 ** (level + 1) <= DS_]
        h_act = Steps("hg_act", "exp_neg_f exp_neg_g stage_i ln_f ln_small exp_end exp_cum v_nat v_nat_s exp0 exp1 exp2 "
                      "k_nat k_nat_s exp3 exp4 exp5 exp6 out out_s ln_ms root out_hi")
        h_dve = Steps("hg_dve", "one_plus sigma f k log_f cum dend dend_s d0q d0k recip_g " +
                      " ".join((f"d{n + 1}q d{n + 1}k " if n + 1 < NL else "") + f"m{n}q m{n}k" +
                               (f" p{n - 1}" if n else "") + (" state0 state1 state2 state3" if n == 4 else "")
                               for n in range(NL)) +
                      f" p{NL - 1} p_diag ps0 ps1 ps2 snew ms r2 r3 r4 y y2 out_lo")
        h_pe = Steps("hg_pe", "it diag lv0 lv1 kt lv2 lv3 state lv4 lv5 lv6 lvs sstate out out_s ss")
        h_pool = Steps("hg_pool", "clip_f clip_small one_plus_g k_end q_cum v_wide sdec silu_g sq")

        ring_top[0] = RING
        h_f = buf("h_f", [P, T])
        h_k = buf("h_k", [P, T])
        h_c1 = buf("h_c1", [P, T])
        h_c2 = buf("h_c2", [P, T])
        h_A = buf("h_cum", [P, T])
        h_ex = [buf(f"h_ex{n}", [P, T]) for n in range(2)]
        h_qk = [buf(f"h_qk{n}", [P, T]) for n in range(2)]
        h_eA = buf("h_exp_cum", [P, T])
        h_qA = buf("h_q_cum", [P, T])
        h_kE = buf("h_k_end", [P, T])
        h_i = buf("h_values", [P, T])
        h_g = buf("h_gate", [P, T])
        h_o = buf("h_out", [P, T])
        h_ms = buf("h_ms", [P, T])
        h_r = buf("h_r", [P, T])
        h_v = buf("h_v_nat", [P, TT + 1, P])
        h_kn = buf("h_k_nat", [P, TT + 1, P])
        h_sc = buf("h_scores", [P, SEQ])
        h_scs = buf("h_scores_s", [NS, NS])
        h_S = buf("h_states", [P, TT, P])
        h_S0 = buf("h_states_in", [P, DB, P])
        h_Sn = buf("h_states_out", [P, DB, P])
        h_vw = buf("h_v_wide", [NS, DB, P])
        settled = const("settled", [P, NL + 5])
        bmask = const("bmask", [NS, DB])
        sc_zero, bmask_step = sem("sc_zero"), sem("bmask_step")
        S0_landed, S_stored, Sn_stored = sem("S0_landed"), sem("S_stored"), sem("Sn_stored")

        def mid2_sync(sp):
            sp.wait_ge(fo_copied, H_FX)
            sp.wait_ge(v_stored, 16 * (TT + 1))
            sp.wait_ge(lf_stored, 32)

            def load_states(h):
                sp.dma_start(h_S0[:, :, :], io["state_hgrn"][0].rearrange("b h k v -> k h b v")[:, ds(h, 1), :, :]
                             .rearrange("k o b v -> k (o b) v")).then_inc(S0_landed, 16)

            def store_states(h):
                sp.wait_ge(h_dve.sem, h_dve.after("state3", h))
                sp.dma_start(s_prompt[0, 0, ds(h, 1)].rearrange("o k v -> k (o v)"), h_S[:, TT - 1, :]).then_inc(S_stored, 16)
                sp.wait_ge(h_dve.sem, h_dve.after("snew", h))
                sp.dma_start(s_sample[0].rearrange("b h k v -> k h b v")[:, ds(h, 1), :, :]
                             .rearrange("k o b v -> k (o b) v"), h_Sn[:, :, :]).then_inc(Sn_stored, 16)

            load_states(0)
            store_states(0)
            with sp.Fori(1, H_HG) as i:
                sp.wait_ge(h_pe.sem, h_pe.after("out_s", i - 1))
                sp.wait_ge(h_pool.sem, h_pool.after("sdec", i - 1))
                load_states(i)
                store_states(i)
            mid3_sync(sp)

        def mid2_stores_waited(sp):
            sp.wait_ge(S_stored, 16 * H_HG)
            sp.wait_ge(Sn_stored, 16 * H_HG)
            mid3_stores_waited(sp)

        def mid2_tensor(pe):
            def chunk(t, c):
                return t[:, c * P:c * P + N_TOK[c]]

            def level(src_k, src_q, b):
                for c in range(TT):
                    mm = pe.matmul(ps[:, b, c * P:(c + 1) * P], chunk(src_k, c), chunk(src_q, c), start=True, stop=True)
                return mm

            def head(i, first=False):
                pe.wait_ge(h_act.sem, h_act.after("stage_i", i))
                if first:
                    pe.wait_ge(sc_zero, 2)
                    pe.wait_ge(fo_copied, H_FX)
                else:
                    pe.wait_ge(h_dve.sem, h_dve.after("out_lo", i - 1))
                for c in range(TT + 1):
                    b, c0 = (3, c * P) if c < TT else (4, 0)
                    mm = pe.transpose(ps[0:N_TOK[c], b, c0:c0 + P], chunk(h_i, c), ident[:, :])
                mm.then_inc(h_pe.sem, 1)
                pe.wait_ge(h_dve.sem, h_dve.after("k", i))
                level(h_k, mix_tile(T_Q, i), 2).then_inc(h_pe.sem, 1)

                def decayed(n):
                    pe.wait_ge(h_dve.sem, h_dve.after(f"m{n}k", i))
                    level(h_qk[n % 2], h_qk[n % 2], n % 2).then_inc(h_pe.sem, 1)

                decayed(0)
                decayed(1)
                pe.wait_ge(h_pool.sem, h_pool.after("k_end", i))
                pe.wait_ge(h_act.sem, h_act.after("v_nat_s", i))
                for c in range(TT + 1):
                    b, c0 = (3, c * P) if c < TT else (4, 0)
                    mm = pe.transpose(ps[0:N_TOK[c], b, c0:c0 + P], chunk(h_kE, c), ident[:, :])
                mm.then_inc(h_pe.sem, 1)
                decayed(2)
                decayed(3)
                pe.wait_ge(h_act.sem, h_act.after("k_nat_s", i))
                for c in range(TT):
                    mm = pe.matmul(ps[:, 5, c * P:(c + 1) * P], h_kn[:, c, :], h_v[:, c, :], start=True, stop=True)
                mm.then_inc(h_pe.sem, 1)
                for n in range(4, NL):
                    decayed(n)
                for m, n in enumerate(S_LEVELS):
                    s = h_qk[n % 2][:, SEQ:T]
                    pe.matmul(ps[0:NS, 7, m * NS:(m + 1) * NS], s, s, start=True, stop=True)
                m = len(S_LEVELS)
                pe.matmul(ps[0:NS, 7, m * NS:(m + 1) * NS], h_k[:, SEQ:T], mix_tile(T_Q, i, cols=slice(SEQ, T)),
                          start=True, stop=True).then_inc(h_pe.sem, 1)
                pe.wait_ge(h_pool.sem, h_pool.after("v_wide", i))
                for s in range(2):
                    mm = pe.matmul(ps[:, 3 + s, :], h_kn[0:NS, TT, :],
                                   h_vw[:, s * DB // 2:(s + 1) * DB // 2, :].rearrange("t b v -> t (b v)"),
                                   start=True, stop=True)
                mm.then_inc(h_pe.sem, 1)
                pe.wait_ge(h_dve.sem, h_dve.after("ps2", i))
                pe.wait_ge(h_pool.sem, h_pool.after("q_cum", i))
                for c in range(TT):
                    o = ps[:, 6, c * P:(c + 1) * P]
                    mm = pe.matmul(o, h_v[:, c, :], h_sc[:, c * P:(c + 1) * P], start=True, stop=(c == 0))
                    if c:
                        mm = pe.matmul(o, h_S[:, c - 1, :], chunk(h_qA, c), start=False, stop=True)
                mm.then_inc(h_pe.sem, 1)
                pe.wait_ge(S0_landed, i * 16 + 16)
                o = ps[:, 7, P:P + NS]
                pe.matmul(o, h_v[0:NS, TT, :], h_scs[:, :], start=True, stop=False, skip_group_check=True)
                for b in range(DB):
                    mm = pe.matmul(o[:, b * DS_:(b + 1) * DS_], h_S0[:, b, :], h_qA[:, SEQ + b * DS_:SEQ + (b + 1) * DS_],
                                   start=False, stop=(b == DB - 1), skip_group_check=True)
                mm.then_inc(h_pe.sem, 1)
                pe.wait_ge(h_pool.sem, h_pool.after("sq", i))
                pe.wait_ge(h_dve.sem, h_dve.after("snew", i))
                for s in range(2):
                    mm = pe.matmul(ps[:, s, 0:HALF], ones[:, :], h_ms[:, s * HALF:(s + 1) * HALF], start=True, stop=True)
                mm.then_inc(h_pe.sem, 1)

            head(0, first=True)
            with pe.Fori(1, H_HG) as i:
                head(i)
            mid3_tensor(pe)

        def mid2_scalar(act):
            def head(i, first=False):
                def go(out, src, func, **kw):
                    nc.scalar.activation(out, src, func, **kw).then_inc(h_act.sem, 1)

                if first:
                    act.wait_ge(fo_copied, H_FX)
                    act.wait_ge(v_stored, 16 * (TT + 1))
                    act.wait_ge(lf_stored, 32)
                    act.wait_ge(fo_done, H_FX)
                else:
                    act.wait_ge(h_dve.sem, h_dve.after("out_lo", i - 1))
                go(h_f[:, :], mix_tile(T_F, i), ACT.Exp, scale=-1.0)
                go(h_g[:, :], mix_tile(T_G, i), ACT.Exp, scale=-1.0)
                go(h_i[:, :], mix_tile(T_I, i), ACT.Copy)
                act.wait_ge(h_pool.sem, h_pool.after("clip_f", i))
                go(h_c1[:, :], h_c1[:, :], ACT.Ln)
                act.wait_ge(h_pool.sem, h_pool.after("clip_small", i))
                go(h_c2[:, :], h_c2[:, :], ACT.Ln, scale=2.0 ** 60)
                act.wait_ge(h_dve.sem, h_dve.after("dend_s", i))
                go(h_c1[:, :], h_c1[:, :], ACT.Exp)
                go(h_eA[:, :], h_A[:, :], ACT.Exp)
                act.wait_ge(h_pe.sem, h_pe.after("it", i))
                go(h_v[:, 0:TT, :].rearrange("p c v -> p (c v)"), ps[:, 3, :], ACT.Copy)
                go(h_v[0:NS, TT, :], ps[0:NS, 4, 0:P], ACT.Copy)

                def exps(n0, n1):
                    for n in range(n0, n1):
                        act.wait_ge(h_dve.sem, h_dve.after(f"d{n}k", i))
                        c = h_ex[n % 2][:, 0:SEQ if LEVELS[n] > 1 else T]
                        go(c, c, ACT.Exp)

                exps(0, 3)
                act.wait_ge(h_pe.sem, h_pe.after("kt", i))
                go(h_kn[:, 0:TT, :].rearrange("p c v -> p (c v)"), ps[:, 3, :], ACT.Copy)
                go(h_kn[0:NS, TT, :], ps[0:NS, 4, 0:P], ACT.Copy)
                exps(3, NL)
                act.wait_ge(h_pe.sem, h_pe.after("out", i))
                go(h_o[:, 0:SEQ], ps[:, 6, :], ACT.Copy)
                act.wait_ge(h_pe.sem, h_pe.after("out_s", i))
                go(h_o[:, SEQ:T], ps[:, 7, P:P + NS], ACT.Copy)
                act.wait_ge(h_dve.sem, h_dve.after("ms", i))
                go(h_r[:, :], h_ms[:, :], ACT.Ln)
                act.wait_ge(h_act.sem, h_act.after("ln_ms", i))
                go(h_r[:, :], h_r[:, :], ACT.Exp, scale=-0.5)
                act.wait_ge(h_dve.sem, h_dve.after("y2", i))
                go(o_hi[:, ds(i, 1), :].rearrange("p o t -> p (o t)"), h_o[:, :], ACT.Copy)

            head(0, first=True)
            with act.Fori(1, H_HG) as i:
                head(i)
            mid3_scalar(act)

        def mid2_vector(dve):
            def blocks(t, level, c):
                m = 2 ** level
                v = t[:, 0:c].rearrange("p (b h m) -> p b h m", h=2, m=m)
                return v[:, :, 0, :], v[:, :, 1, :], v[:, :, 0, m - 1:m].to_broadcast([P, c // (2 * m), m])

            dve.wait_ge(fo_done, H_FX)
            nc.vector.memset(h_sc[:, :], 0.0).then_inc(sc_zero, 1)
            nc.vector.memset(h_scs[:, :], 0.0).then_inc(sc_zero, 1)
            dve.wait_ge(sc_zero, 2)

            def head(i, first=False):
                def own(step, turn=i):
                    dve.wait_ge(h_dve.sem, h_dve.after(step, turn))

                def act_done(step):
                    dve.wait_ge(h_act.sem, h_act.after(step, i))

                def pe_done(step):
                    dve.wait_ge(h_pe.sem, h_pe.after(step, i))

                def pool_done(step):
                    dve.wait_ge(h_pool.sem, h_pool.after(step, i))

                act_done("exp_neg_f")
                nc.vector.tensor_scalar(h_f[:, :], h_f[:, :], 1.0, None, ALU.add).then_inc(h_dve.sem, 1)
                own("one_plus")
                nc.vector.reciprocal(h_f[:, :], h_f[:, :]).then_inc(h_dve.sem, 1)
                own("sigma")
                nc.vector.tensor_scalar(h_f[:, :], h_f[:, :], one_lb[:, ds(i, 1)], lb[:, ds(i, 1)], ALU.mult,
                                        ALU.add).then_inc(h_dve.sem, 1)
                own("f")
                nc.vector.tensor_scalar(h_k[:, :], h_f[:, :], -1.0, 1.0, ALU.mult, ALU.add).then_inc(h_dve.sem, 1)
                act_done("ln_small")
                nc.vector.tensor_tensor(h_c1[:, :], h_c1[:, :], h_c2[:, :], ALU.add).then_inc(h_dve.sem, 1)
                own("log_f")
                nc.vector.tensor_tensor_scan(h_A[:, :], hg_reset[:, :], h_c1[:, :], 0.0, ALU.mult,
                                             ALU.add).then_inc(h_dve.sem, 1)
                own("cum")

                def diffs(n):
                    c = SEQ if LEVELS[n] > 1 else T
                    a_k, a_q, a_r = blocks(h_A, LEVELS[n], c)
                    d_k, d_q, _ = blocks(h_ex[n % 2], LEVELS[n], c)
                    nc.vector.tensor_tensor(d_q, a_q, a_r, ALU.subtract).then_inc(h_dve.sem, 1)
                    nc.vector.tensor_tensor(d_k, a_r, a_k, ALU.subtract).then_inc(h_dve.sem, 1)

                def decayed(n):
                    c = SEQ if LEVELS[n] > 1 else T
                    act_done(f"exp{n}")
                    if n >= 2:
                        pe_done(f"lv{n - 2}")
                    e_k, e_q, _ = blocks(h_ex[n % 2], LEVELS[n], c)
                    k, _, _ = blocks(h_k, LEVELS[n], c)
                    _, q, _ = blocks(mix_tile(T_Q, i), LEVELS[n], c)
                    o_k, o_q, _ = blocks(h_qk[n % 2], LEVELS[n], c)
                    nc.vector.tensor_tensor(o_q, q, e_q, ALU.mult).then_inc(h_dve.sem, 1)
                    nc.vector.tensor_tensor(o_k, k, e_k, ALU.mult).then_inc(h_dve.sem, 1)

                def settle(n):
                    nc.vector.memset(settled[:, n:n + 1], 0.0)

                def pick(n):
                    pe_done(f"lv{n}")
                    if n:
                        own(f"p{n - 1}")
                    settle(n)
                    nc.vector.copy_predicated(h_sc[:, :], hg_mask[:, n, :], ps[:, n % 2, :]).then_inc(h_dve.sem, 1)

                end = h_A[:, P - 1:SEQ:P].rearrange("p (c o) -> p c o", o=1)
                ends = h_A[:, SEQ + DS_ - 1:T:DS_].rearrange("p (c o) -> p c o", o=1)
                nc.vector.tensor_tensor(h_c1[:, 0:SEQ].rearrange("p (c t) -> p c t", t=P), end.to_broadcast([P, TT, P]),
                                        h_A[:, 0:SEQ].rearrange("p (c t) -> p c t", t=P), ALU.subtract).then_inc(h_dve.sem, 1)
                nc.vector.tensor_tensor(h_c1[:, SEQ:T].rearrange("p (c t) -> p c t", t=DS_),
                                        ends.to_broadcast([P, DB, DS_]),
                                        h_A[:, SEQ:T].rearrange("p (c t) -> p c t", t=DS_), ALU.subtract).then_inc(h_dve.sem, 1)
                diffs(0)
                pool_done("one_plus_g")
                nc.vector.reciprocal(h_g[:, :], h_g[:, :]).then_inc(h_dve.sem, 1)
                for n in range(NL):
                    if n + 1 < NL:
                        if n:
                            own(f"m{n - 1}k")
                        diffs(n + 1)
                    decayed(n)
                    if n:
                        pick(n - 1)
                    if n == 4:
                        pe_done("state")
                        act_done("exp_cum")
                        if not first:
                            dve.wait_ge(S_stored, i * 16)
                        for c in range(TT):
                            new = ps[:, 5, c * P:(c + 1) * P]
                            if c == 0:
                                nc.vector.tensor_copy(h_S[:, 0, :], new).then_inc(h_dve.sem, 1)
                                continue
                            own(f"state{c - 1}")
                            nc.vector.scalar_tensor_tensor(h_S[:, c, :], h_S[:, c - 1, :],
                                                           h_eA[:, c * P + P - 1:c * P + P], new, ALU.mult,
                                                           ALU.add).then_inc(h_dve.sem, 1)
                pick(NL - 1)
                pe_done("diag")
                own(f"p{NL - 1}")
                settle(NL)
                nc.vector.copy_predicated(h_sc[:, :], hg_mask[:, DIAG, :], ps[:, 2, :]).then_inc(h_dve.sem, 1)
                pe_done("lvs")
                for m, n in enumerate(S_LEVELS + [DIAG]):
                    if m:
                        own(f"ps{m - 1}")
                    settle(NL + 1 + m)
                    nc.vector.copy_predicated(h_scs[:, :], hg_mask[0:NS, n, 0:NS], ps[0:NS, 7, m * NS:(m + 1) * NS])\
                        .then_inc(h_dve.sem, 1)
                pe_done("sstate")
                pool_done("sdec")
                flat = h_Sn[:, :, :].rearrange("p b v -> p (b v)")
                nc.vector.tensor_tensor(flat, flat, ps[:, 3:5, :].rearrange("p b c -> p (b c)"), ALU.add)\
                    .then_inc(h_dve.sem, 1)
                pe_done("ss")
                nc.vector.tensor_scalar(halves(h_ms[:, :]), ps[:, 0:2, 0:HALF], 1.0 / P, EPS, ALU.mult, ALU.add)\
                    .then_inc(h_dve.sem, 1)
                act_done("root")
                nc.vector.tensor_tensor(h_c2[:, :], h_r[:, :], h_r[:, :], ALU.mult).then_inc(h_dve.sem, 1)
                own("r2")
                nc.vector.scalar_tensor_tensor(h_c2[:, :], h_c2[:, :], -0.5, h_ms[:, :], ALU.mult, ALU.mult)\
                    .then_inc(h_dve.sem, 1)
                own("r3")
                nc.vector.scalar_tensor_tensor(h_r[:, :], h_c2[:, :], 1.5, h_r[:, :], ALU.add, ALU.mult)\
                    .then_inc(h_dve.sem, 1)
                own("r4")
                pool_done("sq")
                nc.vector.scalar_tensor_tensor(h_o[:, :], h_o[:, :], hg_gain[:, ds(i, 1)], h_r[:, :], ALU.mult, ALU.mult)\
                    .then_inc(h_dve.sem, 1)
                own("y")
                nc.vector.tensor_tensor(h_o[:, :], h_o[:, :], h_g[:, :], ALU.mult).then_inc(h_dve.sem, 1)
                act_done("out_hi")
                nc.vector.tensor_tensor(o_lo[:, ds(i, 1), :].rearrange("p o t -> p (o t)"), h_o[:, :],
                                        o_hi[:, ds(i, 1), :].rearrange("p o t -> p (o t)").bitcast(F32),
                                        ALU.subtract).then_inc(h_dve.sem, 1)

            head(0, first=True)
            with dve.Fori(1, H_HG) as i:
                head(i)
            mid3_vector(dve)

        def mid2_gpsimd(pool):
            def head(i, first=False):
                def go(op):
                    op.then_inc(h_pool.sem, 1)

                def dve_done(step, turn=i):
                    pool.wait_ge(h_dve.sem, h_dve.after(step, turn))

                dve_done("f")
                nc.gpsimd.tensor_tensor(settled[:, NL + 4:NL + 5], ones[:, 0:1], ones[:, 1:2], ALU.mult)
                go(nc.gpsimd.tensor_scalar(h_c1[:, :], h_f[:, :], 2.0 ** -60, None, ALU.max))
                go(nc.gpsimd.tensor_scalar(h_c2[:, :], h_f[:, :], 2.0 ** -60, TINY, ALU.min, ALU.max))
                pool.wait_ge(h_act.sem, h_act.after("exp_neg_g", i))
                go(nc.gpsimd.tensor_tensor(h_g[:, :], h_g[:, :], ones[:, 0:1].to_broadcast([P, T]), ALU.add))
                pool.wait_ge(h_act.sem, h_act.after("exp_end", i))
                go(nc.gpsimd.tensor_tensor(h_kE[:, :], h_k[:, :], h_c1[:, :], ALU.mult))
                pool.wait_ge(h_act.sem, h_act.after("exp_cum", i))
                go(nc.gpsimd.tensor_tensor(h_qA[:, :], mix_tile(T_Q, i), h_eA[:, :], ALU.mult))
                pool.wait_ge(h_act.sem, h_act.after("v_nat_s", i))
                go(nc.gpsimd.tensor_tensor(h_vw[:, :, :], h_v[0:NS, TT:TT + 1, :].to_broadcast([NS, DB, P]),
                                           bmask[:, :].rearrange("t (b o) -> t b o", o=1).to_broadcast([NS, DB, P]), ALU.mult))
                pool.wait_ge(S0_landed, i * 16 + 16)
                if not first:
                    pool.wait_ge(Sn_stored, i * 16)
                dec = h_eA[:, SEQ + DS_ - 1:T:DS_].rearrange("p (b o) -> p b o", o=1).to_broadcast([P, DB, P])
                go(nc.gpsimd.tensor_tensor(h_Sn[:, :, :], h_S0[:, :, :], dec, ALU.mult))
                dve_done("recip_g")
                go(nc.gpsimd.tensor_tensor(h_g[:, :], h_g[:, :], mix_tile(T_G, i), ALU.mult))
                pool.wait_ge(h_act.sem, h_act.after("out_s", i))
                go(nc.gpsimd.tensor_tensor(h_ms[:, :], h_o[:, :], h_o[:, :], ALU.mult))

            head(0, first=True)
            with pool.Fori(1, H_HG) as i:
                head(i)
            mid3_gpsimd(pool)

        NR = DS_ * H_FX
        NB2 = 2 * NR
        GR = 4
        N_GR = PAGES // GR
        NJ = D_FX // P
        ITEMS = N_GR * NJ
        V_FIRST = 6
        V_AFTER = {n: [] for n in range(ITEMS)}
        for n in range(V_FIRST, ITEMS):
            extra = PAGES - (ITEMS - V_FIRST)
            at_ = n - V_FIRST
            V_AFTER[n] = [2 * at_, 2 * at_ + 1] if at_ < extra else [extra + at_]
        SCORES_AT = {6: 0, 10: 1, 14: 2}

        z_top = [Z0 + 2 * KD * ROW]

        def zbuf(name, shape, dt=F32):
            t = at(name, shape, dt, z_top[0])
            z_top[0] += int(np.prod(shape[1:])) * 4
            assert z_top[0] <= Z0 + 2 * KD * ROW + T_FQ * ROW
            return t

        ring_top[0] = RING
        d_k = [buf(f"d_keys{n}", [P, GR, D_FX]) for n in range(2)]
        d_v = [buf(f"d_values{n}", [P, GR, D_FX]) for n in range(2)]
        d_kh = buf("d_keysT_hi", [P, NJ, GR * PAGE], F32R)
        d_kl = buf("d_keysT_lo", [P, NJ, GR * PAGE], F32R)
        d_vh = buf("d_values_hi", [P, 4, D_FX], F32R)
        d_vl = buf("d_values_lo", [P, 4, D_FX], F32R)
        d_q = buf("d_queries", [P, NJ * (NB2 + 2)], F32R)
        d_pT = buf("d_probT", [P, PAGES, NB2], F32R)
        d_sfx = zbuf("d_suffix", [NR, PAST])
        d_s = zbuf("d_scores", [NR, PAST + NS])
        d_lf = zbuf("d_log_f", [P, PAGE * H_FX])
        d_inc = zbuf("d_log_f_sums", [P, H_FX, PAGE])
        d_x = zbuf("d_scores_lo", [NR, D_FX])
        d_ox = zbuf("d_out_lo", [NR, D_FX])
        d_o = zbuf("d_out", [NR, D_FX])
        d_od = zbuf("d_out_own", [NR, DB, DH])
        d_tot = zbuf("d_page_sums", [P, H_FX])
        ring_top[0] = RING
        fn_q = [buf(f"fn_q{n}", [P, T]) for n in range(2)]
        fn_m = [buf(f"fn_m{n}", [P, T]) for n in range(2)]
        fn_r = [buf(f"fn_r{n}", [P, T]) for n in range(2)]
        d_pTn = zbuf("d_probT_new", [NS, NB2], F32R)
        d_knh = zbuf("d_new_keys_hi", [P, NJ, NS], F32R)
        d_knl = zbuf("d_new_keys_lo", [P, NJ, NS], F32R)
        d_vnh = at("d_new_values_hi", [NS, D_FX], F32R, SUMSQ_AT)
        d_vnl = at("d_new_values_lo", [NS, D_FX], F32R, SQ_AT)
        d_nb = const("d_new_bias", [NR, DB * (NS + DS_)])
        d_cum = const("d_cum_rows", [NR, NS])
        d_cq = const("d_cum_query", [NR, DB])
        d_e8 = const("d_spread", [H_FX, NR])
        d_hm = const("d_head_mask", [NR, H_FX])
        d_sel = const("d_step_mask", [NR, DS_])
        d_causal = const("d_causal", [NR, DS_])
        d_cqx = const("d_cum_pick", [NR, DB, DS_])
        d_later = const("d_later_pages", [P, P])
        d_small = const("d_small", [NR, 4])
        suf_d = nc.dram_tensor("suffix_scratch", (DB * PAGES, H_FX, PAGE), F32, kind="Internal").ap()

        dc_step = sem("dc_step")
        dcx_done = sem("dcx_done")
        dvn_hi, dvn_lo = sem("dvn_hi"), sem("dvn_lo")
        lf_landed, lf_scan, tot_done, suf_ready, suf_stored = (sem(n) for n in (
            "lf_landed", "lf_scan", "tot_done", "suf_ready", "suf_stored"))
        dk_landed = [sem(f"dk_landed{n}") for n in range(2)]
        dv_landed = [sem(f"dv_landed{n}") for n in range(2)]
        sfx_landed = sem("sfx_landed")
        dq_zero, dkn_hi, dkn_lo = sem("dq_zero"), sem("dkn_hi"), sem("dkn_lo")
        qh_done, ql_done = sem("qh_done"), sem("ql_done")
        kT_done, kh_done, kl_done, qk_done, new_done = (sem(n) for n in (
            "kT_done", "kh_done", "kl_done", "qk_done", "new_done"))
        sx_done, s1_done, s2_done = sem("sx_done"), sem("s1_done"), sem("s2_done")
        dmx_done, dexp_done, dinv_done = sem("dmx_done"), sem("dexp_done"), sem("dinv_done")
        pT_done, pth_done, ptl_done = sem("pT_done"), sem("pth_done"), sem("ptl_done")
        vh_done, vl_done, pv_done = sem("vh_done"), sem("vl_done"), sem("pv_done")
        ox_done, o_step, oT_done, oF_done = sem("ox_done"), sem("o_step"), sem("oT_done"), sem("oF_done")
        fn_sq, fn_ss, fn_v, fn_a, fn_hi, fn_lo = (sem(n) for n in ("fn_sq", "fn_ss", "fn_v", "fn_a", "fn_hi", "fn_lo"))
        N_SC = N_GR + 1

        def mid3_sync(sp):
            sp.wait_ge(h_dve.sem, h_dve.after("out_lo", H_HG - 1))
            sp.wait_ge(S_stored, 16 * H_HG)
            sp.wait_ge(Sn_stored, 16 * H_HG)

            def page_loads(b, g, cache, dst, landed):
                for m in range(GR):
                    page = sp.value_load(page_row[0:1, ds(b * PAGES + (g * GR + m), 1)], min_val=0, max_val=N_POOL - 1)
                    sp.dma_start(dst[g % 2][:, m, :], cache[0, ds(page, 1)].rearrange("o s h d -> (o s) (h d)"))\
                        .then_inc(landed[g % 2], 16)

            def keys(b, g, free=None):
                if free is not None:
                    sp.wait_ge(kT_done, free)
                page_loads(b, g, io["cache_k"], d_k, dk_landed)

            def values(b, g, free=None):
                if free is not None:
                    sp.wait_ge(vl_done, free)
                page_loads(b, g, io["cache_v"], d_v, dv_landed)

            def suffix(b, free=None):
                if free is not None:
                    sp.wait_ge(s1_done, free)
                for t in range(DS_):
                    sp.dma_start(d_sfx[t * H_FX:(t + 1) * H_FX, :].rearrange("h (g s) -> h g s", s=PAGE),
                                 suf_d[ds(b * PAGES, PAGES)].rearrange("g h s -> h g s")).then_inc(sfx_landed, 16)

            keys(0, 0)
            keys(0, 1)
            sp.wait_ge(suf_ready, 1)
            sp.dma_start(suf_d, d_inc[:, :, :]).then_inc(suf_stored, 16)
            sp.wait_ge(suf_stored, 16)
            suffix(0)

            def turn(b, first=False):
                keys(b, 2, b * ITEMS + NJ)
                keys(b, 3, b * ITEMS + 2 * NJ)
                if not first:
                    values(b - 1, 2, (b - 1) * PAGES + GR)
                    values(b - 1, 3, (b - 1) * PAGES + 2 * GR)

            def next_turn(b, first=False):
                keys(b + 1, 0, b * ITEMS + 3 * NJ)
                values(b, 0, None if first else (b - 1) * PAGES + 3 * GR)
                keys(b + 1, 1, b * ITEMS + 4 * NJ)
                values(b, 1, None if first else (b - 1) * PAGES + 4 * GR)
                suffix(b + 1, b * N_SC + N_GR)

            turn(0, True)
            next_turn(0, True)
            with sp.Fori(1, DB - 1) as b:
                turn(b)
                next_turn(b)
            turn(DB - 1)
            values(DB - 1, 0, (DB - 2) * PAGES + 3 * GR)
            values(DB - 1, 1, (DB - 2) * PAGES + 4 * GR)
            values(DB - 1, 2, (DB - 1) * PAGES + GR)
            values(DB - 1, 3, (DB - 1) * PAGES + 2 * GR)
            sp.wait_ge(vl_done, DB * PAGES)
            sp.wait_ge(pv_done, DB * (PAGES + 1))
            sp.wait_ge(fn_lo, NJ)

        def mid3_stores_waited(sp):
            pass

        def new_rows_tensor(pe):
            pe.wait_ge(dc_step, 1)
            pe.wait_ge(fx_step, 8)
            pe.wait_ge(lf_copied, 1)
            pe.matmul(ps[0:NR, 7, 0:NS], d_e8[:, :], fx_cum[:, SEQ:T], start=True, stop=True).then_inc(dcx_done, 1)

        def new_rows_vector(dve):
            nc.vector.tensor_copy(d_e8[:, :].rearrange("k (t h) -> k t h", h=H_FX),
                                  ident[0:H_FX, 0:H_FX].rearrange("k (o h) -> k o h", o=1).to_broadcast([H_FX, DS_, H_FX]))\
                .then_inc(dc_step, 1)
            nc.vector.tensor_reduce(d_hm[:, :], ident[0:NR, 0:NR].rearrange("p (t h) -> p h t", h=H_FX), AX_X,
                                    ALU.add).then_inc(dc_step, 1)
            nc.vector.memset(d_nb[:, :], NEG).then_inc(dc_step, 1)
            dve.wait_ge(dvn_hi, 1)
            nc.vector.tensor_tensor(d_vnl[:, :], v_nat[0:NS, TT, :], d_vnh[:, :].bitcast(F32), ALU.subtract)\
                .then_inc(dvn_lo, 1)
            dve.wait_ge(dcx_done, 1)
            nc.vector.tensor_copy(d_cum[:, :], ps[0:NR, 7, 0:NS]).then_inc(dc_step, 1)
            dve.wait_ge(dc_step, 4)
            own = d_cum[:, :].rearrange("p (b s) -> p b s", s=DS_)

            def each(t):
                return t[:, :].rearrange("p (o s) -> p o s", o=1).to_broadcast([NR, DB, DS_])

            nc.vector.tensor_tensor(d_cqx[:, :, :], own, each(d_sel), ALU.mult).then_inc(dc_step, 1)
            nc.vector.tensor_tensor(d_nb[:, :].rearrange("p (b c) -> p b c", b=DB)[:, :, 0:DS_], each(d_causal), own,
                                    ALU.subtract).then_inc(dc_step, 1)
            dve.wait_ge(dc_step, 6)
            nc.vector.tensor_reduce(d_cq[:, :], d_cqx[:, :, :], AX_X, ALU.add).then_inc(dc_step, 1)

        def new_rows_scalar(act):
            act.wait_ge(v_copied, TT + 1)
            nc.scalar.activation(d_vnh[:, :], v_nat[0:NS, TT, :], ACT.Copy).then_inc(dvn_hi, 1)

        def mid3_tensor(pe):
            def items(b):
                return b * ITEMS

            def keysT(b, n):
                g, j = divmod(n, NJ)
                if j == 0:
                    pe.wait_ge(dk_landed[g % 2], b * (2 * GR * 16) + (g // 2 + 1) * GR * 16)
                if not (isinstance(b, int) and b == 0 and n < 4):
                    pe.wait_ge(kl_done, items(b) + (n - 3))
                for m in range(GR):
                    mm = pe.transpose(ps[:, j, m * PAGE:(m + 1) * PAGE], d_k[g % 2][:, m, j * P:(j + 1) * P], ident[:, :])
                mm.then_inc(kT_done, 1)

            def qk(b, n):
                g, j = divmod(n, NJ)
                if n == 0:
                    pe.wait_ge(ql_done, b * 2 + 2)
                if j == 0 and not (isinstance(b, int) and b == 0 and g < 2):
                    last = {0: 0, 1: -1, 2: 1, 3: 2}[g]
                    pe.wait_ge(s1_done, b * N_SC + last)
                    pe.wait_ge(sx_done, b * N_SC + last)
                    if g == 1:
                        pe.wait_ge(ptl_done, b * 2)
                pe.wait_ge(kl_done, items(b) + (n + 1))
                q = d_q[:, j * NB2:(j + 1) * NB2]
                pe.matmul(ps[0:NB2, 4 + g % 2, :], q, d_kh[:, j, :], start=(j == 0), stop=False, skip_group_check=True)
                pe.matmul(ps[0:NR, 4 + g % 2, :], q[:, 0:NR], d_kl[:, j, :], start=False, stop=(j == NJ - 1),
                          skip_group_check=True).then_inc(qk_done, 1)

            def new_keys(b):
                pe.wait_ge(s1_done, b * N_SC + 3)
                pe.wait_ge(sx_done, b * N_SC + 3)
                for j in range(NJ):
                    q = d_q[:, j * NB2:(j + 1) * NB2]
                    pe.matmul(ps[0:NB2, 4, 0:NS], q, d_knh[:, j, :], start=(j == 0), stop=False, skip_group_check=True)
                    mm = pe.matmul(ps[0:NR, 4, 0:NS], q[:, 0:NR], d_knl[:, j, :], start=False, stop=(j == NJ - 1),
                                   skip_group_check=True)
                mm.then_inc(new_done, 1)

            def probsT(b):
                for m in range(PAGES):
                    pe.transpose(ps[:, 7, m * NR:(m + 1) * NR], d_s[:, m * PAGE:(m + 1) * PAGE], ident[0:NR, 0:NR])
                pe.transpose(ps[0:NS, 5, 0:NR], d_s[:, PAST:PAST + NS], ident[0:NR, 0:NR]).then_inc(pT_done, 1)

            def pv(b, m):
                if m == 0:
                    pe.wait_ge(ptl_done, b * 2 + 2)
                    pe.wait_ge(vl_done, b * PAGES + 1)
                elif m < PAGES:
                    pe.wait_ge(vl_done, b * PAGES + (m + 1))
                hi, lo, p = (d_vh[:, m % 4, :], d_vl[:, m % 4, :], d_pT[:, m, :]) if m < PAGES else \
                    (d_vnh[:, :], d_vnl[:, :], d_pTn[:, :])
                pe.matmul(ps[0:NB2, 6, :], p, hi, start=(m == 0), stop=False, skip_group_check=True)
                pe.matmul(ps[0:NR, 6, :], p[:, 0:NR], lo, start=False, stop=(m == PAGES), skip_group_check=True)\
                    .then_inc(pv_done, 1)

            def turn(b, with_keys=True, with_values=True):
                for n in range(ITEMS):
                    if with_keys:
                        keysT(b, n)
                    if with_values and n == 3:
                        pe.wait_ge(dexp_done, b)
                    if with_keys and n >= 2:
                        qk(b, n - 2)
                    if with_values:
                        if n == 3:
                            probsT(b - 1)
                        for m in V_AFTER[n]:
                            pv(b - 1, m)
                if with_keys:
                    qk(b, ITEMS - 2)
                    qk(b, ITEMS - 1)
                    new_keys(b)
                if with_values:
                    pv(b - 1, PAGES)

            pe.wait_ge(lf_scan, H_FX)
            pe.matmul(ps[:, 7, 0:H_FX], d_later[:, :], d_tot[:, :], start=True, stop=True).then_inc(tot_done, 1)
            pe.wait_ge(dkn_lo, 1)
            turn(0, with_values=False)
            with pe.Fori(1, DB) as b:
                turn(b)
            turn(DB, with_keys=False)
            pe.wait_ge(o_step, 3 * DB)
            for b in range(DB):
                mm = pe.transpose(ps[0:DH, 4, b * NR:(b + 1) * NR], d_od[:, b, :], ident[0:NR, 0:NR])
            mm.then_inc(oT_done, 1)
            for i in range(NJ):
                pe.wait_ge(fn_sq, i + 1)
                b0 = 2 * (i % 2)
                if i >= 2:
                    pe.wait_ge(fn_v, 5 * (i - 2) + 1)
                for s in range(2):
                    mm = pe.matmul(ps[:, b0 + s, 0:HALF], two_heads[:, :], fn_q[i % 2][:, s * HALF:(s + 1) * HALF],
                                   start=True, stop=True)
                mm.then_inc(fn_ss, 1)
            pe.wait_ge(fn_lo, NJ)

        def mid3_scalar(act):
            act.wait_ge(h_dve.sem, h_dve.after("out_lo", H_HG - 1))
            nc.scalar.activation(d_knh[:, :, :], pT[:, T_FK:T_FK + NJ, SEQ:T], ACT.Copy).then_inc(dkn_hi, 1)
            act.wait_ge(dq_zero, 1)

            def turn(b, with_keys=True, with_values=True):
                if with_keys:
                    if not (isinstance(b, int) and b == 0):
                        act.wait_ge(new_done, b)
                    for p in range(2):
                        half = slice(p * DH, (p + 1) * DH)
                        dst = d_q[half, :].rearrange("k (j c) -> k j c", j=NJ)[:, :, p:p + NR:H_FX]
                        nc.scalar.activation(dst, pT[half, T_FQ:T_FQ + NJ, ds(b * DS_ + SEQ, DS_)], ACT.Copy,
                                             scale=SCALE).then_inc(qh_done, 1)
                for n in range(ITEMS):
                    if with_keys:
                        act.wait_ge(kT_done, b * ITEMS + (n + 1))
                        if not (isinstance(b, int) and b == 0 and n < 4):
                            act.wait_ge(qk_done, b * ITEMS + (n - 3))
                        nc.scalar.activation(d_kh[:, n % NJ, :], ps[:, n % NJ, :], ACT.Copy).then_inc(kh_done, 1)
                    if with_values:
                        if n == 1:
                            act.wait_ge(dmx_done, (b - 1) * 2 + 2)
                            nc.scalar.activation(d_s[:, :], d_s[:, :], ACT.Exp, bias=d_small[:, 1:2],
                                                 accum_out=d_small[:, 2:3]).then_inc(dexp_done, 1)
                        if n == V_FIRST - 1:
                            act.wait_ge(pT_done, b)
                            nc.scalar.activation(d_pT[:, :, 0:NR], ps[:, 7, :].rearrange("s (g r) -> s g r", r=NR),
                                                 ACT.Copy).then_inc(pth_done, 1)
                            nc.scalar.activation(d_pTn[:, 0:NR], ps[0:NS, 5, 0:NR], ACT.Copy).then_inc(pth_done, 1)
                    if with_keys and n in SCORES_AT:
                        scores_low(b, SCORES_AT[n])
                    if with_values:
                        for m in V_AFTER[n]:
                            if m % GR == 0:
                                g = m // GR
                                act.wait_ge(dv_landed[g % 2], (b - 1) * (2 * GR * 16) + (g // 2 + 1) * GR * 16)
                            if m >= 4:
                                act.wait_ge(pv_done, (b - 1) * (PAGES + 1) + (m - 3))
                            nc.scalar.activation(d_vh[:, m % 4, :], d_v[m // GR % 2][:, m % GR, :], ACT.Copy)\
                                .then_inc(vh_done, 1)
                if with_keys:
                    scores_low(b, N_GR - 1)
                    act.wait_ge(new_done, b + 1)
                    if_free(b, N_GR)
                    nc.scalar.activation(d_x[:, 0:NS], ps[NR:NB2, 4, 0:NS], ACT.Copy).then_inc(sx_done, 1)
                if with_values:
                    act.wait_ge(pv_done, b * (PAGES + 1))
                    nc.scalar.activation(d_ox[:, :], ps[NR:NB2, 6, :], ACT.Copy).then_inc(ox_done, 1)

            def if_free(b, g):
                if not (isinstance(b, int) and b == 0 and g == 0):
                    act.wait_ge(s2_done, b * N_SC + g)

            def scores_low(b, g):
                act.wait_ge(qk_done, b * ITEMS + (g + 1) * NJ)
                if_free(b, g)
                nc.scalar.activation(d_x[:, :], ps[NR:NB2, 4 + g % 2, :], ACT.Copy).then_inc(sx_done, 1)

            turn(0, with_values=False)
            with act.Fori(1, DB) as b:
                turn(b)
            turn(DB, with_keys=False)
            for i in range(NJ):
                act.wait_ge(fn_v, 5 * i + 1)
                nc.scalar.activation(fn_r[i % 2][:, :], fn_m[i % 2][:, :], ACT.Ln).then_inc(fn_a, 1)
                act.wait_ge(fn_a, 2 * i + 1)
                nc.scalar.activation(fn_r[i % 2][:, :], fn_r[i % 2][:, :], ACT.Exp, scale=-0.5).then_inc(fn_a, 1)
                act.wait_ge(fn_v, 5 * i + 5)
                nc.scalar.activation(o_hi[:, H_HG + i, :], oF[:, T_FV + i, :], ACT.Copy).then_inc(fn_hi, 1)

        def mid3_vector(dve):
            dve.wait_ge(h_dve.sem, h_dve.after("out_lo", H_HG - 1))
            nc.vector.memset(d_q[:, :].bitcast(F32), 0.0).then_inc(dq_zero, 1)
            dve.wait_ge(lf_landed, 16)
            for h in range(H_FX):
                x = d_lf[:, h:PAGE * H_FX:H_FX]
                nc.vector.tensor_tensor_scan(d_inc[:, h, :], ones[:, :], x, 0.0, ALU.mult, ALU.add)
                op = nc.vector.tensor_reduce(d_tot[:, h:h + 1], x, AX_X, ALU.add)
                op.then_inc(lf_scan, 1)
            dve.wait_ge(tot_done, 1)
            nc.vector.tensor_copy(d_tot[:, :], ps[:, 7, 0:H_FX]).then_inc(lf_scan, 1)
            dve.wait_ge(lf_scan, H_FX + 1)
            nc.vector.tensor_tensor(d_inc[:, :, :], d_tot[:, :].rearrange("p (h o) -> p h o", o=1)
                                    .to_broadcast([P, H_FX, PAGE]), d_inc[:, :, :], ALU.subtract).then_inc(suf_ready, 1)
            dve.wait_ge(dkn_hi, 1)
            nc.vector.tensor_tensor(d_knl[:, :, :], pT[:, T_FK:T_FK + NJ, SEQ:T], d_knh[:, :, :].bitcast(F32),
                                    ALU.subtract).then_inc(dkn_lo, 1)

            def add_scores(b, g):
                if g < N_GR:
                    dve.wait_ge(qk_done, b * ITEMS + (g + 1) * NJ)
                    src, dst = ps[0:NR, 4 + g % 2, :], d_s[:, g * 512:(g + 1) * 512]
                    bias = d_sfx[:, g * 512:(g + 1) * 512]
                    if g == 0:
                        dve.wait_ge(sfx_landed, b * (16 * DS_) + 16 * DS_)
                        if not (isinstance(b, int) and b == 0):
                            dve.wait_ge(pT_done, b)
                else:
                    dve.wait_ge(new_done, b + 1)
                    src, dst, bias = ps[0:NR, 4, 0:NS], d_s[:, PAST:PAST + NS], d_nb[:, ds(b * NS, NS)]
                nc.vector.scalar_tensor_tensor(dst, src, d_cq[:, ds(b, 1)], bias, ALU.add, ALU.add).then_inc(s1_done, 1)

            def turn(b, with_keys=True, with_values=True):
                if with_values:
                    dve.wait_ge(s2_done, b * N_SC)
                    nc.vector.tensor_reduce(d_small[:, 0:1], d_s[:, :], AX_X, ALU.max).then_inc(dmx_done, 1)
                    dve.wait_ge(dmx_done, b * 2 - 1)
                    nc.vector.tensor_scalar(d_small[:, 1:2], d_small[:, 0:1], -1.0, None, ALU.mult).then_inc(dmx_done, 1)
                if with_keys:
                    dve.wait_ge(qh_done, b * 2 + 2)
                    for p in range(2):
                        half = slice(p * DH, (p + 1) * DH)
                        v = d_q[half, :].rearrange("k (j c) -> k j c", j=NJ)
                        nc.vector.scalar_tensor_tensor(v[:, :, NR + p:NR + p + NR:H_FX],
                                                       pT[half, T_FQ:T_FQ + NJ, ds(b * DS_ + SEQ, DS_)], SCALE,
                                                       v[:, :, p:p + NR:H_FX].bitcast(F32), ALU.mult, ALU.subtract)\
                            .then_inc(ql_done, 1)
                for n in range(ITEMS):
                    if with_keys:
                        dve.wait_ge(kh_done, b * ITEMS + (n + 1))
                        nc.vector.tensor_tensor(d_kl[:, n % NJ, :], ps[:, n % NJ, :], d_kh[:, n % NJ, :].bitcast(F32),
                                                ALU.subtract).then_inc(kl_done, 1)
                    if with_values:
                        if n == 3:
                            dve.wait_ge(dexp_done, b)
                            nc.vector.reciprocal(d_small[:, 3:4], d_small[:, 2:3]).then_inc(dinv_done, 1)
                        if n == V_FIRST - 1:
                            dve.wait_ge(pth_done, b * 2)
                            nc.vector.tensor_tensor(d_pT[:, :, NR:NB2], ps[:, 7, :].rearrange("s (g r) -> s g r", r=NR),
                                                    d_pT[:, :, 0:NR].bitcast(F32), ALU.subtract).then_inc(ptl_done, 1)
                            nc.vector.tensor_tensor(d_pTn[:, NR:NB2], ps[0:NS, 5, 0:NR], d_pTn[:, 0:NR].bitcast(F32),
                                                    ALU.subtract).then_inc(ptl_done, 1)
                    if with_keys and n in SCORES_AT:
                        add_scores(b, SCORES_AT[n])
                if with_keys:
                    add_scores(b, N_GR - 1)
                    add_scores(b, N_GR)
                if with_values:
                    dve.wait_ge(ox_done, b)
                    nc.vector.tensor_tensor(d_o[:, :], ps[0:NR, 6, :], d_ox[:, :], ALU.add).then_inc(o_step, 1)
                    dve.wait_ge(o_step, b * 3 - 2)
                    o3 = d_o[:, :].rearrange("r (h d) -> r h d", d=DH)
                    own = d_hm[:, :].rearrange("r (h o) -> r h o", o=1).to_broadcast([NR, H_FX, DH])
                    nc.vector.scalar_tensor_tensor(o3, o3, d_small[:, 3:4], own, ALU.mult, ALU.mult).then_inc(o_step, 1)
                    dve.wait_ge(o_step, b * 3 - 1)
                    nc.vector.tensor_reduce(d_od[:, ds(b - 1, 1), :].rearrange("r o d -> r (o d)"),
                                            d_o[:, :].rearrange("r (h d) -> r d h", d=DH), AX_X, ALU.add)\
                        .then_inc(o_step, 1)

            turn(0, with_values=False)
            with dve.Fori(1, DB) as b:
                turn(b)
            turn(DB, with_keys=False)
            dve.wait_ge(oT_done, 1)
            for p in range(2):
                for j in range(NJ):
                    src = ps[0:DH, 4, 0:DB * NR].rearrange("d (b t h) -> d b t h", b=DB, h=H_FX)[:, :, :, 2 * j + p]
                    nc.vector.tensor_copy(oF[p * DH:(p + 1) * DH, T_FV + j, SEQ:T].rearrange("d (b t) -> d b t", t=DS_),
                                          src).then_inc(oF_done, 1)
            dve.wait_ge(oF_done, 2 * NJ)
            for i in range(NJ):
                dve.wait_ge(fn_ss, i + 1)
                b0 = 2 * (i % 2)
                m, r, t = fn_m[i % 2], fn_r[i % 2], fn_q[i % 2]
                nc.vector.tensor_scalar(halves(m[:, :]), ps[:, b0:b0 + 2, 0:HALF], 1.0 / DH, EPS, ALU.mult, ALU.add)\
                    .then_inc(fn_v, 1)
                dve.wait_ge(fn_a, 2 * i + 2)
                nc.vector.tensor_tensor(t[:, :], r[:, :], r[:, :], ALU.mult).then_inc(fn_v, 1)
                dve.wait_ge(fn_v, 5 * i + 2)
                nc.vector.scalar_tensor_tensor(t[:, :], t[:, :], -0.5, m[:, :], ALU.mult, ALU.mult).then_inc(fn_v, 1)
                dve.wait_ge(fn_v, 5 * i + 3)
                nc.vector.scalar_tensor_tensor(r[:, :], t[:, :], 1.5, r[:, :], ALU.add, ALU.mult).then_inc(fn_v, 1)
                dve.wait_ge(fn_v, 5 * i + 4)
                o = oF[:, T_FV + i, :]
                nc.vector.scalar_tensor_tensor(o, o, fx_gain[:, i:i + 1], r[:, :], ALU.mult, ALU.mult).then_inc(fn_v, 1)
                dve.wait_ge(fn_hi, i + 1)
                nc.vector.tensor_tensor(o_lo[:, H_HG + i, :], o, o_hi[:, H_HG + i, :].bitcast(F32), ALU.subtract)\
                    .then_inc(fn_lo, 1)

        def mid3_gpsimd(pool):
            pool.wait_ge(h_dve.sem, h_dve.after("out_lo", H_HG - 1))
            pool.indirect_dma_start(out=d_lf[:, :], out_offset=None, in_=io["cache_logf"][0].rearrange("n s h -> n (s h)"),
                                    in_offset=bass.IndirectOffsetOnAxis(ap=page_ids[:, 0:1], axis=0)).then_inc(lf_landed, 16)

            def add_low(b, g):
                n = N_SC * b + g
                pool.wait_ge(s1_done, b * N_SC + (g + 1))
                pool.wait_ge(sx_done, b * N_SC + (g + 1))
                if g < N_GR:
                    s, x = d_s[:, g * 512:(g + 1) * 512], d_x[:, :]
                else:
                    s, x = d_s[:, PAST:PAST + NS], d_x[:, 0:NS]
                nc.gpsimd.tensor_tensor(s, s, x, ALU.add).then_inc(s2_done, 1)

            def turn(b, with_keys=True, with_values=True):
                for n in range(ITEMS):
                    if with_keys and n in SCORES_AT:
                        add_low(b, SCORES_AT[n])
                    if with_values:
                        for m in V_AFTER[n]:
                            pool.wait_ge(vh_done, (b - 1) * PAGES + (m + 1))
                            nc.gpsimd.tensor_tensor(d_vl[:, m % 4, :], d_v[m // GR % 2][:, m % GR, :],
                                                    d_vh[:, m % 4, :].bitcast(F32), ALU.subtract).then_inc(vl_done, 1)
                if with_keys:
                    add_low(b, N_GR - 1)
                    add_low(b, N_GR)

            turn(0, with_values=False)
            with pool.Fori(1, DB) as b:
                turn(b)
            turn(DB, with_keys=False)
            pool.wait_ge(oF_done, 2 * NJ)
            for i in range(NJ):
                if i >= 2:
                    pool.wait_ge(fn_v, 5 * (i - 2) + 5)
                nc.gpsimd.tensor_tensor(fn_q[i % 2][:, :], oF[:, T_FV + i, :], oF[:, T_FV + i, :], ALU.mult)\
                    .then_inc(fn_sq, 1)

        @block.sync
        def _(sp):
            for i in range(TT + 1):
                src = io["x_prompt"][0, i * P:(i + 1) * P, :] if i < TT else io["x_sample"].rearrange("b t d -> (b t) d")
                sp.dma_start(x_nat[0:N_TOK[i], i, :], src).then_inc(x_landed[i], 16)
            for i, g in enumerate(("norm_ffn1", "norm_mix", "norm_ffn2")):
                sp.dma_start(gains[:, i, :], io[g][0].rearrange("(k p) -> p k", p=P),
                             allow_slow_non_contiguous=True).then_inc(gains_landed, 16)
            sp.dma_start(gains[:, 3, :], io["norm_final"].rearrange("(k p) -> p k", p=P),
                         allow_slow_non_contiguous=True).then_inc(gains_landed, 16)
            sp.dma_start(wf[:, :, :], io["w_in_mix"][0].rearrange("(k p) n -> p k n", p=P)[:, :, D_IN - H_FX:D_IN],
                         allow_slow_non_contiguous=True).then_inc(gains_landed, 16)

            for t, name in ((hg_lb, "hgrn_lb"), (hg_gain, "hgrn_out_gain"), (fx_gain, "fox_out_gain")):
                sp.dma_start(t[:, :], io[name][0].rearrange("(h p) -> p h", p=P),
                             allow_slow_non_contiguous=True).then_inc(gains_landed, 16)
            sp.dma_start(page_ids[:, :], io["page_table"].rearrange("b (g o) -> (b g) o", o=1)).then_inc(gains_landed, 16)
            sp.dma_start(page_row[:, :], io["page_table"].rearrange("(o b) g -> o (b g)", o=1)).then_inc(gains_landed, 16)
            sp.dma_start(f_bias[:, :], io["fox_f_bias"][0].rearrange("(h o) -> h o", o=1)).then_inc(gains_landed, 16)

            def slot_free(pair, j, first=False):
                if not first:
                    sp.wait_ge(w_lo_ready, 2 * pair + j - 1)

            def load_gate_up(pair, tile, j, w, first=False):
                slot_free(pair, j, first)
                dst = w_raw[j][:, 0:KD * UC].rearrange("p (k c) -> p k c", c=UC)
                src = w[0].rearrange("(k p) n -> p k n", p=P)
                sp.dma_start(dst[:, :, 0:P], src[:, :, ds(tile * P, P)]).then_inc(w_landed[j], 16)
                sp.dma_start(dst[:, :, P:UC], src[:, :, ds(tile * P + D_FF, P)]).then_inc(w_landed[j], 16)

            def load_columns(pair, unit, j, w, k0, kt):
                slot_free(pair, j)
                dst = w_raw[j][:, 0:kt * UC].rearrange("p (k c) -> p k c", c=UC)
                src = w[0, k0 * P:(k0 + kt) * P, :].rearrange("(k p) n -> p k n", p=P)
                h = kt // 2
                sp.dma_start(dst[:, 0:h, :], src[:, 0:h, ds(unit * UC, UC)]).then_inc(w_landed[j], 16)
                sp.dma_start(dst[:, h:kt, :], src[:, h:kt, ds(unit * UC, UC)]).then_inc(w_landed[j], 16)

            def ffn_loads(p0, w_in, w_out, first):
                tile0 = 0
                for c, pairs in zip(CHUNKS, (IN_A, IN_B)):
                    skip = 1 if first and tile0 == 0 else 0
                    for i in range(skip):
                        for j in range(2):
                            load_gate_up(0, j, j, w_in, first=True)
                    with sp.Fori(skip, pairs) as i:
                        for j in range(2):
                            load_gate_up(i + p0, i * 2 + (tile0 + j), j, w_in)
                    p0 += pairs
                    with sp.Fori(0, KD // 4) as i:
                        for j in range(2):
                            load_columns(i + p0, i * 2 + j, j, w_out, tile0, c)
                    p0 += KD // 4
                    tile0 += c

            ffn_loads(P_FFN[0], io["ffn1_w_in"], io["ffn1_w_out"], True)
            with sp.Fori(0, MIX_PAIRS) as i:
                for j in range(2):
                    load_columns(i + P_MIX_IN, i * 2 + j, j, io["w_in_mix"], 0, KD)
            mid_sync(sp)
            with sp.Fori(0, KD // 4) as i:
                for j in range(2):
                    load_columns(i + P_MIX_OUT, i * 2 + j, j, io["w_out_mix"], 0, KD)
            ffn_loads(P_FFN[1], io["ffn2_w_in"], io["ffn2_w_out"], False)
            for i in range(TT + 1):
                sp.wait_ge(y_copied, 2 * (i + 1))
                dst = y_prompt[0, i * P:(i + 1) * P, :] if i < TT else y_sample.rearrange("b t d -> (b t) d")
                sp.dma_start(dst, y_nat[0:N_TOK[i], i % 2, :]).then_inc(y_stored[i % 2], 16)
            sp.wait_ge(y_stored[0], 16 * ((TT + 2) // 2))
            sp.wait_ge(y_stored[1], 16 * ((TT + 1) // 2))
            mid_stores_waited(sp)

        @block.tensor
        def _(pe):
            pe.wait_ge(const_ready, 2)
            for i in range(TT + 1):
                n = N_TOK[i]
                pe.wait_ge(x_landed[i], 16)
                for q in range(2):
                    b = 2 * (i % 2) + q
                    if i >= 2:
                        pe.wait_ge(xt_copied, 2 * (i - 2) + q + 1)
                    for d in range(4):
                        mm = pe.transpose(ps[:, b, d * P:d * P + n], x_nat[0:n, i, (4 * q + d) * P:(4 * q + d + 1) * P],
                                          ident[0:n, 0:n])
                    mm.then_inc(xt_done, 1)

            def unit(pair, j, kt, x_hi, x_lo, x_wait=None, first=False, second_tile=None):
                pe.wait_ge(w_hi_ready, 2 * pair + j + 1)
                pe.wait_ge(w_lo_ready, 2 * pair + j + 1)
                if not first:
                    pe.wait_ge(drained, 2 * pair + j - 1)
                for t in range(2):
                    if t and second_tile:
                        second_tile()
                    for k in range(kt):
                        if x_wait is not None and t == 0:
                            x_wait(k)
                        w = [s[j][:, k * UC + t * P:k * UC + (t + 1) * P] for s in (w_hi, w_lo)]
                        for wp, xp in ((w[0], x_hi), (w[0], x_lo), (w[1], x_hi)):
                            for s in range(2):
                                mm = pe.matmul(bank(4 * j + 2 * t + s), wp, xp[:, k, s * HALF:(s + 1) * HALF],
                                               start=(k == 0 and wp is w[0] and xp is x_hi),
                                               stop=(k == kt - 1 and wp is w[1]))
                mm.then_inc(mm_done, 1)

            def sum_squares(stage, drained_units=0):
                pe.wait_ge(sumsq_ready, stage)
                if drained_units:
                    pe.wait_ge(drained, drained_units)
                for s in range(2):
                    mm = pe.matmul(SS[:, s, :], ones[:, :], sumsq[:, s * HALF:(s + 1) * HALF], start=True, stop=True)
                mm.then_inc(ss_done, 1)

            def x_in(stage):
                def wait(k):
                    pe.wait_ge(n_ready, KD * stage + k + 1)
                return wait

            def first_pair(p0, stage, x_hi, x_lo):
                unit(p0, 0, KD, x_hi, x_lo, x_in(stage), first=(p0 == 0))
                sum_squares(stage + 1, 2 * p0)
                unit(p0, 1, KD, x_hi, x_lo, first=(p0 == 0), second_tile=lambda: pe.wait_ge(ms_ready, stage + 1))

            def ffn(f, p0, stage):
                done = f * KF
                for c, (kt, pairs) in enumerate(zip(CHUNKS, (IN_A, IN_B))):
                    if c == 0:
                        first_pair(p0, stage, n_hi[f], n_lo[f])
                    with pe.Fori(1 if c == 0 else 0, pairs) as i:
                        for j in range(2):
                            unit(i + p0, j, KD, n_hi[f], n_lo[f])
                    p0 += pairs
                    done += kt

                    def g_wait(k):
                        if k == 0 or k == kt - 1:
                            pe.wait_ge(g_ready, done - 1 if k == 0 else done)
                    with pe.Fori(0, KD // 4) as i:
                        for j in range(2):
                            unit(i + p0, j, kt, g_hi[f], g_lo[f], g_wait)
                    p0 += KD // 4

            ffn(0, P_FFN[0], 0)
            first_pair(P_MIX_IN, 1, n_hi[0], n_lo[0])
            with pe.Fori(1, MIX_PAIRS) as i:
                for j in range(2):
                    unit(i + P_MIX_IN, j, KD, n_hi[0], n_lo[0])
            pe.wait_ge(wf_split, 2)
            pe.wait_ge(drained, 2 * P_MIX_OUT - 1)
            for k in range(KD):
                for n, (wp, xp) in enumerate(((wf_hi, n_hi[0]), (wf_hi, n_lo[0]), (wf_lo, n_hi[0]))):
                    for s in range(2):
                        mm = pe.matmul(ps[0:H_FX, s, 0:HALF], wp[:, k, :], xp[:, k, s * HALF:(s + 1) * HALF],
                                       start=(k == 0 and n == 0), stop=(k == KD - 1 and n == 2))
            mm.then_inc(ff_done, 1)
            mid_tensor(pe)
            with pe.Fori(0, KD // 4) as i:
                for j in range(2):
                    unit(i + P_MIX_OUT, j, KD, o_hi, o_lo)
            ffn(1, P_FFN[1], 2)
            sum_squares(4, 2 * (P_FFN[1] + P_MIX_IN))
            for i in range(TT + 1):
                n = N_TOK[i]
                for q in range(2):
                    if i >= 2:
                        pe.wait_ge(y_copied, 2 * (i - 2) + q + 1)
                    for d in range(4):
                        if i == 0:
                            pe.wait_ge(yt_ready, 4 * q + d + 1)
                        mm = pe.transpose(ps[0:n, 2 * (i % 2) + q, d * P:(d + 1) * P],
                                          yT[:, 4 * q + d, i * P:i * P + n], ident[:, :])
                    mm.then_inc(yt_done, 1)

        @block.scalar
        def _(act):
            def split_hi(pair, j, kt, first=False):
                act.wait_ge(w_landed[j], pair * 32 + 32)
                if not first:
                    act.wait_ge(mm_done, 2 * pair + j - 1)
                nc.scalar.activation(w_hi[j][:, 0:kt * UC], w_raw[j][:, 0:kt * UC], ACT.Copy).then_inc(w_hi_ready, 1)

            def norm_in(stage, x_wait):
                f = 0 if stage < 2 else 1
                for d in range(KD):
                    x_wait(d)
                    nc.scalar.activation(n_hi[f][:, d, :], xT[:, d, :], ACT.Copy,
                                         scale=gains[:, stage, d:d + 1]).then_inc(nhi_ready, 1)

            def root_mean_square(stage):
                act.wait_ge(ms_ready, stage)
                nc.scalar.activation(root[:, :], ms[:, :], ACT.Sqrt).then_inc(root_ready, 1)

            def gate_step(pair, j, q, f, tile, next_kt, stage=None):
                if stage is not None:
                    root_mean_square(stage)
                split_hi(pair + 1, j, next_kt)
                act.wait_ge(a_ready, q + 1)
                nc.scalar.activation(a_silu[:, :, :], a_n[:, :, :], ACT.Silu).then_inc(silu_done, 1)
                act.wait_ge(gated_ready, q + 1)
                nc.scalar.activation(halves(g_hi[f][:, ds(tile, 1), :].rearrange("p o t -> p (o t)")), g_f[:, :, :],
                                     ACT.Copy).then_inc(ghi_ready, 1)

            def ffn(f, p0, stage):
                q0 = f * KF
                for c, (kt, pairs) in enumerate(zip(CHUNKS, (IN_A, IN_B))):
                    peel = 1 if c == 0 else 0
                    if peel:
                        for j in range(2):
                            gate_step(p0, j, q0 + j, f, j, KD, stage + 1 if j == 0 else None)
                    with act.Fori(peel, pairs - 1) as i:
                        for j in range(2):
                            gate_step(i + p0, j, i * 2 + (q0 + j), f, i * 2 + j, KD)
                    for j in range(2):
                        tile = 2 * (pairs - 1) + j
                        gate_step(p0 + pairs - 1, j, q0 + tile, f, tile, kt)
                    p0 += pairs
                    q0 += kt
                    for i in range(KD // 4):
                        for j in range(2):
                            last = i == KD // 4 - 1
                            end = f == 1 and c == 1
                            if not (last and end):
                                split_hi(p0 + i + 1, j, KD if last else kt)
                            else:
                                act.wait_ge(mm_done, 2 * (p0 + i) + j + 1)
                            if c == 1 and f == 0:
                                next_input(stage + 1, 2 * (2 * i + j))
                    p0 += KD // 4

            def next_input(stage, d0):
                f = 0 if stage < 2 else 1
                for d in range(d0, d0 + 2):
                    act.wait_ge(x_ready, KD * (stage - 1) + d + 1)
                    nc.scalar.activation(n_hi[f][:, d, :], xT[:, d, :], ACT.Copy,
                                         scale=gains[:, stage, d:d + 1]).then_inc(nhi_ready, 1)

            for j in range(2):
                split_hi(0, j, KD, first=True)
            act.wait_ge(gains_landed, 16 * N_CONST_LOADS)
            mix_prologue_scalar(act)
            nc.scalar.activation(wf_hi[:, :, :], wf[:, :, :], ACT.Copy).then_inc(wf_split, 1)
            norm_in(0, lambda d: act.wait_ge(xt_copied, 2 * (TT + 1)))
            ffn(0, P_FFN[0], 0)
            root_mean_square(2)
            with act.Fori(0, MIX_PAIRS - 1) as i:
                for j in range(2):
                    split_hi(i + (P_MIX_IN + 1), j, KD)
            mid_scalar(act)
            for j in range(2):
                split_hi(P_MIX_OUT, j, KD)
            for i in range(KD // 4):
                for j in range(2):
                    split_hi(P_MIX_OUT + i + 1, j, KD)
                    next_input(2, 2 * (2 * i + j))
            ffn(1, P_FFN[1], 2)
            root_mean_square(4)
            for i in range(TT + 1):
                for q in range(2):
                    act.wait_ge(yt_done, 2 * i + q + 1)
                    if i >= 2:
                        act.wait_ge(y_stored[i % 2], 16 * (i // 2))
                    nc.scalar.activation(y_nat[0:N_TOK[i], i % 2, q * 512:(q + 1) * 512],
                                         ps[0:N_TOK[i], 2 * (i % 2) + q, :], ACT.Copy).then_inc(y_copied, 1)

        @block.vector
        def _(dve):
            def split_lo(pair, j, kt):
                dve.wait_ge(w_hi_ready, 2 * pair + j + 1)
                nc.vector.tensor_tensor(w_lo[j][:, 0:kt * UC], w_raw[j][:, 0:kt * UC],
                                        w_hi[j][:, 0:kt * UC].bitcast(F32), ALU.subtract).then_inc(w_lo_ready, 1)

            def input_lo(stage, d):
                f = 0 if stage < 2 else 1
                if stage:
                    dve.wait_ge(x_ready, KD * (stage - 1) + d + 1)
                dve.wait_ge(nhi_ready, KD * stage + d + 1)
                nc.vector.scalar_tensor_tensor(n_lo[f][:, d, :], xT[:, d, :], gains[:, stage, d:d + 1],
                                               n_hi[f][:, d, :].bitcast(F32), ALU.mult, ALU.subtract).then_inc(n_ready, 1)

            def mean_squares(stage):
                dve.wait_ge(ss_done, stage)
                nc.vector.tensor_scalar(halves(ms[:, :]), SS, 1.0 / D, EPS, ALU.mult, ALU.add).then_inc(ms_ready, 1)
                dve.wait_ge(root_ready, stage)
                r = rstd[:, :, :].rearrange("p s c -> p (s c)")
                nc.vector.reciprocal(r, root[:, :]).then_inc(rstd_step, 1)
                dve.wait_ge(rstd_step, 4 * stage - 3)
                nc.vector.tensor_tensor(root[:, :], r, r, ALU.mult).then_inc(rstd_step, 1)
                dve.wait_ge(rstd_step, 4 * stage - 2)
                nc.vector.scalar_tensor_tensor(root[:, :], root[:, :], -0.5, ms[:, :], ALU.mult, ALU.mult)\
                    .then_inc(rstd_step, 1)
                dve.wait_ge(rstd_step, 4 * stage - 1)
                nc.vector.scalar_tensor_tensor(r, root[:, :], 1.5, r, ALU.add, ALU.mult).then_inc(rstd_step, 1)
                dve.wait_ge(rstd_step, 4 * stage)

            def gate_step(pair, j, q, f, tile, next_kt, stage=None):
                dve.wait_ge(mm_done, 2 * pair + j + 1)
                if stage is not None:
                    mean_squares(stage)
                nc.vector.tensor_tensor(a_n[:, :, :], unit_psum(j, 0), rstd[:, :, :], ALU.mult).then_inc(a_ready, 1)
                nc.vector.tensor_tensor(b_n[:, :, :], unit_psum(j, 1), rstd[:, :, :], ALU.mult).then_inc(drained, 1)
                split_lo(pair + 1, j, next_kt)
                dve.wait_ge(silu_done, q + 1)
                dve.wait_ge(drained, 2 * pair + j + 1)
                nc.vector.tensor_tensor(g_f[:, :, :], a_silu[:, :, :], b_n[:, :, :], ALU.mult).then_inc(gated_ready, 1)
                dve.wait_ge(ghi_ready, q + 1)
                hi = halves(g_hi[f][:, ds(tile, 1), :].rearrange("p o t -> p (o t)"))
                lo = halves(g_lo[f][:, ds(tile, 1), :].rearrange("p o t -> p (o t)"))
                nc.vector.tensor_tensor(lo, g_f[:, :, :], hi.bitcast(F32), ALU.subtract).then_inc(g_ready, 1)

            def add_out(pair, j, i, weight, last, x_tiles=0):
                dve.wait_ge(mm_done, 2 * pair + j + 1)
                for t in range(2):
                    x = halves(xT[:, 4 * i + 2 * j + t, :])
                    op = nc.vector.scalar_tensor_tensor(x, unit_psum(j, t), weight, x, ALU.mult, ALU.add)
                    if last:
                        op.then_inc(x_ready, 1)
                if last:
                    dve.wait_ge(x_ready, x_tiles + 2)
                    dve.sem_inc(drained, 1)
                else:
                    op.then_inc(drained, 1)

            def ffn(f, p0, stage):
                q0 = f * KF
                for c, (kt, pairs) in enumerate(zip(CHUNKS, (IN_A, IN_B))):
                    peel = 1 if c == 0 else 0
                    if peel:
                        gate_step(p0, 0, q0, f, 0, KD, stage + 1)
                        gate_step(p0, 1, q0 + 1, f, 1, KD)
                    with dve.Fori(peel, pairs - 1) as i:
                        for j in range(2):
                            gate_step(i + p0, j, i * 2 + (q0 + j), f, i * 2 + j, KD)
                    for j in range(2):
                        tile = 2 * (pairs - 1) + j
                        gate_step(p0 + pairs - 1, j, q0 + tile, f, tile, kt)
                    p0 += pairs
                    q0 += kt
                    for i in range(KD // 4):
                        for j in range(2):
                            last = i == KD // 4 - 1
                            add_out(p0 + i, j, i, 0.5, c == 1, KD * stage + 4 * i + 2 * j)
                            if not (last and f == 1 and c == 1):
                                split_lo(p0 + i + 1, j, KD if last else kt)
                            if c == 1 and f == 0:
                                for t in range(2):
                                    input_lo(stage + 1, 4 * i + 2 * j + t)
                    p0 += KD // 4

            mix_prologue(dve)
            for j in range(2):
                split_lo(0, j, KD)
            dve.wait_ge(wf_split, 1)
            nc.vector.tensor_tensor(wf_lo[:, :, :], wf[:, :, :], wf_hi[:, :, :].bitcast(F32),
                                    ALU.subtract).then_inc(wf_split, 1)
            for i in range(TT + 1):
                for q in range(2):
                    dve.wait_ge(xt_done, 2 * i + q + 1)
                    src = ps[:, 2 * (i % 2) + q, :].rearrange("p (d c) -> p d c", c=P)[:, :, 0:N_TOK[i]]
                    nc.vector.tensor_copy(xT[:, 4 * q:4 * q + 4, i * P:i * P + N_TOK[i]], src).then_inc(xt_copied, 1)
            dve.wait_ge(xt_copied, 2 * (TT + 1))
            for d in range(KD):
                input_lo(0, d)
            ffn(0, P_FFN[0], 0)

            def project_out(pair, j, tile):
                dve.wait_ge(mm_done, 2 * pair + j + 1)
                for t in range(2):
                    out = pT[:, ds(tile + t, 1), :].rearrange("p o t -> p (o t)")
                    op = nc.vector.tensor_tensor(halves(out), unit_psum(j, t), rstd[:, :, :], ALU.mult)
                op.then_inc(drained, 1)

            for j in range(2):
                if j == 0:
                    dve.wait_ge(mm_done, 2 * P_MIX_IN + 1)
                    mean_squares(2)
                project_out(P_MIX_IN, j, 2 * j)
                split_lo(P_MIX_IN + 1, j, KD)
            with dve.Fori(1, MIX_PAIRS - 1) as i:
                for j in range(2):
                    project_out(i + P_MIX_IN, j, i * 4 + 2 * j)
                    split_lo(i + (P_MIX_IN + 1), j, KD)
            for j in range(2):
                project_out(P_MIX_OUT - 1, j, MIX_TILES - 4 + 2 * j)
            dve.wait_ge(ff_done, 1)
            nc.vector.tensor_tensor(halves(ffT[:, :]), ps[0:H_FX, 0:2, 0:HALF], rstd[0:H_FX, :, :],
                                    ALU.mult).then_inc(ff_ready, 1)
            mid_vector(dve)
            for j in range(2):
                split_lo(P_MIX_OUT, j, KD)
            for i in range(KD // 4):
                for j in range(2):
                    add_out(P_MIX_OUT + i, j, i, 1.0, True, KD + 4 * i + 2 * j)
                    split_lo(P_MIX_OUT + i + 1, j, KD)
                    for t in range(2):
                        input_lo(2, 4 * i + 2 * j + t)
            ffn(1, P_FFN[1], 2)
            mean_squares(4)
            for d in range(KD):
                nc.vector.scalar_tensor_tensor(halves(yT[:, d, :]), halves(xT[:, d, :]), gains[:, 3, d:d + 1],
                                               rstd[:, :, :], ALU.mult, ALU.mult).then_inc(yt_ready, 1)

        @block.gpsimd
        def _(pool):
            nc.gpsimd.memset(ones[:, :], 1.0).then_inc(const_ready, 1)
            pool.wait_ge(const_ready, 1)
            nc.gpsimd.affine_select(ident[:, :], ones[:, :], pattern=[[-1, P]], compare_op=ALU.is_equal, fill=0.0,
                                    base=0, channel_multiplier=1).then_inc(const_ready, 1)

            make_mix_consts(pool)

            def squares(stage, x_wait):
                for d in range(KD):
                    x_wait(d)
                    n = stage * KD + d
                    if d == 0:
                        if stage:
                            pool.wait_ge(ss_done, stage)
                        nc.gpsimd.tensor_tensor(sumsq[:, :], xT[:, d, :], xT[:, d, :], ALU.mult).then_inc(sq_added, 1)
                        continue
                    pool.wait_ge(sq_added, n)
                    nc.gpsimd.tensor_tensor(sq[:, :], xT[:, d, :], xT[:, d, :], ALU.mult).then_inc(sq_done, 1)
                    pool.wait_ge(sq_done, n - stage)
                    add = nc.gpsimd.tensor_tensor(sumsq[:, :], sumsq[:, :], sq[:, :], ALU.add)
                    add.then_inc(sq_added, 1)
                pool.wait_ge(sq_added, (stage + 1) * KD)
                pool.sem_inc(sumsq_ready, 1)

            squares(0, lambda d: pool.wait_ge(xt_copied, 2 * (TT + 1)))
            squares(1, lambda d: pool.wait_ge(x_ready, d + 1))
            mid_gpsimd(pool)
            squares(2, lambda d: pool.wait_ge(x_ready, KD + d + 1))
            squares(3, lambda d: pool.wait_ge(x_ready, 2 * KD + d + 1))


_INS = ["x_prompt", "x_sample", "cache_k", "cache_v", "cache_logf", "state_hgrn", "page_table", "norm_ffn1",
        "ffn1_w_in", "ffn1_w_out", "norm_mix", "w_in_mix", "hgrn_lb", "fox_f_bias", "hgrn_out_gain", "fox_out_gain",
        "w_out_mix", "norm_ffn2", "ffn2_w_in", "ffn2_w_out", "norm_final"]
_OUTS = [(1, SEQ, D), (DB, DS_, D), (1, 1, SEQ, H_FX, DH), (1, 1, SEQ, H_FX, DH), (1, 1, SEQ, H_FX),
         (1, 1, H_HG, P, P), (1, DB, DS_, H_FX, DH), (1, DB, DS_, H_FX, DH), (1, DB, DS_, H_FX), (1, DB, H_HG, P, P)]


def kernel(**inputs):
    import concourse.bacc as bacc
    from concourse.bass_utils import run_bass_kernel_spmd

    nc = bacc.Bacc("TRN2", target_bir_lowering=False, num_devices=1)
    arrays, io = {}, {}
    for name in _INS:
        a = np.ascontiguousarray(inputs[name])
        arrays[f"in_{name}"] = a
        io[name] = nc.dram_tensor(f"in_{name}", a.shape, mybir.dt.from_np(a.dtype), kind="ExternalInput").ap()
    io["outs"] = [nc.dram_tensor(f"out_{i}", s, F32, kind="ExternalOutput").ap() for i, s in enumerate(_OUTS)]
    build(nc, io)
    r = run_bass_kernel_spmd(nc, [arrays], core_ids=[0])
    return tuple(r.results[0][f"out_{i}"] for i in range(len(_OUTS)))
```

```python
from contextlib import ExitStack

import numpy as np

import concourse.bass as bass
from concourse import mybir

F32 = mybir.dt.float32
F32R = mybir.dt.float32r
I32 = mybir.dt.int32
U8 = mybir.dt.uint8
ACT = mybir.ActivationFunctionType
ALU = mybir.AluOpType
AX_X = mybir.AxisListType.X
ds = bass.ds

P = 128
EPS = 1e-6
TINY = 1e-30
NEG = -1e30

D = 1024
SEQ = 512
DB, DS_ = 8, 4
NS = DB * DS_
T = SEQ + NS
HALF = T // 2
TT = SEQ // P
D_FF = 2816
KD = D // P
KF = D_FF // P
CHUNKS = (12, 10)
H_HG, H_FX, DH = 4, 8, 64
D_HG = D_FX = 512
D_IN = 4 * D_HG + 3 * D_FX + H_FX
MIX_TILES = (4 * D_HG + 3 * D_FX) // P
PAGES, PAGE, N_POOL = 16, 128, 160
PAST = PAGES * PAGE
UC = 2 * P
SLOT = max(CHUNKS) * UC
SCALE = DH ** -0.5

assert sum(CHUNKS) == KF and all(c % 2 == 0 for c in CHUNKS) and SEQ % P == 0


def build(nc, io):
    y_prompt, y_sample, k_prompt, v_prompt, lf_prompt, s_prompt, k_sample, v_sample, lf_sample, s_sample = io["outs"]
    ctx = ExitStack()
    with ctx:
        ROW = 4 * T
        X0 = (nc.sbuf_base + 63) // 64 * 64
        Z0 = X0 + KD * ROW
        T0 = Z0 + 2 * KD * ROW + 2 * CHUNKS[0] * ROW
        RING = T0 + 4 * ROW
        C0 = RING + 6 * 4 * SLOT
        END = nc.sbuf_usable_end

        def at(name, shape, dt, offset):
            size = int(np.prod(shape[1:])) * (1 if dt == U8 else 4)
            assert offset + size <= END, (name, offset + size, END)
            return nc.alloc_sbuf_tensor_at(name, shape, dt, offset=offset)

        top = [C0]

        def const(name, shape, dt=F32):
            t = at(name, shape, dt, top[0])
            top[0] += (int(np.prod(shape[1:])) * (1 if dt == U8 else 4) + 31) // 32 * 32
            return t

        xT = at("xT", [P, KD, T], F32, X0)
        n_hi = [at("n1_hi", [P, KD, T], F32R, Z0), at("n2_hi", [P, KD, T], F32R, Z0 + 2 * CHUNKS[0] * ROW)]
        n_lo = [at("n1_lo", [P, KD, T], F32R, Z0 + KD * ROW),
                at("n2_lo", [P, KD, T], F32R, Z0 + (2 * CHUNKS[0] + KD) * ROW)]
        g_hi = [at("g1_hi", [P, CHUNKS[0], T], F32R, Z0 + 2 * KD * ROW), at("g2_hi", [P, CHUNKS[0], T], F32R, Z0)]
        g_lo = [at("g1_lo", [P, CHUNKS[0], T], F32R, Z0 + (2 * KD + CHUNKS[0]) * ROW),
                at("g2_lo", [P, CHUNKS[0], T], F32R, Z0 + CHUNKS[0] * ROW)]
        pT = at("mix_projT", [P, MIX_TILES, T], F32, Z0 + 2 * KD * ROW)
        o_hi = at("mix_out_hi", [P, KD, T], F32R, Z0)
        o_lo = at("mix_out_lo", [P, KD, T], F32R, Z0 + KD * ROW)
        x_nat = at("x_nat", [P, TT + 1, D], F32, Z0 + 2 * KD * ROW)
        yT = at("yT", [P, KD, T], F32, Z0 + 2 * KD * ROW)
        y_nat = at("y_nat", [P, 2, D], F32, RING)
        a_n = at("ffn_a", [P, 2, HALF], F32, T0)
        b_n = at("ffn_b", [P, 2, HALF], F32, T0 + ROW)
        a_silu = at("ffn_a_silu", [P, 2, HALF], F32, T0 + 2 * ROW)
        g_f = at("ffn_gated", [P, 2, HALF], F32, T0 + 3 * ROW)
        w_raw = [at(f"w_raw{s}", [P, SLOT], F32, RING + s * 4 * SLOT) for s in range(2)]
        w_hi = [at(f"w_hi{s}", [P, SLOT], F32R, RING + (2 + s) * 4 * SLOT) for s in range(2)]
        w_lo = [at(f"w_lo{s}", [P, SLOT], F32R, RING + (4 + s) * 4 * SLOT) for s in range(2)]
        rstd = const("rstd", [P, 2, HALF])
        SUMSQ_AT = top[0]
        sumsq = const("sumsq", [P, T])
        SQ_AT = top[0]
        sq = const("sq", [P, T])
        ms = const("mean_sq", [P, T])
        root = sq
        ident = const("ident", [P, P])
        ones = const("ones", [P, P])
        gains = const("gains", [P, 4, KD])
        wf = const("w_forget", [P, KD, H_FX])
        wf_hi = const("w_forget_hi", [P, KD, H_FX], F32R)
        wf_lo = const("w_forget_lo", [P, KD, H_FX], F32R)
        ffT = const("forgetT", [H_FX, T])

        ps = ctx.enter_context(nc.psum_tensor("ps", [P, 8, 512], F32))

        def sem(name):
            return ctx.enter_context(nc.semaphore(name))

        const_ready = sem("const_ready")
        gains_landed = sem("gains_landed")
        x_landed = [sem(f"x_landed{i}") for i in range(TT + 1)]
        w_landed = [sem("w_landed0"), sem("w_landed1")]
        w_hi_ready = sem("w_hi_ready")
        w_lo_ready = sem("w_lo_ready")
        mm_done = sem("mm_done")
        drained = sem("drained")
        xt_done = sem("xt_done")
        xt_copied = sem("xt_copied")
        x_ready = sem("x_ready")
        nhi_ready = sem("nhi_ready")
        n_ready = sem("n_ready")
        a_ready = sem("a_ready")
        silu_done = sem("silu_done")
        gated_ready = sem("gated_ready")
        ghi_ready = sem("ghi_ready")
        g_ready = sem("g_ready")
        sq_done = sem("sq_done")
        sq_added = sem("sq_added")
        sumsq_ready = sem("sumsq_ready")
        ss_done = sem("ss_done")
        ms_ready = sem("ms_ready")
        root_ready = sem("root_ready")
        rstd_step = sem("rstd_step")
        wf_split = sem("wf_split")
        ff_done = sem("ff_done")
        ff_ready = sem("ff_ready")
        yt_ready = sem("yt_ready")
        yt_done = sem("yt_done")
        y_copied = sem("y_copied")
        y_stored = [sem("y_stored0"), sem("y_stored1")]

        P_FFN = [0, 24]
        IN_A, OUT_A = CHUNKS[0] // 2, KD // 4
        IN_B, OUT_B = CHUNKS[1] // 2, KD // 4
        P_MIX_IN = IN_A + OUT_A + IN_B + OUT_B
        MIX_PAIRS = MIX_TILES // 4
        P_MIX_OUT = P_MIX_IN + MIX_PAIRS
        P_FFN[1] = P_MIX_OUT + KD // 4
        N_CONST_LOADS = 11
        N_TOK = [P] * TT + [NS]

        def halves(t):
            return t.rearrange("p (s c) -> p s c", s=2)

        def bank(b, n=HALF):
            return ps[:, b, 0:n]

        def unit_psum(j, t):
            return ps[:, 4 * j + 2 * t:4 * j + 2 * t + 2, 0:HALF]

        SS = unit_psum(1, 1)

        block = ctx.enter_context(nc.Block())

        T_Q, T_F, T_I, T_G, T_FQ, T_FK, T_FV = (4 * n for n in range(7))
        LEVELS = (6, 5, 4, 3, 2, 1, 0)
        DIAG = len(LEVELS)

        neg_mask = const("neg_mask", [P, P])
        hg_reset = const("hg_reset", [P, T])
        fx_reset = const("fx_reset", [H_FX, T])
        hg_mask = const("hg_mask", [P, DIAG + 1, SEQ], U8)
        f_bias = const("f_bias", [H_FX, 1])
        hg_lb = const("hg_lb", [P, H_HG])
        hg_gain = const("hg_gain", [P, H_HG])
        fx_gain = const("fx_gain", [P, H_HG])
        lb = const("lb", [P, H_HG])
        one_lb = const("one_minus_lb", [P, H_HG])
        two_heads = const("two_heads", [P, P])
        page_ids = const("page_ids", [P, 1], I32)
        page_row = const("page_row", [1, P], I32)

        ring_top = [RING]

        def buf(name, shape, dt=F32):
            t = at(name, shape, dt, ring_top[0])
            ring_top[0] += (int(np.prod(shape[1:])) * (1 if dt == U8 else 4) + 31) // 32 * 32
            assert ring_top[0] <= C0, (name, ring_top[0] - C0)
            return t

        v_nat = buf("v_nat", [P, TT + 1, D_FX])
        k_st = buf("k_staged", [P, 2, D_FX])
        fx_z = buf("forget_z", [H_FX, T])
        fx_t = buf("forget_t", [H_FX, T])
        fx_lf = buf("forget_log", [H_FX, T])
        fx_cum = buf("forget_cum", [H_FX, T])
        fx_ncum = buf("forget_neg_cum", [H_FX, T])
        lf_nat = buf("lf_nat", [P, TT + 1, H_FX])
        q_aug = [buf(f"q_aug{j}", [97, SEQ]) for j in range(2)]
        k_aug = [buf(f"k_aug{j}", [97, SEQ]) for j in range(2)]
        v_st = [buf(f"v_head{j}", [P, TT, DH]) for j in range(2)]
        prob = [buf(f"prob{j}", [P, TT, SEQ]) for j in range(2)]
        probT = buf("probT", [P, TT, SEQ])
        fx_max = buf("fx_max", [P, 2, TT])
        fx_nmax = buf("fx_neg_max", [P, 2, TT])
        fx_sum = buf("fx_sum", [P, 2, TT])
        fx_inv = buf("fx_inv", [P, 2, TT])
        oF = pT
        cum_d = nc.dram_tensor("cum_scratch", (2, H_FX, SEQ), F32, kind="Internal").ap()

        gates_done = sem("gates_done")
        const_done = sem("const_done")
        mix_consts = sem("mix_consts")
        kt_done, vt_done = sem("kt_done"), sem("vt_done")
        k_copied, v_copied = sem("k_copied"), sem("v_copied")
        k_stored = [sem("k_stored0"), sem("k_stored1")]
        v_stored = sem("v_stored")
        fx_step = sem("fx_step")
        lft_done, lf_copied, lf_stored = sem("lft_done"), sem("lf_copied"), sem("lf_stored")
        cum_stored = sem("cum_stored")
        aug_const = sem("aug_const")
        q_staged, k_staged, v_staged = sem("q_staged"), sem("k_staged_s"), sem("v_staged")
        cum_landed = [sem("cum_landed0"), sem("cum_landed1")]
        fs_done = sem("fs_done")
        fs_masked = sem("fs_masked")
        fs_max = sem("fs_max")
        fs_exp = sem("fs_exp")
        fs_inv = sem("fs_inv")
        fs_prob = sem("fs_prob")
        fpt_done = sem("fpt_done")
        fpt_copied = sem("fpt_copied")
        fo_done, fo_copied = sem("fo_done"), sem("fo_copied")

        def mix_tile(base, i, parts=slice(0, P), cols=slice(0, T)):
            return pT[parts, ds(i + base, 1), cols].rearrange("p o t -> p (o t)")

        def nat(dst_prompt, dst_sample, i):
            if i < TT:
                return dst_prompt[0, 0, i * P:(i + 1) * P].rearrange("t h d -> t (h d)")
            return dst_sample[0].rearrange("b t h d -> (b t) (h d)")

        def mid_sync(sp):
            for i in range(TT + 1):
                n = N_TOK[i]
                sp.wait_ge(k_copied, i + 1)
                sp.dma_start(nat(k_prompt, k_sample, i), k_st[0:n, i % 2, :]).then_inc(k_stored[i % 2], 16)
                sp.wait_ge(v_copied, i + 1)
                sp.dma_start(nat(v_prompt, v_sample, i), v_nat[0:n, i, :]).then_inc(v_stored, 16)
            sp.wait_ge(fx_step, 8)
            sp.dma_start(cum_d[0], fx_cum[:, 0:SEQ]).then_inc(cum_stored, 16)
            sp.dma_start(cum_d[1], fx_ncum[:, 0:SEQ]).then_inc(cum_stored, 16)
            sp.wait_ge(lf_copied, 1)
            sp.dma_start(lf_prompt[0, 0].rearrange("(i p) h -> p i h", p=P), lf_nat[:, 0:TT, :],
                         allow_slow_non_contiguous=True).then_inc(lf_stored, 16)
            sp.dma_start(lf_sample[0].rearrange("b t h -> (b t) h"), lf_nat[0:NS, TT, :]).then_inc(lf_stored, 16)
            sp.wait_ge(cum_stored, 32)
            sp.wait_ge(aug_const, 8)

            def cum_rows(h, j):
                sp.dma_start(q_aug[j][64:65, :], cum_d[0, ds(h, 1), :]).then_inc(cum_landed[j], 16)
                sp.dma_start(k_aug[j][96:97, :], cum_d[1, ds(h, 1), :]).then_inc(cum_landed[j], 16)

            for j in range(2):
                cum_rows(j, j)
            with sp.Fori(1, H_FX // 2) as i:
                for j in range(2):
                    sp.wait_ge(fs_done, i * (2 * TT) + (j - 1) * TT)
                    cum_rows(i * 2 + j, j)
            mid2_sync(sp)

        def mid_stores_waited(sp):
            sp.wait_ge(k_stored[0], 16 * 3)
            sp.wait_ge(k_stored[1], 16 * 2)
            sp.wait_ge(v_stored, 16 * (TT + 1))
            sp.wait_ge(lf_stored, 32)
            mid2_stores_waited(sp)

        def mid_tensor(pe):
            for i in range(TT + 1):
                n = N_TOK[i]
                for src, b, copied, done in ((T_FK, 2 + i % 2, k_copied, kt_done), (T_FV, 4 + i % 2, v_copied, vt_done)):
                    if i >= 2:
                        pe.wait_ge(copied, i - 1)
                    else:
                        pe.wait_ge(drained, 2 * P_MIX_OUT)
                    for q in range(4):
                        mm = pe.transpose(ps[0:n, b, q * P:(q + 1) * P], pT[:, src + q, i * P:i * P + n], ident[:, :])
                    mm.then_inc(done, 1)
            pe.wait_ge(fx_step, 6)
            for i in range(TT + 1):
                n = N_TOK[i]
                mm = pe.transpose(ps[0:n, 6, i * H_FX:(i + 1) * H_FX], fx_lf[:, i * P:i * P + n], ident[0:H_FX, 0:H_FX])
            mm.then_inc(lft_done, 1)

            def scores(h, j, pair, first=False):
                pe.wait_ge(q_staged, h + 1)
                pe.wait_ge(k_staged, h + 1)
                pe.wait_ge(cum_landed[j], pair * 32 + 32)
                for t in range(TT):
                    if not first:
                        pe.wait_ge(fs_exp, h * TT + (t + 1 - TT))
                    pe.matmul(ps[:, t, 0:(t + 1) * P], q_aug[j][:, t * P:(t + 1) * P], k_aug[j][:, 0:(t + 1) * P],
                              start=True, stop=True).then_inc(fs_done, 1)

            def attend(h, j, first=False):
                pe.wait_ge(fs_prob, h * TT + TT)
                pe.wait_ge(v_staged, h + 1)
                for s in range(TT):
                    b = 4 + s % 2
                    if first and s < 2:
                        pe.wait_ge(v_copied, TT + 1)
                    else:
                        pe.wait_ge(fpt_copied, h * TT + (s - 1))
                    for t in range(s, TT):
                        mm = pe.transpose(ps[:, b, (t - s) * P:(t - s + 1) * P], prob[j][:, t, s * P:(s + 1) * P],
                                          ident[:, :])
                    mm.then_inc(fpt_done, 1)
                if first:
                    pe.wait_ge(lf_copied, 1)
                else:
                    pe.wait_ge(fo_copied, h)
                for s in range(TT):
                    pe.wait_ge(fpt_copied, h * TT + (s + 1))
                    mm = pe.matmul(ps[0:DH, 6, s * P:SEQ], v_st[j][:, s, :], probT[:, s, 0:SEQ - s * P],
                                   start=(s == 0), stop=(s == TT - 1))
                mm.then_inc(fo_done, 1)

            pe.wait_ge(k_copied, TT + 1)
            pe.wait_ge(ff_ready, 1)
            scores(0, 0, 0, first=True)
            scores(1, 1, 0)
            attend(0, 0, first=True)
            with pe.Fori(1, H_FX // 2) as i:
                scores(i * 2, 0, i)
                attend(i * 2 - 1, 1)
                scores(i * 2 + 1, 1, i)
                attend(i * 2, 0)
            attend(H_FX - 1, 1)
            new_rows_tensor(pe)
            mid2_tensor(pe)

        def mid_scalar(act):
            for i in range(TT + 1):
                n = N_TOK[i]
                act.wait_ge(kt_done, i + 1)
                if i >= 2:
                    act.wait_ge(k_stored[i % 2], 16 * (i // 2))
                nc.scalar.activation(k_st[0:n, i % 2, :], ps[0:n, 2 + i % 2, :], ACT.Copy).then_inc(k_copied, 1)
                if i == 1:
                    act.wait_ge(fx_step, 3)
                    nc.scalar.activation(fx_t[:, :], fx_t[:, :], ACT.Exp).then_inc(fx_step, 1)
                    act.wait_ge(fx_step, 4)
                    nc.scalar.activation(fx_t[:, :], fx_t[:, :], ACT.Ln, bias=1.0).then_inc(fx_step, 1)

            act.wait_ge(aug_const, 8)
            act.preload_act_table_set("natural_log_exp_and_others")

            def stage_q(j, i):
                nc.scalar.activation(q_aug[j][0:DH, :], mix_tile(T_FQ, i, slice(j * DH, (j + 1) * DH), slice(0, SEQ)),
                                     ACT.Copy, scale=SCALE).then_inc(q_staged, 1)

            def exps(h, j, alone=False):
                for t in range(TT):
                    if not alone:
                        copy_probT(h - 1, t)
                    act.wait_ge(fs_max, h * TT + (t + 1))
                    nc.scalar.activation(prob[j][:, t, 0:(t + 1) * P], ps[:, t, 0:(t + 1) * P], ACT.Exp,
                                         bias=fx_nmax[:, j, t:t + 1], accum_out=fx_sum[:, j, t:t + 1]).then_inc(fs_exp, 1)

            def copy_probT(h, s):
                act.wait_ge(fpt_done, h * TT + (s + 1))
                nc.scalar.activation(probT[:, s, 0:SEQ - s * P], ps[:, 4 + s % 2, 0:SEQ - s * P],
                                     ACT.Copy).then_inc(fpt_copied, 1)

            for j in range(2):
                stage_q(j, 0)
            exps(0, 0, alone=True)
            gates_scalar(act, 0)
            exps(1, 1)
            with act.Fori(1, H_FX // 2) as i:
                for j in range(2):
                    act.wait_ge(fs_done, i * (2 * TT) + (j - 1) * TT)
                    stage_q(j, i)
                for j in range(2):
                    act.wait_ge(fpt_done, i * (2 * TT) + (j - 1) * TT)
                    exps(i * 2 + j, j)
                    if j == 0:
                        gates_scalar(act, i)
            for s in range(TT):
                copy_probT(H_FX - 1, s)
            new_rows_scalar(act)
            mid2_scalar(act)

        def mid_vector(dve):
            dve.wait_ge(ff_ready, 1)
            dve.wait_ge(gains_landed, 16 * N_CONST_LOADS)
            nc.vector.tensor_scalar(fx_z[:, :], ffT[:, :], f_bias[:, 0:1], None, ALU.add).then_inc(fx_step, 1)
            dve.wait_ge(fx_step, 1)
            nc.vector.tensor_scalar(fx_t[:, :], fx_z[:, :], -1.0, None, ALU.mult).then_inc(fx_step, 1)
            dve.wait_ge(fx_step, 2)
            nc.vector.tensor_tensor(fx_t[:, :], fx_t[:, :], fx_z[:, :], ALU.min).then_inc(fx_step, 1)
            for j in range(2):
                nc.vector.memset(q_aug[j][:, :], 0.0).then_inc(aug_const, 1)
                nc.vector.memset(k_aug[j][:, :], 0.0).then_inc(aug_const, 1)
            dve.wait_ge(aug_const, 4)
            for j in range(2):
                nc.vector.memset(q_aug[j][96:97, :], 1.0).then_inc(aug_const, 1)
                nc.vector.memset(k_aug[j][64:65, :], 1.0).then_inc(aug_const, 1)
            for i in range(TT + 1):
                dve.wait_ge(vt_done, i + 1)
                nc.vector.tensor_copy(v_nat[0:N_TOK[i], i, :], ps[0:N_TOK[i], 4 + i % 2, :]).then_inc(v_copied, 1)
            dve.wait_ge(fx_step, 5)
            nc.vector.scalar_tensor_tensor(fx_lf[:, :], fx_z[:, :], 0.0, fx_t[:, :], ALU.min,
                                           ALU.subtract).then_inc(fx_step, 1)
            dve.wait_ge(fx_step, 6)
            dve.wait_ge(mix_consts, 1)
            nc.vector.tensor_tensor_scan(fx_cum[:, :], fx_reset[:, :], fx_lf[:, :], 0.0, ALU.mult,
                                         ALU.add).then_inc(fx_step, 1)
            dve.wait_ge(fx_step, 7)
            nc.vector.tensor_scalar(fx_ncum[:, :], fx_cum[:, :], -1.0, None, ALU.mult).then_inc(fx_step, 1)
            dve.wait_ge(lft_done, 1)
            nc.vector.tensor_copy(lf_nat[:, 0:TT, :], ps[:, 6, 0:TT * H_FX].rearrange("p (i h) -> p i h", h=H_FX))
            nc.vector.tensor_copy(lf_nat[0:NS, TT, :], ps[0:NS, 6, TT * H_FX:(TT + 1) * H_FX]).then_inc(lf_copied, 1)
            dve.wait_ge(lf_copied, 1)

            def stage_k(j, i):
                nc.vector.tensor_copy(k_aug[j][0:DH, :], mix_tile(T_FK, i, slice(j * DH, (j + 1) * DH), slice(0, SEQ)))\
                    .then_inc(k_staged, 1)

            def maxima(h, j):
                for t in range(TT):
                    dve.wait_ge(fs_done, h * TT + (t + 1))
                    tile = ps[:, t, t * P:(t + 1) * P]
                    nc.vector.tensor_tensor(tile, tile, neg_mask[:, :], ALU.add).then_inc(fs_masked, 1)
                    dve.wait_ge(fs_masked, h * (2 * TT) + (2 * t + 1))
                    nc.vector.tensor_reduce(fx_max[:, j, t:t + 1], ps[:, t, 0:(t + 1) * P], AX_X, ALU.max)\
                        .then_inc(fs_masked, 1)
                    dve.wait_ge(fs_masked, h * (2 * TT) + (2 * t + 2))
                    nc.vector.tensor_scalar(fx_nmax[:, j, t:t + 1], fx_max[:, j, t:t + 1], -1.0, None,
                                            ALU.mult).then_inc(fs_max, 1)

            def normalise(h, j):
                for t in range(TT):
                    dve.wait_ge(fs_exp, h * TT + (t + 1))
                    nc.vector.reciprocal(fx_inv[:, j, t:t + 1], fx_sum[:, j, t:t + 1]).then_inc(fs_inv, 1)
                    dve.wait_ge(fs_inv, h * TT + (t + 1))
                    row = prob[j][:, t, 0:(t + 1) * P]
                    nc.vector.tensor_scalar(row, row, fx_inv[:, j, t:t + 1], None, ALU.mult).then_inc(fs_prob, 1)

            def copy_out(h, j, i):
                dve.wait_ge(fo_done, h + 1)
                nc.vector.tensor_copy(mix_tile(T_FV, i, slice(j * DH, (j + 1) * DH), slice(0, SEQ)),
                                      ps[0:DH, 6, :]).then_inc(fo_copied, 1)

            dve.wait_ge(aug_const, 8)
            for j in range(2):
                stage_k(j, 0)
            gates_vector(dve, 0, "f")
            maxima(0, 0)
            normalise(0, 0)
            maxima(1, 1)
            normalise(1, 1)
            gates_vector(dve, 0, "cum")
            copy_out(0, 0, 0)
            with dve.Fori(1, H_FX // 2) as i:
                for j in range(2):
                    dve.wait_ge(fs_done, i * (2 * TT) + (j - 1) * TT)
                    stage_k(j, i)
                gates_vector(dve, i, "f")
                for j in range(2):
                    maxima(i * 2 + j, j)
                    normalise(i * 2 + j, j)
                    copy_out(i * 2 + (j - 1), 1 - j, i - (1 - j))
                gates_vector(dve, i, "cum")
            copy_out(H_FX - 1, 1, H_FX // 2 - 1)
            new_rows_vector(dve)
            mid2_vector(dve)

        def mid_gpsimd(pool):
            def stage_v(h, j):
                src = v_nat[:, 0:TT, ds(h * DH, DH)]
                nc.gpsimd.tensor_copy(v_st[j][:, :, :], src).then_inc(v_staged, 1)

            pool.wait_ge(v_copied, TT + 1)
            for j in range(2):
                stage_v(j, j)
            gates_gpsimd(pool, 0)
            with pool.Fori(1, H_FX // 2) as i:
                for j in range(2):
                    pool.wait_ge(fo_done, i * 2 + (j - 1))
                    stage_v(i * 2 + j, j)
                gates_gpsimd(pool, i)
            mid2_gpsimd(pool)

        tok_t = at("tok_t", [P, SEQ], I32, Z0 + (2 * KD + CHUNKS[0]) * ROW)
        tok_s = at("tok_s", [P, SEQ], I32, Z0 + (2 * KD + CHUNKS[0] + 1) * ROW)
        tok_x = at("tok_x", [P, SEQ], I32, Z0 + (2 * KD + CHUNKS[0] + 2) * ROW)
        tok_y = at("tok_y", [P, 2, SEQ], I32, Z0 + (2 * KD + CHUNKS[0] + 3) * ROW)
        iota_done, mask_step = sem("iota_done"), sem("mask_step")
        lb_step = sem("lb_step")

        def mix_prologue_scalar(act):
            act.wait_ge(lb_step, 1)
            nc.scalar.activation(lb[:, :], lb[:, :], ACT.Exp).then_inc(lb_step, 1)

        def mix_prologue(dve):
            dve.wait_ge(iota_done, 3)
            nc.vector.tensor_tensor(tok_t[:, :], tok_t[:, :], tok_s[:, :], ALU.bitwise_xor).then_inc(mask_step, 1)
            dve.wait_ge(mask_step, 1)
            nc.vector.tensor_tensor(tok_x[:, :], tok_t[:, :], tok_x[:, :], ALU.mult).then_inc(mask_step, 1)
            dve.wait_ge(mask_step, 2)
            nc.vector.tensor_scalar(hg_mask[:, DIAG, :], tok_t[:, :], 0.0, None, ALU.is_equal)
            for n, level in enumerate(LEVELS):
                nc.vector.tensor_scalar(tok_y[:, n % 2, :], tok_x[:, :], level, None,
                                        ALU.logical_shift_right).then_inc(mask_step, 1)
                dve.wait_ge(mask_step, 3 + n)
                nc.vector.tensor_scalar(hg_mask[:, n, :], tok_y[:, n % 2, :], 1.0, None, ALU.is_equal)
            dve.wait_ge(gains_landed, 16 * N_CONST_LOADS)
            nc.vector.tensor_tensor(lb[:, :], hg_lb[:, :], hg_lb[:, :], ALU.subtract).then_inc(lb_step, 1)
            dve.wait_ge(lb_step, 2)
            nc.vector.reciprocal(one_lb[:, :], lb[:, :]).then_inc(lb_step, 1)
            dve.wait_ge(lb_step, 3)
            nc.vector.tensor_tensor(lb[:, :], lb[:, :], one_lb[:, :], ALU.mult).then_inc(lb_step, 1)
            dve.wait_ge(lb_step, 4)
            nc.vector.tensor_tensor(lb[:, :], lb[:, :], lb[:, :], ALU.subtract).then_inc(lb_step, 1)
            dve.wait_ge(lb_step, 5)
            nc.vector.tensor_scalar(one_lb[:, :], lb[:, :], -1.0, 1.0, ALU.mult, ALU.add).then_inc(lb_step, 1)

        def make_mix_consts(pool):
            nc.gpsimd.iota(tok_t[:, :], pattern=[[0, TT], [1, P]], base=0, channel_multiplier=0).then_inc(iota_done, 1)
            nc.gpsimd.iota(tok_s[:, :], pattern=[[0, SEQ]], base=0, channel_multiplier=1).then_inc(iota_done, 1)
            nc.gpsimd.memset(tok_x[:, :], 1).then_inc(const_done, 1)
            pool.wait_ge(const_done, 1)
            nc.gpsimd.affine_select(tok_x[:, :], tok_x[:, :], pattern=[[0, TT], [1, P]], compare_op=ALU.is_gt, fill=0.0,
                                    base=0, channel_multiplier=-1).then_inc(iota_done, 1)
            nc.gpsimd.memset(neg_mask[:, :], 0.0).then_inc(const_done, 1)
            nc.gpsimd.memset(hg_reset[:, :], 1.0).then_inc(const_done, 1)
            nc.gpsimd.memset(fx_reset[:, :], 1.0).then_inc(const_done, 1)
            pool.wait_ge(const_done, 4)
            nc.gpsimd.affine_select(neg_mask[:, :], neg_mask[:, :], pattern=[[-1, P]], compare_op=ALU.is_ge, fill=NEG,
                                    base=0, channel_multiplier=1).then_inc(const_done, 1)
            nc.gpsimd.memset(hg_reset[:, 0:SEQ:P], 0.0).then_inc(const_done, 1)
            nc.gpsimd.memset(hg_reset[:, SEQ:T:DS_], 0.0).then_inc(const_done, 1)
            nc.gpsimd.memset(fx_reset[:, SEQ:T:DS_], 0.0).then_inc(const_done, 1)
            nc.gpsimd.memset(bmask[:, :], 1.0).then_inc(const_done, 1)
            pool.wait_ge(const_done, 9)
            nc.gpsimd.affine_select(bmask[:, :], bmask[:, :], pattern=[[-DS_, DB]], compare_op=ALU.is_ge, fill=0.0,
                                    base=0, channel_multiplier=1).then_inc(const_done, 1)
            pool.wait_ge(const_done, 10)
            nc.gpsimd.affine_select(bmask[:, :], bmask[:, :], pattern=[[DS_, DB]], compare_op=ALU.is_ge, fill=0.0,
                                    base=DS_ - 1, channel_multiplier=-1).then_inc(const_done, 1)
            pool.wait_ge(const_done, 11)
            nc.gpsimd.memset(d_sel[:, :], 1.0).then_inc(const_done, 1)
            nc.gpsimd.memset(d_causal[:, :], 0.0).then_inc(const_done, 1)
            pool.wait_ge(const_done, 13)
            nc.gpsimd.affine_select(two_heads[:, :].rearrange("p (a c) -> p a c", c=DH), ones[:, :].rearrange(
                "p (a c) -> p a c", c=DH), pattern=[[-DH, 2], [0, DH]], compare_op=ALU.is_ge, fill=0.0, base=0,
                channel_multiplier=1).then_inc(const_done, 1)
            nc.gpsimd.affine_select(d_later[:, :], ones[:, :], pattern=[[-1, P]], compare_op=ALU.is_ge, fill=0.0,
                                    base=0, channel_multiplier=1).then_inc(const_done, 1)
            nc.gpsimd.affine_select(d_sel[:, :], d_sel[:, :], pattern=[[-H_FX, DS_]], compare_op=ALU.is_ge, fill=0.0,
                                    base=0, channel_multiplier=1).then_inc(const_done, 1)
            nc.gpsimd.affine_select(d_causal[:, :], d_causal[:, :], pattern=[[-H_FX, DS_]], compare_op=ALU.is_ge,
                                    fill=NEG, base=0, channel_multiplier=1).then_inc(const_done, 1)
            pool.wait_ge(const_done, 17)
            nc.gpsimd.affine_select(two_heads[:, :].rearrange("p (a c) -> p a c", c=DH), two_heads[:, :].rearrange(
                "p (a c) -> p a c", c=DH), pattern=[[DH, 2], [0, DH]], compare_op=ALU.is_ge, fill=0.0, base=DH - 1,
                channel_multiplier=-1).then_inc(const_done, 1)
            nc.gpsimd.affine_select(d_later[:, :].rearrange("p (b g) -> p b g", g=PAGES), d_later[:, :].rearrange(
                "p (b g) -> p b g", g=PAGES), pattern=[[PAGES, DB], [0, PAGES]], compare_op=ALU.is_ge, fill=0.0,
                base=PAGES - 1, channel_multiplier=-1).then_inc(const_done, 1)
            nc.gpsimd.affine_select(d_sel[:, :], d_sel[:, :], pattern=[[H_FX, DS_]], compare_op=ALU.is_ge, fill=0.0,
                                    base=H_FX - 1, channel_multiplier=-1).then_inc(const_done, 1)
            pool.wait_ge(const_done, 20)
            pool.sem_inc(mix_consts, 1)

        class Steps:

            def __init__(self, name, steps):
                self.sem, self.steps = sem(name), steps.split()

            def after(self, step, turn):
                return turn * len(self.steps) + (self.steps.index(step) + 1)

        NL = len(LEVELS)
        S_LEVELS = [n for n, level in enumerate(LEVELS) if 2 ** (level + 1) <= DS_]
        h_act = Steps("hg_act", "stage_i exp_end exp_cum v_nat v_nat_s exp0 exp1 exp2 "
                      "k_nat k_nat_s exp3 exp4 exp5 exp6")
        h_dve = Steps("hg_dve", "k dend dend_s d0q d0k " +
                      " ".join((f"d{n + 1}q d{n + 1}k " if n + 1 < NL else "") + f"m{n}q" +
                               (f" p{n - 1}" if n else "") + (" state0 state1 state2 state3 snew" if n == 4 else "")
                               for n in range(NL)) +
                      f" p{NL - 1} p_diag ps0 ps1 ps2")
        h_pe = Steps("hg_pe", "it diag lv0 lv1 kt lv2 lv3 state sstate lv4 lv5 lv6 lvs out out_s")
        h_pool = Steps("hg_pool", "k_end m0k m1k v_wide m2k m3k sdec m4k q_cum m5k m6k")
        NORM_AT = {2: ("ms",), 3: ("r2", "r3"), 4: ("r4", "y"), 5: ("y2",), 6: ("out_lo",)}
        t_act = Steps("hg_norm_act", "out out_s ln_ms root out_hi")
        t_dve = Steps("hg_norm_dve", "ms r2 r3 r4 y y2 out_lo")
        t_pe = Steps("hg_norm_pe", "ss")
        t_pool = Steps("hg_norm_pool", "sq")

        ring_top[0] = RING
        h_k = buf("h_k", [P, T])
        h_c1 = buf("h_c1", [P, T])
        h_ex = [buf(f"h_ex{n}", [P, T]) for n in range(2)]
        h_qk = [buf(f"h_qk{n}", [P, T]) for n in range(2)]
        h_eA = buf("h_exp_cum", [P, T])
        h_qA = buf("h_q_cum", [P, T])
        h_kE = buf("h_k_end", [P, T])
        h_i = buf("h_values", [P, T])
        h_t = buf("h_root_step", [P, T])
        h_o = buf("h_out", [P, T])
        h_ms = buf("h_ms", [P, T])
        h_r = buf("h_r", [P, T])
        h_v = buf("h_v_nat", [P, TT + 1, P])
        h_kn = buf("h_k_nat", [P, TT + 1, P])
        h_sc = buf("h_scores", [P, SEQ])
        h_scs = buf("h_scores_s", [NS, NS])
        h_S = buf("h_states", [P, TT, P])
        h_S0 = buf("h_states_in", [P, DB, P])
        h_Sn = buf("h_states_out", [P, DB, P])
        h_vw = buf("h_v_wide", [NS, DB, P])
        settled = const("settled", [P, NL + 4])
        bmask = const("bmask", [NS, DB])
        sc_zero, bmask_step = sem("sc_zero"), sem("bmask_step")
        S0_landed, S_stored, Sn_stored = sem("S0_landed"), sem("S_stored"), sem("Sn_stored")

        T_A = T_F
        g_dve = Steps("hg_gate_dve", "f clip_f clip_small cum")
        g_pool = Steps("hg_gate_pool", "log_f")
        g_act = Steps("hg_gate_act", "ln_f ln_small")
        gate_f = at("hg_f", [P, H_HG, T], F32, Z0)
        gate_log = at("hg_log_f", [P, T], F32, Z0 + KD * ROW)
        gate_small = at("hg_log_small_f", [P, T], F32, Z0 + (KD + 1) * ROW)

        def f_tile(i):
            return gate_f[:, ds(i, 1), :].rearrange("p o t -> p (o t)")

        def gates_vector(dve, i, step):
            if step == "f":
                if isinstance(i, int):
                    dve.wait_ge(gates_done, 2 * H_HG)
                nc.vector.tensor_scalar(f_tile(i), mix_tile(T_F, i), one_lb[:, ds(i, 1)], lb[:, ds(i, 1)], ALU.mult,
                                        ALU.add).then_inc(g_dve.sem, 1)
                dve.wait_ge(g_dve.sem, g_dve.after("f", i))
                nc.vector.tensor_scalar(gate_log[:, :], f_tile(i), 2.0 ** -60, None, ALU.max).then_inc(g_dve.sem, 1)
                nc.vector.tensor_scalar(gate_small[:, :], f_tile(i), 2.0 ** -60, TINY, ALU.min, ALU.max)\
                    .then_inc(g_dve.sem, 1)
            else:
                dve.wait_ge(g_pool.sem, g_pool.after("log_f", i))
                nc.vector.tensor_tensor_scan(mix_tile(T_A, i), hg_reset[:, :], gate_log[:, :], 0.0, ALU.mult,
                                             ALU.add).then_inc(g_dve.sem, 1)

        def gates_scalar(act, i):
            act.wait_ge(g_dve.sem, g_dve.after("clip_small", i))
            nc.scalar.activation(gate_log[:, :], gate_log[:, :], ACT.Ln).then_inc(g_act.sem, 1)
            nc.scalar.activation(gate_small[:, :], gate_small[:, :], ACT.Ln, scale=2.0 ** 60).then_inc(g_act.sem, 1)

        def gates_gpsimd(pool, i):
            pool.wait_ge(g_act.sem, g_act.after("ln_small", i))
            nc.gpsimd.tensor_tensor(gate_log[:, :], gate_log[:, :], gate_small[:, :], ALU.add).then_inc(g_pool.sem, 1)

        def mid2_sync(sp):
            sp.wait_ge(fo_copied, H_FX)
            sp.wait_ge(v_stored, 16 * (TT + 1))
            sp.wait_ge(lf_stored, 32)

            def load_states(h):
                sp.dma_start(h_S0[:, :, :], io["state_hgrn"][0].rearrange("b h k v -> k h b v")[:, ds(h, 1), :, :]
                             .rearrange("k o b v -> k (o b) v")).then_inc(S0_landed, 16)

            def store_states(h):
                sp.wait_ge(h_dve.sem, h_dve.after("state3", h))
                sp.dma_start(s_prompt[0, 0, ds(h, 1)].rearrange("o k v -> k (o v)"), h_S[:, TT - 1, :]).then_inc(S_stored, 16)
                sp.wait_ge(h_dve.sem, h_dve.after("snew", h))
                sp.dma_start(s_sample[0].rearrange("b h k v -> k h b v")[:, ds(h, 1), :, :]
                             .rearrange("k o b v -> k (o b) v"), h_Sn[:, :, :]).then_inc(Sn_stored, 16)

            load_states(0)
            store_states(0)
            with sp.Fori(1, H_HG) as i:
                sp.wait_ge(h_pe.sem, h_pe.after("out_s", i - 1))
                sp.wait_ge(h_pool.sem, h_pool.after("sdec", i - 1))
                load_states(i)
                store_states(i)
            mid3_sync(sp)

        def mid2_stores_waited(sp):
            sp.wait_ge(S_stored, 16 * H_HG)
            sp.wait_ge(Sn_stored, 16 * H_HG)
            mid3_stores_waited(sp)

        def blocks(t, level, c):
            m = 2 ** level
            v = t[:, 0:c].rearrange("p (b h m) -> p b h m", h=2, m=m)
            return v[:, :, 0, :], v[:, :, 1, :], v[:, :, 0, m - 1:m].to_broadcast([P, c // (2 * m), m])

        def mid2_tensor(pe):
            def chunk(t, c):
                return t[:, c * P:c * P + N_TOK[c]]

            def level(src_k, src_q, b):
                for c in range(TT):
                    mm = pe.matmul(ps[:, b, c * P:(c + 1) * P], chunk(src_k, c), chunk(src_q, c), start=True, stop=True)
                return mm

            def head(i, first=False):
                pe.wait_ge(h_act.sem, h_act.after("stage_i", i))
                if first:
                    pe.wait_ge(sc_zero, 2)
                    pe.wait_ge(fo_copied, H_FX)
                else:
                    pe.wait_ge(h_dve.sem, h_dve.after("snew", i - 1))
                for c in range(TT + 1):
                    b, c0 = (3, c * P) if c < TT else (4, 0)
                    mm = pe.transpose(ps[0:N_TOK[c], b, c0:c0 + P], chunk(h_i, c), ident[:, :])
                mm.then_inc(h_pe.sem, 1)
                pe.wait_ge(h_dve.sem, h_dve.after("k", i))
                level(h_k, mix_tile(T_Q, i), 2).then_inc(h_pe.sem, 1)

                def decayed(n):
                    pe.wait_ge(h_dve.sem, h_dve.after(f"m{n}q", i))
                    pe.wait_ge(h_pool.sem, h_pool.after(f"m{n}k", i))
                    level(h_qk[n % 2], h_qk[n % 2], n % 2).then_inc(h_pe.sem, 1)

                decayed(0)
                decayed(1)
                if not first:
                    norm(i - 1)
                pe.wait_ge(h_pool.sem, h_pool.after("k_end", i))
                pe.wait_ge(h_act.sem, h_act.after("v_nat_s", i))
                for c in range(TT + 1):
                    b, c0 = (3, c * P) if c < TT else (4, 0)
                    mm = pe.transpose(ps[0:N_TOK[c], b, c0:c0 + P], chunk(h_kE, c), ident[:, :])
                mm.then_inc(h_pe.sem, 1)
                decayed(2)
                decayed(3)
                pe.wait_ge(h_act.sem, h_act.after("k_nat_s", i))
                for c in range(TT):
                    mm = pe.matmul(ps[:, 5, c * P:(c + 1) * P], h_kn[:, c, :], h_v[:, c, :], start=True, stop=True)
                mm.then_inc(h_pe.sem, 1)
                pe.wait_ge(h_pool.sem, h_pool.after("v_wide", i))
                for s in range(2):
                    mm = pe.matmul(ps[:, 3 + s, :], h_kn[0:NS, TT, :],
                                   h_vw[:, s * DB // 2:(s + 1) * DB // 2, :].rearrange("t b v -> t (b v)"),
                                   start=True, stop=True)
                mm.then_inc(h_pe.sem, 1)
                for n in range(4, NL):
                    decayed(n)
                if not first:
                    pe.wait_ge(t_dve.sem, t_dve.after("ms", i - 1))
                for m, n in enumerate(S_LEVELS):
                    s = h_qk[n % 2][:, SEQ:T]
                    pe.matmul(ps[0:NS, 7, m * NS:(m + 1) * NS], s, s, start=True, stop=True)
                m = len(S_LEVELS)
                pe.matmul(ps[0:NS, 7, m * NS:(m + 1) * NS], h_k[:, SEQ:T], mix_tile(T_Q, i, cols=slice(SEQ, T)),
                          start=True, stop=True).then_inc(h_pe.sem, 1)
                pe.wait_ge(h_dve.sem, h_dve.after("ps2", i))
                pe.wait_ge(h_pool.sem, h_pool.after("q_cum", i))
                for c in range(TT):
                    o = ps[:, 6, c * P:(c + 1) * P]
                    mm = pe.matmul(o, h_v[:, c, :], h_sc[:, c * P:(c + 1) * P], start=True, stop=(c == 0))
                    if c:
                        mm = pe.matmul(o, h_S[:, c - 1, :], chunk(h_qA, c), start=False, stop=True)
                mm.then_inc(h_pe.sem, 1)
                pe.wait_ge(S0_landed, i * 16 + 16)
                o = ps[:, 7, P:P + NS]
                pe.matmul(o, h_v[0:NS, TT, :], h_scs[:, :], start=True, stop=False, skip_group_check=True)
                for b in range(DB):
                    mm = pe.matmul(o[:, b * DS_:(b + 1) * DS_], h_S0[:, b, :], h_qA[:, SEQ + b * DS_:SEQ + (b + 1) * DS_],
                                   start=False, stop=(b == DB - 1), skip_group_check=True)
                mm.then_inc(h_pe.sem, 1)

            def norm(i):
                pe.wait_ge(t_pool.sem, t_pool.after("sq", i))
                for s in range(2):
                    mm = pe.matmul(ps[:, 6 + s, 0:HALF], ones[:, :], h_ms[:, s * HALF:(s + 1) * HALF], start=True,
                                   stop=True)
                mm.then_inc(t_pe.sem, 1)

            head(0, first=True)
            with pe.Fori(1, H_HG) as i:
                head(i)
            norm(H_HG - 1)
            mid3_tensor(pe)

        def mid2_scalar(act):
            def head(i, first=False):
                def go(out, src, func, **kw):
                    nc.scalar.activation(out, src, func, **kw).then_inc(h_act.sem, 1)

                if first:
                    act.wait_ge(fo_copied, H_FX)
                    act.wait_ge(v_stored, 16 * (TT + 1))
                    act.wait_ge(lf_stored, 32)
                    act.wait_ge(fo_done, H_FX)
                else:
                    act.wait_ge(h_dve.sem, h_dve.after("snew", i - 1))
                go(h_i[:, :], mix_tile(T_I, i), ACT.Copy)
                act.wait_ge(h_dve.sem, h_dve.after("dend_s", i))
                go(h_c1[:, :], h_c1[:, :], ACT.Exp)
                go(h_eA[:, :], mix_tile(T_A, i), ACT.Exp)
                act.wait_ge(h_pe.sem, h_pe.after("it", i))
                go(h_v[:, 0:TT, :].rearrange("p c v -> p (c v)"), ps[:, 3, :], ACT.Copy)
                go(h_v[0:NS, TT, :], ps[0:NS, 4, 0:P], ACT.Copy)

                def exps(n0, n1):
                    for n in range(n0, n1):
                        act.wait_ge(h_dve.sem, h_dve.after(f"d{n}k", i))
                        c = h_ex[n % 2][:, 0:SEQ if LEVELS[n] > 1 else T]
                        go(c, c, ACT.Exp)

                exps(0, 1)
                if not first:
                    take_out(i - 1)
                exps(1, 3)
                act.wait_ge(h_pe.sem, h_pe.after("kt", i))
                go(h_kn[:, 0:TT, :].rearrange("p c v -> p (c v)"), ps[:, 3, :], ACT.Copy)
                go(h_kn[0:NS, TT, :], ps[0:NS, 4, 0:P], ACT.Copy)
                exps(3, 4)
                if not first:
                    root(i - 1)
                exps(4, NL)
                if not first:
                    out_hi(i - 1)

            def take_out(i):
                act.wait_ge(h_pe.sem, h_pe.after("out", i))
                nc.scalar.activation(h_o[:, 0:SEQ], ps[:, 6, :], ACT.Copy).then_inc(t_act.sem, 1)
                act.wait_ge(h_pe.sem, h_pe.after("out_s", i))
                nc.scalar.activation(h_o[:, SEQ:T], ps[:, 7, P:P + NS], ACT.Copy).then_inc(t_act.sem, 1)

            def root(i):
                act.wait_ge(t_dve.sem, t_dve.after("ms", i))
                nc.scalar.activation(h_r[:, :], h_ms[:, :], ACT.Ln).then_inc(t_act.sem, 1)
                act.wait_ge(t_act.sem, t_act.after("ln_ms", i))
                nc.scalar.activation(h_r[:, :], h_r[:, :], ACT.Exp, scale=-0.5).then_inc(t_act.sem, 1)

            def out_hi(i):
                act.wait_ge(t_dve.sem, t_dve.after("y2", i))
                nc.scalar.activation(o_hi[:, ds(i, 1), :].rearrange("p o t -> p (o t)"), h_o[:, :], ACT.Copy)\
                    .then_inc(t_act.sem, 1)

            head(0, first=True)
            with act.Fori(1, H_HG) as i:
                head(i)
            take_out(H_HG - 1)
            root(H_HG - 1)
            out_hi(H_HG - 1)
            mid3_scalar(act)

        def mid2_vector(dve):
            dve.wait_ge(fo_done, H_FX)
            dve.wait_ge(v_stored, 16 * (TT + 1))
            dve.wait_ge(lf_stored, 32)
            dve.wait_ge(fo_copied, H_FX)
            nc.vector.memset(h_sc[:, :], 0.0).then_inc(sc_zero, 1)
            nc.vector.memset(h_scs[:, :], 0.0).then_inc(sc_zero, 1)
            dve.wait_ge(sc_zero, 2)

            def head(i, first=False):
                def own(step, turn=i):
                    dve.wait_ge(h_dve.sem, h_dve.after(step, turn))

                def act_done(step):
                    dve.wait_ge(h_act.sem, h_act.after(step, i))

                def pe_done(step):
                    dve.wait_ge(h_pe.sem, h_pe.after(step, i))

                def pool_done(step):
                    dve.wait_ge(h_pool.sem, h_pool.after(step, i))

                if first:
                    dve.wait_ge(g_dve.sem, g_dve.after("cum", H_HG - 1))
                nc.vector.tensor_scalar(h_k[:, :], f_tile(i), -1.0, 1.0, ALU.mult, ALU.add).then_inc(h_dve.sem, 1)
                A = mix_tile(T_A, i)

                def diffs(n):
                    c = SEQ if LEVELS[n] > 1 else T
                    a_k, a_q, a_r = blocks(A, LEVELS[n], c)
                    d_k, d_q, _ = blocks(h_ex[n % 2], LEVELS[n], c)
                    nc.vector.tensor_tensor(d_q, a_q, a_r, ALU.subtract).then_inc(h_dve.sem, 1)
                    nc.vector.tensor_tensor(d_k, a_r, a_k, ALU.subtract).then_inc(h_dve.sem, 1)

                def decayed(n):
                    c = SEQ if LEVELS[n] > 1 else T
                    act_done(f"exp{n}")
                    if n >= 2:
                        pe_done(f"lv{n - 2}")
                    _, e_q, _ = blocks(h_ex[n % 2], LEVELS[n], c)
                    _, q, _ = blocks(mix_tile(T_Q, i), LEVELS[n], c)
                    _, o_q, _ = blocks(h_qk[n % 2], LEVELS[n], c)
                    nc.vector.tensor_tensor(o_q, q, e_q, ALU.mult).then_inc(h_dve.sem, 1)

                def settle(n):
                    nc.vector.memset(settled[:, n:n + 1], 0.0)

                def pick(n):
                    pe_done(f"lv{n}")
                    if n:
                        own(f"p{n - 1}")
                    settle(n)
                    nc.vector.copy_predicated(h_sc[:, :], hg_mask[:, n, :], ps[:, n % 2, :]).then_inc(h_dve.sem, 1)

                end = A[:, P - 1:SEQ:P].rearrange("p (c o) -> p c o", o=1)
                ends = A[:, SEQ + DS_ - 1:T:DS_].rearrange("p (c o) -> p c o", o=1)
                nc.vector.tensor_tensor(h_c1[:, 0:SEQ].rearrange("p (c t) -> p c t", t=P), end.to_broadcast([P, TT, P]),
                                        A[:, 0:SEQ].rearrange("p (c t) -> p c t", t=P), ALU.subtract).then_inc(h_dve.sem, 1)
                nc.vector.tensor_tensor(h_c1[:, SEQ:T].rearrange("p (c t) -> p c t", t=DS_),
                                        ends.to_broadcast([P, DB, DS_]),
                                        A[:, SEQ:T].rearrange("p (c t) -> p c t", t=DS_), ALU.subtract).then_inc(h_dve.sem, 1)
                diffs(0)
                for n in range(NL):
                    if n + 1 < NL:
                        if n:
                            own(f"m{n - 1}q")
                            pool_done(f"m{n - 1}k")
                        diffs(n + 1)
                    decayed(n)
                    if n:
                        pick(n - 1)
                    if not first and n in NORM_AT:
                        norm(i - 1, NORM_AT[n])
                    if n == 4:
                        pe_done("state")
                        act_done("exp_cum")
                        if not first:
                            dve.wait_ge(S_stored, i * 16)
                        for c in range(TT):
                            new = ps[:, 5, c * P:(c + 1) * P]
                            if c == 0:
                                nc.vector.tensor_copy(h_S[:, 0, :], new).then_inc(h_dve.sem, 1)
                                continue
                            own(f"state{c - 1}")
                            nc.vector.scalar_tensor_tensor(h_S[:, c, :], h_S[:, c - 1, :],
                                                           h_eA[:, c * P + P - 1:c * P + P], new, ALU.mult,
                                                           ALU.add).then_inc(h_dve.sem, 1)
                        pe_done("sstate")
                        pool_done("sdec")
                        flat = h_Sn[:, :, :].rearrange("p b v -> p (b v)")
                        nc.vector.tensor_tensor(flat, flat, ps[:, 3:5, :].rearrange("p b c -> p (b c)"), ALU.add)\
                            .then_inc(h_dve.sem, 1)
                pick(NL - 1)
                pe_done("diag")
                own(f"p{NL - 1}")
                settle(NL)
                nc.vector.copy_predicated(h_sc[:, :], hg_mask[:, DIAG, :], ps[:, 2, :]).then_inc(h_dve.sem, 1)
                pe_done("lvs")
                for m, n in enumerate(S_LEVELS + [DIAG]):
                    if m:
                        own(f"ps{m - 1}")
                    settle(NL + 1 + m)
                    nc.vector.copy_predicated(h_scs[:, :], hg_mask[0:NS, n, 0:NS], ps[0:NS, 7, m * NS:(m + 1) * NS])\
                        .then_inc(h_dve.sem, 1)

            def norm(i, steps):
                def own(step):
                    dve.wait_ge(t_dve.sem, t_dve.after(step, i))

                for step in steps:
                    if step == "ms":
                        dve.wait_ge(t_pe.sem, t_pe.after("ss", i))
                        op = nc.vector.tensor_scalar(halves(h_ms[:, :]), ps[:, 6:8, 0:HALF], 1.0 / P, EPS, ALU.mult, ALU.add)
                    elif step == "r2":
                        dve.wait_ge(t_act.sem, t_act.after("root", i))
                        op = nc.vector.tensor_tensor(h_t[:, :], h_r[:, :], h_r[:, :], ALU.mult)
                    elif step == "r3":
                        own("r2")
                        op = nc.vector.scalar_tensor_tensor(h_t[:, :], h_t[:, :], -0.5, h_ms[:, :], ALU.mult, ALU.mult)
                    elif step == "r4":
                        own("r3")
                        op = nc.vector.scalar_tensor_tensor(h_r[:, :], h_t[:, :], 1.5, h_r[:, :], ALU.add, ALU.mult)
                    elif step == "y":
                        own("r4")
                        op = nc.vector.scalar_tensor_tensor(h_o[:, :], h_o[:, :], hg_gain[:, ds(i, 1)], h_r[:, :], ALU.mult,
                                                            ALU.mult)
                    elif step == "y2":
                        own("y")
                        op = nc.vector.tensor_tensor(h_o[:, :], h_o[:, :], mix_tile(T_G, i), ALU.mult)
                    else:
                        dve.wait_ge(t_act.sem, t_act.after("out_hi", i))
                        op = nc.vector.tensor_tensor(o_lo[:, ds(i, 1), :].rearrange("p o t -> p (o t)"), h_o[:, :],
                                                     o_hi[:, ds(i, 1), :].rearrange("p o t -> p (o t)").bitcast(F32),
                                                     ALU.subtract)
                    op.then_inc(t_dve.sem, 1)

            head(0, first=True)
            with dve.Fori(1, H_HG) as i:
                head(i)
            norm(H_HG - 1, t_dve.steps)
            mid3_vector(dve)

        def mid2_gpsimd(pool):
            def head(i, first=False):
                def go(op):
                    op.then_inc(h_pool.sem, 1)

                def dve_done(step, turn=i):
                    pool.wait_ge(h_dve.sem, h_dve.after(step, turn))

                pool.wait_ge(h_act.sem, h_act.after("exp_end", i))
                go(nc.gpsimd.tensor_tensor(h_kE[:, :], h_k[:, :], h_c1[:, :], ALU.mult))

                def keys(n):
                    c = SEQ if LEVELS[n] > 1 else T
                    pool.wait_ge(h_act.sem, h_act.after(f"exp{n}", i))
                    if n >= 2:
                        pool.wait_ge(h_pe.sem, h_pe.after(f"lv{n - 2}", i))
                    (o, _, _), (k, _, _), (e, _, _) = (blocks(t, LEVELS[n], c) for t in (h_qk[n % 2], h_k, h_ex[n % 2]))
                    go(nc.gpsimd.tensor_tensor(o, k, e, ALU.mult))

                keys(0)
                if not first:
                    squares_of_out(i - 1)
                keys(1)
                pool.wait_ge(h_act.sem, h_act.after("v_nat_s", i))
                go(nc.gpsimd.tensor_tensor(h_vw[:, :, :], h_v[0:NS, TT:TT + 1, :].to_broadcast([NS, DB, P]),
                                           bmask[:, :].rearrange("t (b o) -> t b o", o=1).to_broadcast([NS, DB, P]), ALU.mult))
                keys(2)
                keys(3)
                pool.wait_ge(S0_landed, i * 16 + 16)
                if not first:
                    pool.wait_ge(Sn_stored, i * 16)
                dec = h_eA[:, SEQ + DS_ - 1:T:DS_].rearrange("p (b o) -> p b o", o=1).to_broadcast([P, DB, P])
                go(nc.gpsimd.tensor_tensor(h_Sn[:, :, :], h_S0[:, :, :], dec, ALU.mult))
                keys(4)
                go(nc.gpsimd.tensor_tensor(h_qA[:, :], mix_tile(T_Q, i), h_eA[:, :], ALU.mult))
                keys(5)
                keys(6)

            def squares_of_out(i):
                pool.wait_ge(t_act.sem, t_act.after("out_s", i))
                nc.gpsimd.tensor_tensor(h_ms[:, :], h_o[:, :], h_o[:, :], ALU.mult).then_inc(t_pool.sem, 1)

            head(0, first=True)
            with pool.Fori(1, H_HG) as i:
                head(i)
            squares_of_out(H_HG - 1)
            mid3_gpsimd(pool)

        NR = DS_ * H_FX
        NB2 = 2 * NR
        GR = 4
        N_GR = PAGES // GR
        NJ = D_FX // P
        ITEMS = N_GR * NJ
        N_MAX, N_EXP, N_PT, N_PC = 1, 2, 5, 6
        V_LAG = 2
        A_PAGES = {n: [] for n in range(ITEMS)}
        B_PAGES = {n: [] for n in range(ITEMS)}
        for m in range(PAGES):
            if N_PC + 1 + m < ITEMS - 1:
                A_PAGES[N_PC + 1 + m].append(m)
            elif N_PC + 1 + m <= ITEMS:
                A_PAGES[ITEMS - 1].append(m)
            else:
                B_PAGES[min(m - (ITEMS - N_PC), N_PT - V_LAG)].append(m)
        HALF_PAGES = PAGES // 2
        V_UNTIL = [[2, 4, 6, 8][g] for g in range(N_GR)]
        SCORES_AT = {6: 0, 10: 1, 14: 2}
        MAX_AT = {9: 0, 13: 1}
        OUT_AT = {N_PC: 0, N_PC + 1: 1, N_PC + 3: 2}

        z_top = [Z0 + 2 * KD * ROW]

        def zbuf(name, shape, dt=F32):
            t = at(name, shape, dt, z_top[0])
            z_top[0] += int(np.prod(shape[1:])) * 4
            assert z_top[0] <= Z0 + 2 * KD * ROW + T_FQ * ROW
            return t

        ring_top[0] = RING
        d_k = [buf(f"d_keys{n}", [P, GR, D_FX]) for n in range(2)]
        d_v = [buf(f"d_values{n}", [P, GR, D_FX]) for n in range(2)]
        d_kh = buf("d_keysT_hi", [P, NJ, GR * PAGE], F32R)
        d_kl = buf("d_keysT_lo", [P, NJ, GR * PAGE], F32R)
        d_vh = buf("d_values_hi", [P, 4, D_FX], F32R)
        d_vl = buf("d_values_lo", [P, 4, D_FX], F32R)
        d_q = buf("d_queries", [P, NJ * (NB2 + 2)], F32R)
        d_pT = buf("d_probT", [P, PAGES, NB2], F32R)
        d_sfx = zbuf("d_suffix", [NR, PAST])
        d_s = zbuf("d_scores", [NR, PAST + NS])
        d_lf = zbuf("d_log_f", [P, PAGE * H_FX])
        d_inc = zbuf("d_log_f_sums", [P, H_FX, PAGE])
        d_x = zbuf("d_scores_lo", [NR, D_FX + NS])
        d_ox = zbuf("d_out_lo", [NR, D_FX])
        d_o = zbuf("d_out", [NR, D_FX])
        d_od = zbuf("d_out_own", [NR, DB, DH])
        d_tot = zbuf("d_page_sums", [P, H_FX])
        ring_top[0] = RING
        fn_q = [buf(f"fn_q{n}", [P, T]) for n in range(2)]
        fn_m = [buf(f"fn_m{n}", [P, T]) for n in range(2)]
        fn_r = [buf(f"fn_r{n}", [P, T]) for n in range(2)]
        d_pTn = zbuf("d_probT_new", [NS, NB2], F32R)
        d_knh = zbuf("d_new_keys_hi", [P, NJ, NS], F32R)
        d_knl = zbuf("d_new_keys_lo", [P, NJ, NS], F32R)
        d_vnh = at("d_new_values_hi", [NS, D_FX], F32R, SUMSQ_AT)
        d_vnl = at("d_new_values_lo", [NS, D_FX], F32R, SQ_AT)
        d_nb = const("d_new_bias", [NR, DB * (NS + DS_)])
        d_cum = const("d_cum_rows", [NR, NS])
        d_cq = const("d_cum_query", [NR, DB])
        d_e8 = const("d_spread", [H_FX, NR])
        d_hm = const("d_head_mask", [NR, H_FX])
        d_sel = const("d_step_mask", [NR, DS_])
        d_causal = const("d_causal", [NR, DS_])
        d_cqx = const("d_cum_pick", [NR, DB, DS_])
        d_later = const("d_later_pages", [P, P])
        d_small = const("d_small", [NR, 6 + N_GR])
        suf_d = nc.dram_tensor("suffix_scratch", (DB * PAGES, H_FX, PAGE), F32, kind="Internal").ap()

        dc_step = sem("dc_step")
        dcx_done = sem("dcx_done")
        dvn_hi, dvn_lo = sem("dvn_hi"), sem("dvn_lo")
        lf_landed, lf_scan, tot_done, suf_ready, suf_stored = (sem(n) for n in (
            "lf_landed", "lf_scan", "tot_done", "suf_ready", "suf_stored"))
        dk_landed = [sem(f"dk_landed{n}") for n in range(2)]
        dv_landed = [sem(f"dv_landed{n}") for n in range(2)]
        sfx_landed = sem("sfx_landed")
        dq_zero, dkn_hi, dkn_lo = sem("dq_zero"), sem("dkn_hi"), sem("dkn_lo")
        qh_done, ql_done = sem("qh_done"), sem("ql_done")
        kT_done, kh_done, kl_done, qk_done, new_done = (sem(n) for n in (
            "kT_done", "kh_done", "kl_done", "qk_done", "new_done"))
        sx_done, s1_done, s2_done = sem("sx_done"), sem("s1_done"), sem("s2_done")
        dmg_done = sem("dmg_done")
        dmx_done, dexp_done, dinv_done = sem("dmx_done"), sem("dexp_done"), sem("dinv_done")
        pT_done, pth_done, ptl_done = sem("pT_done"), sem("pth_done"), sem("ptl_done")
        vh_done, pv_done = sem("vh_done"), sem("pv_done")
        vl_done = [sem("vl_done_even"), sem("vl_done_odd")]
        ox_done, o_step, oT_done, oF_done = sem("ox_done"), sem("o_step"), sem("oT_done"), sem("oF_done")
        fn_sq, fn_ss, fn_v, fn_a, fn_hi, fn_lo = (sem(n) for n in ("fn_sq", "fn_ss", "fn_v", "fn_a", "fn_hi", "fn_lo"))
        N_SC = N_GR + 1

        def mid3_sync(sp):
            sp.wait_ge(t_dve.sem, t_dve.after("out_lo", H_HG - 1))
            sp.wait_ge(S_stored, 16 * H_HG)
            sp.wait_ge(Sn_stored, 16 * H_HG)

            def page_loads(b, g, cache, dst, landed):
                _, pages = nc.values_load_multi_w_load_instructions(
                    page_row[0:1, ds(b * PAGES + g * GR, GR)], engines=(mybir.EngineType.SP,), min_val=0,
                    max_val=N_POOL - 1)
                for m, page in enumerate(pages):
                    sp.dma_start(dst[g % 2][:, m, :], cache[0, ds(page, 1)].rearrange("o s h d -> (o s) (h d)"))\
                        .then_inc(landed[g % 2], 16)

            def keys(b, g, free=None):
                if free is not None:
                    sp.wait_ge(kT_done, free)
                page_loads(b, g, io["cache_k"], d_k, dk_landed)

            def values(b, g, free=None):
                if free is not None:
                    for n in range(2):
                        sp.wait_ge(vl_done[n], free)
                page_loads(b, g, io["cache_v"], d_v, dv_landed)

            def suffix(b, free=None):
                if free is not None:
                    sp.wait_ge(s1_done, free)
                for t in range(DS_):
                    sp.dma_start(d_sfx[t * H_FX:(t + 1) * H_FX, :].rearrange("h (g s) -> h g s", s=PAGE),
                                 suf_d[ds(b * PAGES, PAGES)].rearrange("g h s -> h g s")).then_inc(sfx_landed, 16)

            keys(0, 0)
            keys(0, 1)
            sp.wait_ge(suf_ready, 1)
            sp.dma_start(suf_d, d_inc[:, :, :]).then_inc(suf_stored, 16)
            sp.wait_ge(suf_stored, 16)
            suffix(0)

            def turn(b, with_keys=True, next_keys=True, with_values=True, first=False):
                def free(sample, g):
                    return None if first and g < 2 else sample * HALF_PAGES + V_UNTIL[(g + 2) % N_GR]

                s = b - 1
                if with_values:
                    values(s, 0, free(s - 1, 0))
                if with_keys:
                    keys(b, 2, b * ITEMS + NJ)
                if with_values:
                    values(s, 1, free(s - 1, 1))
                if with_keys:
                    keys(b, 3, b * ITEMS + 2 * NJ)
                if with_values:
                    values(s, 2, free(s, 2))
                if next_keys:
                    keys(b + 1, 0, b * ITEMS + 3 * NJ)
                if with_values:
                    values(s, 3, free(s, 3))
                if next_keys:
                    keys(b + 1, 1, b * ITEMS + 4 * NJ)
                    suffix(b + 1, b * N_SC + N_GR)

            turn(0, with_values=False)
            turn(1, first=True)
            with sp.Fori(2, DB - 1) as b:
                turn(b)
            turn(DB - 1, next_keys=False)
            turn(DB, with_keys=False, next_keys=False)
            sp.wait_ge(vl_done[0], DB * HALF_PAGES)
            sp.wait_ge(vl_done[1], DB * HALF_PAGES)
            sp.wait_ge(pv_done, DB * (PAGES + 1))
            sp.wait_ge(fn_lo, NJ)

        def mid3_stores_waited(sp):
            pass

        def new_rows_tensor(pe):
            pe.wait_ge(dc_step, 1)
            pe.wait_ge(fx_step, 8)
            pe.wait_ge(lf_copied, 1)
            pe.matmul(ps[0:NR, 7, 0:NS], d_e8[:, :], fx_cum[:, SEQ:T], start=True, stop=True).then_inc(dcx_done, 1)

        def new_rows_vector(dve):
            nc.vector.tensor_copy(d_e8[:, :].rearrange("k (t h) -> k t h", h=H_FX),
                                  ident[0:H_FX, 0:H_FX].rearrange("k (o h) -> k o h", o=1).to_broadcast([H_FX, DS_, H_FX]))\
                .then_inc(dc_step, 1)
            nc.vector.tensor_reduce(d_hm[:, :], ident[0:NR, 0:NR].rearrange("p (t h) -> p h t", h=H_FX), AX_X,
                                    ALU.add).then_inc(dc_step, 1)
            nc.vector.memset(d_nb[:, :], NEG).then_inc(dc_step, 1)
            dve.wait_ge(dvn_hi, 1)
            nc.vector.tensor_tensor(d_vnl[:, :], v_nat[0:NS, TT, :], d_vnh[:, :].bitcast(F32), ALU.subtract)\
                .then_inc(dvn_lo, 1)
            dve.wait_ge(dcx_done, 1)
            nc.vector.tensor_copy(d_cum[:, :], ps[0:NR, 7, 0:NS]).then_inc(dc_step, 1)
            dve.wait_ge(dc_step, 4)
            own = d_cum[:, :].rearrange("p (b s) -> p b s", s=DS_)

            def each(t):
                return t[:, :].rearrange("p (o s) -> p o s", o=1).to_broadcast([NR, DB, DS_])

            nc.vector.tensor_tensor(d_cqx[:, :, :], own, each(d_sel), ALU.mult).then_inc(dc_step, 1)
            nc.vector.tensor_tensor(d_nb[:, :].rearrange("p (b c) -> p b c", b=DB)[:, :, 0:DS_], each(d_causal), own,
                                    ALU.subtract).then_inc(dc_step, 1)
            dve.wait_ge(dc_step, 6)
            nc.vector.tensor_reduce(d_cq[:, :], d_cqx[:, :, :], AX_X, ALU.add).then_inc(dc_step, 1)

        def new_rows_scalar(act):
            act.wait_ge(v_copied, TT + 1)
            nc.scalar.activation(d_vnh[:, :], v_nat[0:NS, TT, :], ACT.Copy).then_inc(dvn_hi, 1)

        def values_low(engine, m):
            engine.tensor_tensor(d_vl[:, m % 4, :], d_v[m // GR % 2][:, m % GR, :], d_vh[:, m % 4, :].bitcast(F32),
                                 ALU.subtract).then_inc(vl_done[m % 2], 1)

        def mid3_tensor(pe):
            def items(b):
                return b * ITEMS

            def keysT(b, n):
                g, j = divmod(n, NJ)
                if j == 0:
                    pe.wait_ge(dk_landed[g % 2], b * (2 * GR * 16) + (g // 2 + 1) * GR * 16)
                if not (isinstance(b, int) and b == 0 and n < 4):
                    pe.wait_ge(kl_done, items(b) + (n - 3))
                for m in range(GR):
                    mm = pe.transpose(ps[:, j, m * PAGE:(m + 1) * PAGE], d_k[g % 2][:, m, j * P:(j + 1) * P], ident[:, :])
                mm.then_inc(kT_done, 1)

            def qk(b, n):
                g, j = divmod(n, NJ)
                if n == 0:
                    pe.wait_ge(ql_done, b * 2 + 2)
                if j == 0 and not (isinstance(b, int) and b == 0 and g < 2):
                    last = {0: 0, 1: -1, 2: 1, 3: 2}[g]
                    pe.wait_ge(s1_done, b * N_SC + last)
                    pe.wait_ge(sx_done, b * N_SC + last)
                    if g == 1:
                        pe.wait_ge(ptl_done, b * 2 - 1)
                pe.wait_ge(kl_done, items(b) + (n + 1))
                q = d_q[:, j * NB2:(j + 1) * NB2]
                pe.matmul(ps[0:NB2, 4 + g % 2, :], q, d_kh[:, j, :], start=(j == 0), stop=False, skip_group_check=True)
                pe.matmul(ps[0:NR, 4 + g % 2, :], q[:, 0:NR], d_kl[:, j, :], start=False, stop=(j == NJ - 1),
                          skip_group_check=True).then_inc(qk_done, 1)

            def new_keys(b):
                pe.wait_ge(s1_done, b * N_SC + 3)
                pe.wait_ge(sx_done, b * N_SC + 3)
                for j in range(NJ):
                    q = d_q[:, j * NB2:(j + 1) * NB2]
                    pe.matmul(ps[0:NB2, 4, 0:NS], q, d_knh[:, j, :], start=(j == 0), stop=False, skip_group_check=True)
                    mm = pe.matmul(ps[0:NR, 4, 0:NS], q[:, 0:NR], d_knl[:, j, :], start=False, stop=(j == NJ - 1),
                                   skip_group_check=True)
                mm.then_inc(new_done, 1)

            def probsT(b):
                for m in range(PAGES):
                    pe.transpose(ps[:, 7, m * NR:(m + 1) * NR], d_s[:, m * PAGE:(m + 1) * PAGE], ident[0:NR, 0:NR])
                pe.transpose(ps[0:NS, 5, 0:NR], d_s[:, PAST:PAST + NS], ident[0:NR, 0:NR]).then_inc(pT_done, 1)

            def pv(b, m):
                if m == 0:
                    pe.wait_ge(ptl_done, b * 2 + 2)
                    if not (isinstance(b, int) and b == 0):
                        pe.wait_ge(o_step, b * 3 - 2)
                if m < PAGES:
                    pe.wait_ge(vl_done[m % 2], b * HALF_PAGES + (m // 2 + 1))
                hi, lo, p = (d_vh[:, m % 4, :], d_vl[:, m % 4, :], d_pT[:, m, :]) if m < PAGES else \
                    (d_vnh[:, :], d_vnl[:, :], d_pTn[:, :])
                pe.matmul(ps[0:NB2, 6, :], p, hi, start=(m == 0), stop=False, skip_group_check=True)
                pe.matmul(ps[0:NR, 6, :], p[:, 0:NR], lo, start=False, stop=(m == PAGES), skip_group_check=True)\
                    .then_inc(pv_done, 1)

            def turn(b, keys=True, a=True, last=True):
                for n in range(ITEMS):
                    if keys:
                        keysT(b, n)
                    if a and n == N_PT:
                        pe.wait_ge(dexp_done, b * 2)
                    if keys and n >= 2:
                        qk(b, n - 2)
                    if last and n >= V_LAG:
                        for m in B_PAGES[n - V_LAG]:
                            pv(b - 2, m)
                        if n == N_PT:
                            pv(b - 2, PAGES)
                    if a and n == N_PT:
                        probsT(b - 1)
                    if a:
                        for m in A_PAGES[n - V_LAG] if n >= V_LAG else ():
                            pv(b - 1, m)
                for k in range(V_LAG):
                    if keys:
                        qk(b, ITEMS - 2 + k)
                    if a:
                        for m in A_PAGES[ITEMS - V_LAG + k]:
                            pv(b - 1, m)
                if keys:
                    new_keys(b)

            pe.wait_ge(lf_scan, H_FX)
            pe.matmul(ps[:, 7, 0:H_FX], d_later[:, :], d_tot[:, :], start=True, stop=True).then_inc(tot_done, 1)
            pe.wait_ge(dkn_lo, 1)
            turn(0, a=False, last=False)
            turn(1, last=False)
            with pe.Fori(2, DB) as b:
                turn(b)
            turn(DB, keys=False)
            turn(DB + 1, keys=False, a=False)
            pe.wait_ge(o_step, 3 * DB)
            for b in range(DB):
                mm = pe.transpose(ps[0:DH, 4, b * NR:(b + 1) * NR], d_od[:, b, :], ident[0:NR, 0:NR])
            mm.then_inc(oT_done, 1)
            for i in range(NJ):
                pe.wait_ge(fn_sq, i + 1)
                b0 = 2 * (i % 2)
                if i >= 2:
                    pe.wait_ge(fn_v, 5 * (i - 2) + 1)
                for s in range(2):
                    mm = pe.matmul(ps[:, b0 + s, 0:HALF], two_heads[:, :], fn_q[i % 2][:, s * HALF:(s + 1) * HALF],
                                   start=True, stop=True)
                mm.then_inc(fn_ss, 1)
            pe.wait_ge(fn_lo, NJ)

        def mid3_scalar(act):
            act.wait_ge(t_dve.sem, t_dve.after("out_lo", H_HG - 1))
            nc.scalar.activation(d_knh[:, :, :], pT[:, T_FK:T_FK + NJ, SEQ:T], ACT.Copy).then_inc(dkn_hi, 1)
            act.wait_ge(dq_zero, 1)

            def turn(b, keys=True, a=True, last=True):
                if keys:
                    if not (isinstance(b, int) and b == 0):
                        act.wait_ge(new_done, b)
                    for p in range(2):
                        half = slice(p * DH, (p + 1) * DH)
                        dst = d_q[half, :].rearrange("k (j c) -> k j c", j=NJ)[:, :, p:p + NR:H_FX]
                        nc.scalar.activation(dst, pT[half, T_FQ:T_FQ + NJ, ds(b * DS_ + SEQ, DS_)], ACT.Copy,
                                             scale=SCALE).then_inc(qh_done, 1)
                for n in range(ITEMS):
                    if keys:
                        act.wait_ge(kT_done, b * ITEMS + (n + 1))
                        if not (isinstance(b, int) and b == 0 and n < 4):
                            act.wait_ge(qk_done, b * ITEMS + (n - 3))
                        nc.scalar.activation(d_kh[:, n % NJ, :], ps[:, n % NJ, :], ACT.Copy).then_inc(kh_done, 1)
                    if a and n in (N_EXP, N_EXP + 1):
                        part, cols = n - N_EXP, [slice(0, PAST // 2), slice(PAST // 2, PAST + NS)][n - N_EXP]
                        act.wait_ge(dmx_done, (b - 1) * 2 + 2)
                        nc.scalar.activation(d_s[:, cols], d_s[:, cols], ACT.Exp, bias=d_small[:, 1:2],
                                             accum_out=d_small[:, 4 + part:5 + part]).then_inc(dexp_done, 1)
                    if a and n == N_PC:
                        act.wait_ge(pT_done, b)
                        nc.scalar.activation(d_pTn[:, 0:NR], ps[0:NS, 5, 0:NR], ACT.Copy).then_inc(pth_done, 1)
                        nc.scalar.activation(d_pT[:, :, 0:NR], ps[:, 7, :].rearrange("s (g r) -> s g r", r=NR),
                                             ACT.Copy).then_inc(pth_done, 1)
                    if last and n == N_PC:
                        act.wait_ge(pv_done, b * (PAGES + 1) - (PAGES + 1))
                        nc.scalar.activation(d_ox[:, :], ps[NR:NB2, 6, :], ACT.Copy).then_inc(ox_done, 1)
                    if keys and n in SCORES_AT:
                        scores_low(b, SCORES_AT[n])
                    if last:
                        for m in B_PAGES[n]:
                            values_high(b - 2, m)
                    if a:
                        for m in A_PAGES[n]:
                            values_high(b - 1, m)
                if keys:
                    scores_low(b, N_GR - 1)
                    act.wait_ge(new_done, b + 1)
                    nc.scalar.activation(d_x[:, D_FX:D_FX + NS], ps[NR:NB2, 4, 0:NS], ACT.Copy).then_inc(sx_done, 1)

            def values_high(s, m):
                if m % GR == 0:
                    g = m // GR
                    act.wait_ge(dv_landed[g % 2], s * (2 * GR * 16) + (g // 2 + 1) * GR * 16)
                if m >= 4:
                    act.wait_ge(pv_done, s * (PAGES + 1) + (m - 3))
                elif not (isinstance(s, int) and s == 0):
                    act.wait_ge(pv_done, s * (PAGES + 1) + (m - 4))
                nc.scalar.activation(d_vh[:, m % 4, :], d_v[m // GR % 2][:, m % GR, :], ACT.Copy).then_inc(vh_done, 1)

            def if_free(b, g):
                if not (isinstance(b, int) and b == 0 and g == 0):
                    act.wait_ge(s2_done, b * N_SC + g)

            def scores_low(b, g):
                act.wait_ge(qk_done, b * ITEMS + (g + 1) * NJ)
                if_free(b, g)
                nc.scalar.activation(d_x[:, 0:D_FX], ps[NR:NB2, 4 + g % 2, :], ACT.Copy).then_inc(sx_done, 1)

            turn(0, a=False, last=False)
            turn(1, last=False)
            with act.Fori(2, DB) as b:
                turn(b)
            turn(DB, keys=False)
            turn(DB + 1, keys=False, a=False)
            for i in range(NJ):
                act.wait_ge(fn_v, 5 * i + 1)
                nc.scalar.activation(fn_r[i % 2][:, :], fn_m[i % 2][:, :], ACT.Ln).then_inc(fn_a, 1)
                act.wait_ge(fn_a, 2 * i + 1)
                nc.scalar.activation(fn_r[i % 2][:, :], fn_r[i % 2][:, :], ACT.Exp, scale=-0.5).then_inc(fn_a, 1)
                act.wait_ge(fn_v, 5 * i + 5)
                nc.scalar.activation(o_hi[:, H_HG + i, :], oF[:, T_FV + i, :], ACT.Copy).then_inc(fn_hi, 1)

        def mid3_vector(dve):
            dve.wait_ge(t_dve.sem, t_dve.after("out_lo", H_HG - 1))
            nc.vector.memset(d_q[:, :].bitcast(F32), 0.0).then_inc(dq_zero, 1)
            dve.wait_ge(lf_landed, 16)
            for h in range(H_FX):
                x = d_lf[:, h:PAGE * H_FX:H_FX]
                nc.vector.tensor_tensor_scan(d_inc[:, h, :], ones[:, :], x, 0.0, ALU.mult, ALU.add)
                op = nc.vector.tensor_reduce(d_tot[:, h:h + 1], x, AX_X, ALU.add)
                op.then_inc(lf_scan, 1)
            dve.wait_ge(tot_done, 1)
            nc.vector.tensor_copy(d_tot[:, :], ps[:, 7, 0:H_FX]).then_inc(lf_scan, 1)
            dve.wait_ge(lf_scan, H_FX + 1)
            nc.vector.tensor_tensor(d_inc[:, :, :], d_tot[:, :].rearrange("p (h o) -> p h o", o=1)
                                    .to_broadcast([P, H_FX, PAGE]), d_inc[:, :, :], ALU.subtract).then_inc(suf_ready, 1)
            dve.wait_ge(dkn_hi, 1)
            nc.vector.tensor_tensor(d_knl[:, :, :], pT[:, T_FK:T_FK + NJ, SEQ:T], d_knh[:, :, :].bitcast(F32),
                                    ALU.subtract).then_inc(dkn_lo, 1)

            def add_scores(b, g):
                if g < N_GR:
                    dve.wait_ge(qk_done, b * ITEMS + (g + 1) * NJ)
                    src, dst = ps[0:NR, 4 + g % 2, :], d_s[:, g * 512:(g + 1) * 512]
                    bias = d_sfx[:, g * 512:(g + 1) * 512]
                    if g == 0:
                        dve.wait_ge(sfx_landed, b * (16 * DS_) + 16 * DS_)
                        if not (isinstance(b, int) and b == 0):
                            dve.wait_ge(pT_done, b)
                else:
                    dve.wait_ge(new_done, b + 1)
                    src, dst, bias = ps[0:NR, 4, 0:NS], d_s[:, PAST:PAST + NS], d_nb[:, ds(b * NS, NS)]
                nc.vector.scalar_tensor_tensor(dst, src, d_cq[:, ds(b, 1)], bias, ALU.add, ALU.add).then_inc(s1_done, 1)

            def turn(b, keys=True, a=True, last=True):
                if keys:
                    dve.wait_ge(qh_done, b * 2 + 2)
                    for p in range(2):
                        half = slice(p * DH, (p + 1) * DH)
                        v = d_q[half, :].rearrange("k (j c) -> k j c", j=NJ)
                        nc.vector.scalar_tensor_tensor(v[:, :, NR + p:NR + p + NR:H_FX],
                                                       pT[half, T_FQ:T_FQ + NJ, ds(b * DS_ + SEQ, DS_)], SCALE,
                                                       v[:, :, p:p + NR:H_FX].bitcast(F32), ALU.mult, ALU.subtract)\
                            .then_inc(ql_done, 1)
                for n in range(ITEMS):
                    if keys:
                        dve.wait_ge(kh_done, b * ITEMS + (n + 1))
                        nc.vector.tensor_tensor(d_kl[:, n % NJ, :], ps[:, n % NJ, :], d_kh[:, n % NJ, :].bitcast(F32),
                                                ALU.subtract).then_inc(kl_done, 1)
                    if keys and n in MAX_AT:
                        group_max(b, MAX_AT[n])
                    if a and n == 0:
                        group_max(b - 1, N_GR - 2)
                    if a and n == N_MAX:
                        group_max(b - 1, N_GR - 1)
                        dve.wait_ge(dmg_done, b * N_GR)
                        nc.vector.tensor_reduce(d_small[:, 0:1], d_small[:, 6:6 + N_GR], AX_X, ALU.max)\
                            .then_inc(dmx_done, 1)
                        dve.wait_ge(dmx_done, b * 2 - 1)
                        nc.vector.tensor_scalar(d_small[:, 1:2], d_small[:, 0:1], -1.0, None, ALU.mult)\
                            .then_inc(dmx_done, 1)
                    if a and n == N_PC:
                        dve.wait_ge(pth_done, b * 2 - 1)
                        nc.vector.tensor_tensor(d_pTn[:, NR:NB2], ps[0:NS, 5, 0:NR], d_pTn[:, 0:NR].bitcast(F32),
                                                ALU.subtract).then_inc(ptl_done, 1)
                        dve.wait_ge(pth_done, b * 2)
                        nc.vector.tensor_tensor(d_pT[:, :, NR:NB2], ps[:, 7, :].rearrange("s (g r) -> s g r", r=NR),
                                                d_pT[:, :, 0:NR].bitcast(F32), ALU.subtract).then_inc(ptl_done, 1)
                    if last and n in OUT_AT:
                        outputs(b - 2, OUT_AT[n])
                    if a and n == N_PC + 2:
                        nc.vector.tensor_tensor(d_small[:, 2:3], d_small[:, 4:5], d_small[:, 5:6], ALU.add)\
                            .then_inc(dinv_done, 1)
                        dve.wait_ge(dinv_done, b * 2 - 1)
                        nc.vector.reciprocal(d_small[:, 3:4], d_small[:, 2:3]).then_inc(dinv_done, 1)
                    for with_them, pages, s in ((last, B_PAGES, b - 2), (a, A_PAGES, b - 1)):
                        for m in pages[n] if with_them else ():
                            if m % 2:
                                dve.wait_ge(vh_done, s * PAGES + (m + 1))
                                values_low(nc.vector, m)
                    if keys and n in SCORES_AT:
                        add_scores(b, SCORES_AT[n])
                if keys:
                    add_scores(b, N_GR - 1)
                    add_scores(b, N_GR)

            def group_max(b, g):
                end = g == N_GR - 1
                dve.wait_ge(s2_done, b * N_SC + (g + 1 + end))
                nc.vector.tensor_reduce(d_small[:, 6 + g:7 + g], d_s[:, g * 512:(g + 1) * 512 + end * NS], AX_X,
                                        ALU.max).then_inc(dmg_done, 1)

            def outputs(s, step):
                if step == 0:
                    dve.wait_ge(ox_done, s + 1)
                    nc.vector.tensor_tensor(d_o[:, :], ps[0:NR, 6, :], d_ox[:, :], ALU.add).then_inc(o_step, 1)
                    return
                if step == 2:
                    dve.wait_ge(o_step, s * 3 + 2)
                    nc.vector.tensor_reduce(d_od[:, ds(s, 1), :].rearrange("r o d -> r (o d)"),
                                            d_o[:, :].rearrange("r (h d) -> r d h", d=DH), AX_X, ALU.add)\
                        .then_inc(o_step, 1)
                    return
                dve.wait_ge(dinv_done, s * 2 + 2)
                dve.wait_ge(o_step, s * 3 + 1)
                o3 = d_o[:, :].rearrange("r (h d) -> r h d", d=DH)
                own = d_hm[:, :].rearrange("r (h o) -> r h o", o=1).to_broadcast([NR, H_FX, DH])
                nc.vector.scalar_tensor_tensor(o3, o3, d_small[:, 3:4], own, ALU.mult, ALU.mult).then_inc(o_step, 1)
            turn(0, a=False, last=False)
            turn(1, last=False)
            with dve.Fori(2, DB) as b:
                turn(b)
            turn(DB, keys=False)
            turn(DB + 1, keys=False, a=False)
            dve.wait_ge(oT_done, 1)
            for p in range(2):
                for j in range(NJ):
                    src = ps[0:DH, 4, 0:DB * NR].rearrange("d (b t h) -> d b t h", b=DB, h=H_FX)[:, :, :, 2 * j + p]
                    nc.vector.tensor_copy(oF[p * DH:(p + 1) * DH, T_FV + j, SEQ:T].rearrange("d (b t) -> d b t", t=DS_),
                                          src).then_inc(oF_done, 1)
            dve.wait_ge(oF_done, 2 * NJ)
            for i in range(NJ):
                dve.wait_ge(fn_ss, i + 1)
                b0 = 2 * (i % 2)
                m, r, t = fn_m[i % 2], fn_r[i % 2], fn_q[i % 2]
                nc.vector.tensor_scalar(halves(m[:, :]), ps[:, b0:b0 + 2, 0:HALF], 1.0 / DH, EPS, ALU.mult, ALU.add)\
                    .then_inc(fn_v, 1)
                dve.wait_ge(fn_a, 2 * i + 2)
                nc.vector.tensor_tensor(t[:, :], r[:, :], r[:, :], ALU.mult).then_inc(fn_v, 1)
                dve.wait_ge(fn_v, 5 * i + 2)
                nc.vector.scalar_tensor_tensor(t[:, :], t[:, :], -0.5, m[:, :], ALU.mult, ALU.mult).then_inc(fn_v, 1)
                dve.wait_ge(fn_v, 5 * i + 3)
                nc.vector.scalar_tensor_tensor(r[:, :], t[:, :], 1.5, r[:, :], ALU.add, ALU.mult).then_inc(fn_v, 1)
                dve.wait_ge(fn_v, 5 * i + 4)
                o = oF[:, T_FV + i, :]
                nc.vector.scalar_tensor_tensor(o, o, fx_gain[:, i:i + 1], r[:, :], ALU.mult, ALU.mult).then_inc(fn_v, 1)
                dve.wait_ge(fn_hi, i + 1)
                nc.vector.tensor_tensor(o_lo[:, H_HG + i, :], o, o_hi[:, H_HG + i, :].bitcast(F32), ALU.subtract)\
                    .then_inc(fn_lo, 1)

        def mid3_gpsimd(pool):
            pool.wait_ge(t_dve.sem, t_dve.after("out_lo", H_HG - 1))
            pool.indirect_dma_start(out=d_lf[:, :], out_offset=None, in_=io["cache_logf"][0].rearrange("n s h -> n (s h)"),
                                    in_offset=bass.IndirectOffsetOnAxis(ap=page_ids[:, 0:1], axis=0)).then_inc(lf_landed, 16)

            def add_low(b, g):
                n = N_SC * b + g
                pool.wait_ge(s1_done, b * N_SC + (g + 1))
                pool.wait_ge(sx_done, b * N_SC + (g + 1))
                if g < N_GR:
                    s, x = d_s[:, g * 512:(g + 1) * 512], d_x[:, 0:D_FX]
                else:
                    s, x = d_s[:, PAST:PAST + NS], d_x[:, D_FX:D_FX + NS]
                nc.gpsimd.tensor_tensor(s, s, x, ALU.add).then_inc(s2_done, 1)

            def turn(b, keys=True, a=True, last=True):
                for n in range(ITEMS):
                    for with_them, pages, s in ((last, B_PAGES, b - 2), (a, A_PAGES, b - 1)):
                        for m in pages[n] if with_them else ():
                            if m % 2 == 0:
                                pool.wait_ge(vh_done, s * PAGES + (m + 1))
                                values_low(nc.gpsimd, m)
                    if keys and n in SCORES_AT:
                        add_low(b, SCORES_AT[n])
                if keys:
                    add_low(b, N_GR - 1)
                    add_low(b, N_GR)

            turn(0, a=False, last=False)
            turn(1, last=False)
            with pool.Fori(2, DB) as b:
                turn(b)
            turn(DB, keys=False)
            turn(DB + 1, keys=False, a=False)
            pool.wait_ge(oF_done, 2 * NJ)
            for i in range(NJ):
                if i >= 2:
                    pool.wait_ge(fn_v, 5 * (i - 2) + 5)
                nc.gpsimd.tensor_tensor(fn_q[i % 2][:, :], oF[:, T_FV + i, :], oF[:, T_FV + i, :], ALU.mult)\
                    .then_inc(fn_sq, 1)

        @block.sync
        def _(sp):
            for i in range(TT + 1):
                src = io["x_prompt"][0, i * P:(i + 1) * P, :] if i < TT else io["x_sample"].rearrange("b t d -> (b t) d")
                sp.dma_start(x_nat[0:N_TOK[i], i, :], src).then_inc(x_landed[i], 16)
            for i, g in enumerate(("norm_ffn1", "norm_mix", "norm_ffn2")):
                sp.dma_start(gains[:, i, :], io[g][0].rearrange("(k p) -> p k", p=P),
                             allow_slow_non_contiguous=True).then_inc(gains_landed, 16)
            sp.dma_start(gains[:, 3, :], io["norm_final"].rearrange("(k p) -> p k", p=P),
                         allow_slow_non_contiguous=True).then_inc(gains_landed, 16)
            sp.dma_start(wf[:, :, :], io["w_in_mix"][0].rearrange("(k p) n -> p k n", p=P)[:, :, D_IN - H_FX:D_IN],
                         allow_slow_non_contiguous=True).then_inc(gains_landed, 16)

            for t, name in ((hg_lb, "hgrn_lb"), (hg_gain, "hgrn_out_gain"), (fx_gain, "fox_out_gain")):
                sp.dma_start(t[:, :], io[name][0].rearrange("(h p) -> p h", p=P),
                             allow_slow_non_contiguous=True).then_inc(gains_landed, 16)
            sp.dma_start(page_ids[:, :], io["page_table"].rearrange("b (g o) -> (b g) o", o=1)).then_inc(gains_landed, 16)
            sp.dma_start(page_row[:, :], io["page_table"].rearrange("(o b) g -> o (b g)", o=1)).then_inc(gains_landed, 16)
            sp.dma_start(f_bias[:, :], io["fox_f_bias"][0].rearrange("(h o) -> h o", o=1)).then_inc(gains_landed, 16)

            def slot_free(pair, j, first=False):
                if not first:
                    sp.wait_ge(w_lo_ready, 2 * pair + j - 1)

            def load_gate_up(pair, tile, j, w, first=False):
                slot_free(pair, j, first)
                dst = w_raw[j][:, 0:KD * UC].rearrange("p (k c) -> p k c", c=UC)
                src = w[0].rearrange("(k p) n -> p k n", p=P)
                sp.dma_start(dst[:, :, 0:P], src[:, :, ds(tile * P, P)]).then_inc(w_landed[j], 16)
                sp.dma_start(dst[:, :, P:UC], src[:, :, ds(tile * P + D_FF, P)]).then_inc(w_landed[j], 16)

            def load_columns(pair, unit, j, w, k0, kt):
                slot_free(pair, j)
                dst = w_raw[j][:, 0:kt * UC].rearrange("p (k c) -> p k c", c=UC)
                src = w[0, k0 * P:(k0 + kt) * P, :].rearrange("(k p) n -> p k n", p=P)
                h = kt // 2
                sp.dma_start(dst[:, 0:h, :], src[:, 0:h, ds(unit * UC, UC)]).then_inc(w_landed[j], 16)
                sp.dma_start(dst[:, h:kt, :], src[:, h:kt, ds(unit * UC, UC)]).then_inc(w_landed[j], 16)

            def ffn_loads(p0, w_in, w_out, first):
                tile0 = 0
                for c, pairs in zip(CHUNKS, (IN_A, IN_B)):
                    skip = 1 if first and tile0 == 0 else 0
                    for i in range(skip):
                        for j in range(2):
                            load_gate_up(0, j, j, w_in, first=True)
                    with sp.Fori(skip, pairs) as i:
                        for j in range(2):
                            load_gate_up(i + p0, i * 2 + (tile0 + j), j, w_in)
                    p0 += pairs
                    with sp.Fori(0, KD // 4) as i:
                        for j in range(2):
                            load_columns(i + p0, i * 2 + j, j, w_out, tile0, c)
                    p0 += KD // 4
                    tile0 += c

            ffn_loads(P_FFN[0], io["ffn1_w_in"], io["ffn1_w_out"], True)
            with sp.Fori(0, MIX_PAIRS) as i:
                for j in range(2):
                    load_columns(i + P_MIX_IN, i * 2 + j, j, io["w_in_mix"], 0, KD)
            mid_sync(sp)
            with sp.Fori(0, KD // 4) as i:
                for j in range(2):
                    load_columns(i + P_MIX_OUT, i * 2 + j, j, io["w_out_mix"], 0, KD)
            ffn_loads(P_FFN[1], io["ffn2_w_in"], io["ffn2_w_out"], False)
            for i in range(TT + 1):
                sp.wait_ge(y_copied, 2 * (i + 1))
                dst = y_prompt[0, i * P:(i + 1) * P, :] if i < TT else y_sample.rearrange("b t d -> (b t) d")
                sp.dma_start(dst, y_nat[0:N_TOK[i], i % 2, :]).then_inc(y_stored[i % 2], 16)
            sp.wait_ge(y_stored[0], 16 * ((TT + 2) // 2))
            sp.wait_ge(y_stored[1], 16 * ((TT + 1) // 2))
            mid_stores_waited(sp)

        @block.tensor
        def _(pe):
            pe.wait_ge(const_ready, 2)
            for i in range(TT + 1):
                n = N_TOK[i]
                pe.wait_ge(x_landed[i], 16)
                for q in range(2):
                    b = 2 * (i % 2) + q
                    if i >= 2:
                        pe.wait_ge(xt_copied, 2 * (i - 2) + q + 1)
                    for d in range(4):
                        mm = pe.transpose(ps[:, b, d * P:d * P + n], x_nat[0:n, i, (4 * q + d) * P:(4 * q + d + 1) * P],
                                          ident[0:n, 0:n])
                    mm.then_inc(xt_done, 1)

            def unit(pair, j, kt, x_hi, x_lo, x_wait=None, first=False, second_tile=None):
                pe.wait_ge(w_hi_ready, 2 * pair + j + 1)
                pe.wait_ge(w_lo_ready, 2 * pair + j + 1)
                if not first:
                    pe.wait_ge(drained, 2 * pair + j - 1)
                for t in range(2):
                    if t and second_tile:
                        second_tile()
                    for k in range(kt):
                        if x_wait is not None and t == 0:
                            x_wait(k)
                        w = [s[j][:, k * UC + t * P:k * UC + (t + 1) * P] for s in (w_hi, w_lo)]
                        for wp, xp in ((w[0], x_hi), (w[0], x_lo), (w[1], x_hi)):
                            for s in range(2):
                                mm = pe.matmul(bank(4 * j + 2 * t + s), wp, xp[:, k, s * HALF:(s + 1) * HALF],
                                               start=(k == 0 and wp is w[0] and xp is x_hi),
                                               stop=(k == kt - 1 and wp is w[1]))
                mm.then_inc(mm_done, 1)

            def sum_squares(stage, drained_units=0):
                pe.wait_ge(sumsq_ready, stage)
                if drained_units:
                    pe.wait_ge(drained, drained_units)
                for s in range(2):
                    mm = pe.matmul(SS[:, s, :], ones[:, :], sumsq[:, s * HALF:(s + 1) * HALF], start=True, stop=True)
                mm.then_inc(ss_done, 1)

            def x_in(stage):
                def wait(k):
                    pe.wait_ge(n_ready, KD * stage + k + 1)
                return wait

            def first_pair(p0, stage, x_hi, x_lo):
                unit(p0, 0, KD, x_hi, x_lo, x_in(stage), first=(p0 == 0))
                sum_squares(stage + 1, 2 * p0)
                unit(p0, 1, KD, x_hi, x_lo, first=(p0 == 0), second_tile=lambda: pe.wait_ge(ms_ready, stage + 1))

            def ffn(f, p0, stage):
                done = f * KF
                for c, (kt, pairs) in enumerate(zip(CHUNKS, (IN_A, IN_B))):
                    if c == 0:
                        first_pair(p0, stage, n_hi[f], n_lo[f])
                    with pe.Fori(1 if c == 0 else 0, pairs) as i:
                        for j in range(2):
                            unit(i + p0, j, KD, n_hi[f], n_lo[f])
                    p0 += pairs
                    done += kt

                    def g_wait(k):
                        if k == 0 or k == kt - 1:
                            pe.wait_ge(g_ready, done - 1 if k == 0 else done)
                    with pe.Fori(0, KD // 4) as i:
                        for j in range(2):
                            unit(i + p0, j, kt, g_hi[f], g_lo[f], g_wait)
                    p0 += KD // 4

            ffn(0, P_FFN[0], 0)
            first_pair(P_MIX_IN, 1, n_hi[0], n_lo[0])
            with pe.Fori(1, MIX_PAIRS) as i:
                for j in range(2):
                    unit(i + P_MIX_IN, j, KD, n_hi[0], n_lo[0])
            pe.wait_ge(wf_split, 2)
            pe.wait_ge(drained, 2 * P_MIX_OUT - 1)
            for k in range(KD):
                for n, (wp, xp) in enumerate(((wf_hi, n_hi[0]), (wf_hi, n_lo[0]), (wf_lo, n_hi[0]))):
                    for s in range(2):
                        mm = pe.matmul(ps[0:H_FX, s, 0:HALF], wp[:, k, :], xp[:, k, s * HALF:(s + 1) * HALF],
                                       start=(k == 0 and n == 0), stop=(k == KD - 1 and n == 2))
            mm.then_inc(ff_done, 1)
            mid_tensor(pe)
            with pe.Fori(0, KD // 4) as i:
                for j in range(2):
                    unit(i + P_MIX_OUT, j, KD, o_hi, o_lo)
            ffn(1, P_FFN[1], 2)
            sum_squares(4, 2 * (P_FFN[1] + P_MIX_IN))
            for i in range(TT + 1):
                n = N_TOK[i]
                for q in range(2):
                    if i >= 2:
                        pe.wait_ge(y_copied, 2 * (i - 2) + q + 1)
                    for d in range(4):
                        if i == 0:
                            pe.wait_ge(yt_ready, 4 * q + d + 1)
                        mm = pe.transpose(ps[0:n, 2 * (i % 2) + q, d * P:(d + 1) * P],
                                          yT[:, 4 * q + d, i * P:i * P + n], ident[:, :])
                    mm.then_inc(yt_done, 1)

        @block.scalar
        def _(act):
            def split_hi(pair, j, kt, first=False):
                act.wait_ge(w_landed[j], pair * 32 + 32)
                if not first:
                    act.wait_ge(mm_done, 2 * pair + j - 1)
                nc.scalar.activation(w_hi[j][:, 0:kt * UC], w_raw[j][:, 0:kt * UC], ACT.Copy).then_inc(w_hi_ready, 1)

            def norm_in(stage, x_wait):
                f = 0 if stage < 2 else 1
                for d in range(KD):
                    x_wait(d)
                    nc.scalar.activation(n_hi[f][:, d, :], xT[:, d, :], ACT.Copy,
                                         scale=gains[:, stage, d:d + 1]).then_inc(nhi_ready, 1)

            def root_mean_square(stage):
                act.wait_ge(ms_ready, stage)
                nc.scalar.activation(root[:, :], ms[:, :], ACT.Sqrt).then_inc(root_ready, 1)

            def gate_step(pair, j, q, f, tile, next_kt, stage=None):
                if stage is not None:
                    root_mean_square(stage)
                split_hi(pair + 1, j, next_kt)
                act.wait_ge(a_ready, q + 1)
                nc.scalar.activation(a_silu[:, :, :], a_n[:, :, :], ACT.Silu).then_inc(silu_done, 1)
                act.wait_ge(gated_ready, q + 1)
                nc.scalar.activation(halves(g_hi[f][:, ds(tile, 1), :].rearrange("p o t -> p (o t)")), g_f[:, :, :],
                                     ACT.Copy).then_inc(ghi_ready, 1)

            def ffn(f, p0, stage):
                q0 = f * KF
                for c, (kt, pairs) in enumerate(zip(CHUNKS, (IN_A, IN_B))):
                    peel = 1 if c == 0 else 0
                    if peel:
                        for j in range(2):
                            gate_step(p0, j, q0 + j, f, j, KD, stage + 1 if j == 0 else None)
                    with act.Fori(peel, pairs - 1) as i:
                        for j in range(2):
                            gate_step(i + p0, j, i * 2 + (q0 + j), f, i * 2 + j, KD)
                    for j in range(2):
                        tile = 2 * (pairs - 1) + j
                        gate_step(p0 + pairs - 1, j, q0 + tile, f, tile, kt)
                    p0 += pairs
                    q0 += kt
                    for i in range(KD // 4):
                        for j in range(2):
                            last = i == KD // 4 - 1
                            end = f == 1 and c == 1
                            if not (last and end):
                                split_hi(p0 + i + 1, j, KD if last else kt)
                            else:
                                act.wait_ge(mm_done, 2 * (p0 + i) + j + 1)
                            if c == 1 and f == 0:
                                next_input(stage + 1, 2 * (2 * i + j))
                    p0 += KD // 4

            def next_input(stage, d0):
                f = 0 if stage < 2 else 1
                for d in range(d0, d0 + 2):
                    act.wait_ge(x_ready, KD * (stage - 1) + d + 1)
                    nc.scalar.activation(n_hi[f][:, d, :], xT[:, d, :], ACT.Copy,
                                         scale=gains[:, stage, d:d + 1]).then_inc(nhi_ready, 1)

            for j in range(2):
                split_hi(0, j, KD, first=True)
            act.wait_ge(gains_landed, 16 * N_CONST_LOADS)
            mix_prologue_scalar(act)
            nc.scalar.activation(wf_hi[:, :, :], wf[:, :, :], ACT.Copy).then_inc(wf_split, 1)
            norm_in(0, lambda d: act.wait_ge(xt_copied, 2 * (TT + 1)))
            ffn(0, P_FFN[0], 0)
            root_mean_square(2)
            with act.Fori(0, MIX_PAIRS - 1 - H_HG // 2) as i:
                for j in range(2):
                    split_hi(i + (P_MIX_IN + 1), j, KD)
            with act.Fori(0, H_HG // 2) as i:
                for j in range(2):
                    split_hi(i + (P_MIX_OUT - H_HG // 2), j, KD)
                    act.wait_ge(drained, i * 2 + (2 * (P_MIX_IN + H_HG)))
                    for tile, func in ((T_F, ACT.Sigmoid), (T_G, ACT.Silu)):
                        gate = mix_tile(tile + j, i * 2)
                        nc.scalar.activation(gate, gate, func).then_inc(gates_done, 1)
            mid_scalar(act)
            for j in range(2):
                split_hi(P_MIX_OUT, j, KD)
            for i in range(KD // 4):
                for j in range(2):
                    split_hi(P_MIX_OUT + i + 1, j, KD)
                    next_input(2, 2 * (2 * i + j))
            ffn(1, P_FFN[1], 2)
            root_mean_square(4)
            for i in range(TT + 1):
                for q in range(2):
                    act.wait_ge(yt_done, 2 * i + q + 1)
                    if i >= 2:
                        act.wait_ge(y_stored[i % 2], 16 * (i // 2))
                    nc.scalar.activation(y_nat[0:N_TOK[i], i % 2, q * 512:(q + 1) * 512],
                                         ps[0:N_TOK[i], 2 * (i % 2) + q, :], ACT.Copy).then_inc(y_copied, 1)

        @block.vector
        def _(dve):
            def split_lo(pair, j, kt):
                dve.wait_ge(w_hi_ready, 2 * pair + j + 1)
                nc.vector.tensor_tensor(w_lo[j][:, 0:kt * UC], w_raw[j][:, 0:kt * UC],
                                        w_hi[j][:, 0:kt * UC].bitcast(F32), ALU.subtract).then_inc(w_lo_ready, 1)

            def input_lo(stage, d):
                f = 0 if stage < 2 else 1
                if stage:
                    dve.wait_ge(x_ready, KD * (stage - 1) + d + 1)
                dve.wait_ge(nhi_ready, KD * stage + d + 1)
                nc.vector.scalar_tensor_tensor(n_lo[f][:, d, :], xT[:, d, :], gains[:, stage, d:d + 1],
                                               n_hi[f][:, d, :].bitcast(F32), ALU.mult, ALU.subtract).then_inc(n_ready, 1)

            def mean_squares(stage):
                dve.wait_ge(ss_done, stage)
                nc.vector.tensor_scalar(halves(ms[:, :]), SS, 1.0 / D, EPS, ALU.mult, ALU.add).then_inc(ms_ready, 1)
                dve.wait_ge(root_ready, stage)
                r = rstd[:, :, :].rearrange("p s c -> p (s c)")
                nc.vector.reciprocal(r, root[:, :]).then_inc(rstd_step, 1)
                dve.wait_ge(rstd_step, 4 * stage - 3)
                nc.vector.tensor_tensor(root[:, :], r, r, ALU.mult).then_inc(rstd_step, 1)
                dve.wait_ge(rstd_step, 4 * stage - 2)
                nc.vector.scalar_tensor_tensor(root[:, :], root[:, :], -0.5, ms[:, :], ALU.mult, ALU.mult)\
                    .then_inc(rstd_step, 1)
                dve.wait_ge(rstd_step, 4 * stage - 1)
                nc.vector.scalar_tensor_tensor(r, root[:, :], 1.5, r, ALU.add, ALU.mult).then_inc(rstd_step, 1)
                dve.wait_ge(rstd_step, 4 * stage)

            def gate_step(pair, j, q, f, tile, next_kt, stage=None):
                dve.wait_ge(mm_done, 2 * pair + j + 1)
                if stage is not None:
                    mean_squares(stage)
                nc.vector.tensor_tensor(a_n[:, :, :], unit_psum(j, 0), rstd[:, :, :], ALU.mult).then_inc(a_ready, 1)
                nc.vector.tensor_tensor(b_n[:, :, :], unit_psum(j, 1), rstd[:, :, :], ALU.mult).then_inc(drained, 1)
                split_lo(pair + 1, j, next_kt)
                dve.wait_ge(silu_done, q + 1)
                dve.wait_ge(drained, 2 * pair + j + 1)
                nc.vector.tensor_tensor(g_f[:, :, :], a_silu[:, :, :], b_n[:, :, :], ALU.mult).then_inc(gated_ready, 1)
                dve.wait_ge(ghi_ready, q + 1)
                hi = halves(g_hi[f][:, ds(tile, 1), :].rearrange("p o t -> p (o t)"))
                lo = halves(g_lo[f][:, ds(tile, 1), :].rearrange("p o t -> p (o t)"))
                nc.vector.tensor_tensor(lo, g_f[:, :, :], hi.bitcast(F32), ALU.subtract).then_inc(g_ready, 1)

            def add_out(pair, j, i, weight, last, x_tiles=0):
                dve.wait_ge(mm_done, 2 * pair + j + 1)
                for t in range(2):
                    x = halves(xT[:, 4 * i + 2 * j + t, :])
                    op = nc.vector.scalar_tensor_tensor(x, unit_psum(j, t), weight, x, ALU.mult, ALU.add)
                    if last:
                        op.then_inc(x_ready, 1)
                if last:
                    dve.wait_ge(x_ready, x_tiles + 2)
                    dve.sem_inc(drained, 1)
                else:
                    op.then_inc(drained, 1)

            def ffn(f, p0, stage):
                q0 = f * KF
                for c, (kt, pairs) in enumerate(zip(CHUNKS, (IN_A, IN_B))):
                    peel = 1 if c == 0 else 0
                    if peel:
                        gate_step(p0, 0, q0, f, 0, KD, stage + 1)
                        gate_step(p0, 1, q0 + 1, f, 1, KD)
                    with dve.Fori(peel, pairs - 1) as i:
                        for j in range(2):
                            gate_step(i + p0, j, i * 2 + (q0 + j), f, i * 2 + j, KD)
                    for j in range(2):
                        tile = 2 * (pairs - 1) + j
                        gate_step(p0 + pairs - 1, j, q0 + tile, f, tile, kt)
                    p0 += pairs
                    q0 += kt
                    for i in range(KD // 4):
                        for j in range(2):
                            last = i == KD // 4 - 1
                            add_out(p0 + i, j, i, 0.5, c == 1, KD * stage + 4 * i + 2 * j)
                            if not (last and f == 1 and c == 1):
                                split_lo(p0 + i + 1, j, KD if last else kt)
                            if c == 1 and f == 0:
                                for t in range(2):
                                    input_lo(stage + 1, 4 * i + 2 * j + t)
                    p0 += KD // 4

            mix_prologue(dve)
            for j in range(2):
                split_lo(0, j, KD)
            dve.wait_ge(wf_split, 1)
            nc.vector.tensor_tensor(wf_lo[:, :, :], wf[:, :, :], wf_hi[:, :, :].bitcast(F32),
                                    ALU.subtract).then_inc(wf_split, 1)
            for i in range(TT + 1):
                for q in range(2):
                    dve.wait_ge(xt_done, 2 * i + q + 1)
                    src = ps[:, 2 * (i % 2) + q, :].rearrange("p (d c) -> p d c", c=P)[:, :, 0:N_TOK[i]]
                    nc.vector.tensor_copy(xT[:, 4 * q:4 * q + 4, i * P:i * P + N_TOK[i]], src).then_inc(xt_copied, 1)
            dve.wait_ge(xt_copied, 2 * (TT + 1))
            for d in range(KD):
                input_lo(0, d)
            ffn(0, P_FFN[0], 0)

            def project_out(pair, j, tile):
                dve.wait_ge(mm_done, 2 * pair + j + 1)
                for t in range(2):
                    out = pT[:, ds(tile + t, 1), :].rearrange("p o t -> p (o t)")
                    op = nc.vector.tensor_tensor(halves(out), unit_psum(j, t), rstd[:, :, :], ALU.mult)
                op.then_inc(drained, 1)

            for j in range(2):
                if j == 0:
                    dve.wait_ge(mm_done, 2 * P_MIX_IN + 1)
                    mean_squares(2)
                project_out(P_MIX_IN, j, 2 * j)
                split_lo(P_MIX_IN + 1, j, KD)
            with dve.Fori(1, MIX_PAIRS - 1) as i:
                for j in range(2):
                    project_out(i + P_MIX_IN, j, i * 4 + 2 * j)
                    split_lo(i + (P_MIX_IN + 1), j, KD)
            for j in range(2):
                project_out(P_MIX_OUT - 1, j, MIX_TILES - 4 + 2 * j)
            dve.wait_ge(ff_done, 1)
            nc.vector.tensor_tensor(halves(ffT[:, :]), ps[0:H_FX, 0:2, 0:HALF], rstd[0:H_FX, :, :],
                                    ALU.mult).then_inc(ff_ready, 1)
            mid_vector(dve)
            for j in range(2):
                split_lo(P_MIX_OUT, j, KD)
            for i in range(KD // 4):
                for j in range(2):
                    add_out(P_MIX_OUT + i, j, i, 1.0, True, KD + 4 * i + 2 * j)
                    split_lo(P_MIX_OUT + i + 1, j, KD)
                    for t in range(2):
                        input_lo(2, 4 * i + 2 * j + t)
            ffn(1, P_FFN[1], 2)
            mean_squares(4)
            for d in range(KD):
                nc.vector.scalar_tensor_tensor(halves(yT[:, d, :]), halves(xT[:, d, :]), gains[:, 3, d:d + 1],
                                               rstd[:, :, :], ALU.mult, ALU.mult).then_inc(yt_ready, 1)

        @block.gpsimd
        def _(pool):
            nc.gpsimd.memset(ones[:, :], 1.0).then_inc(const_ready, 1)
            pool.wait_ge(const_ready, 1)
            nc.gpsimd.affine_select(ident[:, :], ones[:, :], pattern=[[-1, P]], compare_op=ALU.is_equal, fill=0.0,
                                    base=0, channel_multiplier=1).then_inc(const_ready, 1)

            make_mix_consts(pool)

            def squares(stage, x_wait):
                for d in range(KD):
                    x_wait(d)
                    n = stage * KD + d
                    if d == 0:
                        if stage:
                            pool.wait_ge(ss_done, stage)
                        nc.gpsimd.tensor_tensor(sumsq[:, :], xT[:, d, :], xT[:, d, :], ALU.mult).then_inc(sq_added, 1)
                        continue
                    pool.wait_ge(sq_added, n)
                    nc.gpsimd.tensor_tensor(sq[:, :], xT[:, d, :], xT[:, d, :], ALU.mult).then_inc(sq_done, 1)
                    pool.wait_ge(sq_done, n - stage)
                    add = nc.gpsimd.tensor_tensor(sumsq[:, :], sumsq[:, :], sq[:, :], ALU.add)
                    add.then_inc(sq_added, 1)
                pool.wait_ge(sq_added, (stage + 1) * KD)
                pool.sem_inc(sumsq_ready, 1)

            squares(0, lambda d: pool.wait_ge(xt_copied, 2 * (TT + 1)))
            squares(1, lambda d: pool.wait_ge(x_ready, d + 1))
            mid_gpsimd(pool)
            squares(2, lambda d: pool.wait_ge(x_ready, KD + d + 1))
            squares(3, lambda d: pool.wait_ge(x_ready, 2 * KD + d + 1))


_INS = ["x_prompt", "x_sample", "cache_k", "cache_v", "cache_logf", "state_hgrn", "page_table", "norm_ffn1",
        "ffn1_w_in", "ffn1_w_out", "norm_mix", "w_in_mix", "hgrn_lb", "fox_f_bias", "hgrn_out_gain", "fox_out_gain",
        "w_out_mix", "norm_ffn2", "ffn2_w_in", "ffn2_w_out", "norm_final"]
_OUTS = [(1, SEQ, D), (DB, DS_, D), (1, 1, SEQ, H_FX, DH), (1, 1, SEQ, H_FX, DH), (1, 1, SEQ, H_FX),
         (1, 1, H_HG, P, P), (1, DB, DS_, H_FX, DH), (1, DB, DS_, H_FX, DH), (1, DB, DS_, H_FX), (1, DB, H_HG, P, P)]


def kernel(**inputs):
    import concourse.bacc as bacc
    from concourse.bass_utils import run_bass_kernel_spmd

    nc = bacc.Bacc("TRN2", target_bir_lowering=False, num_devices=1)
    arrays, io = {}, {}
    for name in _INS:
        a = np.ascontiguousarray(inputs[name])
        arrays[f"in_{name}"] = a
        io[name] = nc.dram_tensor(f"in_{name}", a.shape, mybir.dt.from_np(a.dtype), kind="ExternalInput").ap()
    io["outs"] = [nc.dram_tensor(f"out_{i}", s, F32, kind="ExternalOutput").ap() for i, s in enumerate(_OUTS)]
    build(nc, io)
    r = run_bass_kernel_spmd(nc, [arrays], core_ids=[0])
    return tuple(r.results[0][f"out_{i}"] for i in range(len(_OUTS)))
```
